# Optimizing a Trainium2 kernel written in Bass

```python
import jax, jax.numpy as jnp
from jax import lax
import numpy as np

D_MODEL = 1024
BATCH = 1
SEQ = 256
DEPTH = 1

EPS = 1e-6
MLA_HEADS = 8
QK_NOPE = 64
QK_ROPE = 32
QK_HEAD = QK_NOPE + QK_ROPE
V_HEAD = 64
Q_RANK = 384
KV_RANK = 256
ROPE_BASE = 10000.0
Q_BLOCK = 128
MLA_WIDTH = MLA_HEADS * V_HEAD
SG_GROUPS = 4
SG_GROUP_DIM = 128
SG_WIDTH = SG_GROUPS * SG_GROUP_DIM
CHUNK = 128
CONV_WIDTH = 512
CONV_K = 3
N_GROUPS = 4
EXPERTS_PER_GROUP = 8
N_EXPERTS = N_GROUPS * EXPERTS_PER_GROUP
TOP_K = 2
D_EXPERT = 256
IN_SIZES = (Q_RANK, KV_RANK, QK_ROPE, SG_WIDTH, SG_WIDTH,
            CONV_WIDTH, CONV_WIDTH, CONV_WIDTH, D_MODEL, D_MODEL, D_MODEL)
D_IN = Q_RANK + KV_RANK + QK_ROPE + 2 * SG_WIDTH + 3 * CONV_WIDTH + 3 * D_MODEL

kernel_name = "hybrid_mla_sgmlp_shortconv_hmoe"

def rmsnorm(x, g):
    xf = x.astype(jnp.float32)
    y = xf * lax.rsqrt(jnp.mean(xf * xf, axis=-1, keepdims=True) + EPS)
    return (y * g.astype(jnp.float32)).astype(x.dtype)

def split_cols(a, sizes):
    out, start = [], 0
    for s in sizes:
        out.append(a[..., start:start + s])
        start += s
    return out

def rope_tables(positions):
    inv = ROPE_BASE ** (-jnp.arange(0, QK_ROPE, 2, dtype=jnp.float32) / QK_ROPE)
    ang = positions.astype(jnp.float32)[..., None] * inv
    return jnp.cos(ang), jnp.sin(ang)

def apply_rope(x, cos, sin):
    xf = x.astype(jnp.float32)
    x1, x2 = xf[..., :QK_ROPE // 2], xf[..., QK_ROPE // 2:]
    return jnp.concatenate([x1 * cos - x2 * sin, x2 * cos + x1 * sin], axis=-1).astype(x.dtype)

def mla_branch(c_q, c_kv, k_rope_raw, cos, sin, q_norm, w_q_up, kv_norm, w_kv_up):
    B, S, _ = c_q.shape
    q = (rmsnorm(c_q, q_norm) @ w_q_up).reshape(B, S, MLA_HEADS, QK_HEAD)
    q_nope, q_rope = q[..., :QK_NOPE], q[..., QK_NOPE:]
    q_rope = apply_rope(q_rope, cos[:, :, None, :], sin[:, :, None, :])
    q = jnp.concatenate([q_nope, q_rope], axis=-1)
    kv = (rmsnorm(c_kv, kv_norm) @ w_kv_up).reshape(B, S, MLA_HEADS, QK_NOPE + V_HEAD)
    k_nope, v = kv[..., :QK_NOPE], kv[..., QK_NOPE:]
    k_rope = apply_rope(k_rope_raw[:, :, None, :], cos[:, :, None, :], sin[:, :, None, :])
    k = jnp.concatenate([k_nope, jnp.broadcast_to(k_rope, (B, S, MLA_HEADS, QK_ROPE))], axis=-1)
    scale = QK_HEAD ** -0.5
    nb = S // Q_BLOCK
    q_blocks = q.reshape(B, nb, Q_BLOCK, MLA_HEADS, QK_HEAD).transpose(1, 0, 2, 3, 4)
    k_pos = jnp.arange(S)
    neg = jnp.finfo(jnp.float32).min

    def attend(args):
        q_blk, blk = args
        q_pos = blk * Q_BLOCK + jnp.arange(Q_BLOCK)
        s = jnp.einsum('bqhd,bkhd->bhqk', q_blk, k).astype(jnp.float32) * scale
        s = jnp.where(k_pos[None, :] <= q_pos[:, None], s, neg)
        p = jax.nn.softmax(s, axis=-1).astype(v.dtype)
        return jnp.einsum('bhqk,bkhd->bqhd', p, v)

    o = lax.map(attend, (q_blocks, jnp.arange(nb)))
    return o.transpose(1, 0, 2, 3, 4).reshape(B, S, MLA_WIDTH)

def spatial_gating_branch(u, v, sg_norm, w_s, b_s):
    B, S, _ = u.shape
    u = jax.nn.gelu(u)
    v = rmsnorm(jax.nn.gelu(v), sg_norm)
    v = v.reshape(B, S // CHUNK, CHUNK, SG_GROUPS, SG_GROUP_DIM)
    w = w_s * jnp.tril(jnp.ones((CHUNK, CHUNK), dtype=w_s.dtype))[None]
    mixed = jnp.einsum('gts,bcsgd->bctgd', w, v) + b_s.T[:, :, None]
    return u * mixed.reshape(B, S, SG_WIDTH)

def short_conv_branch(b_gate, c_gate, h, conv_w):
    S = h.shape[1]
    z = c_gate * h
    zp = jnp.pad(z, ((0, 0), (CONV_K - 1, 0), (0, 0)))
    y = conv_w[0] * zp[:, 0:S]
    for j in range(1, CONV_K):
        y = y + conv_w[j] * zp[:, j:j + S]
    return b_gate * y

def hier_moe(h, w_group_router, b_group_router, w_expert_router, b_expert_router, w_gate_up, w_down):
    B, S, D = h.shape
    t = h.reshape(B * S, D)
    T = t.shape[0]
    g_prob = jax.nn.softmax((t @ w_group_router).astype(jnp.float32) + b_group_router.astype(jnp.float32), axis=-1)
    g_p, g_idx = lax.top_k(g_prob, 1)
    e_logits = ((t @ w_expert_router).astype(jnp.float32) + b_expert_router.astype(jnp.float32))
    e_logits = e_logits.reshape(T, N_GROUPS, EXPERTS_PER_GROUP)
    e_sel = jnp.take_along_axis(e_logits, g_idx[:, :, None], axis=1)[:, 0]
    e_prob = jax.nn.softmax(e_sel, axis=-1)
    top_p, top_i = lax.top_k(e_prob, TOP_K)
    weights = g_p * (top_p / jnp.sum(top_p, axis=-1, keepdims=True))
    expert_id = g_idx * EXPERTS_PER_GROUP + top_i
    combine = jnp.einsum('tk,tke->te', weights, jax.nn.one_hot(expert_id, N_EXPERTS, dtype=jnp.float32))
    combine = combine.astype(t.dtype)
    out = jnp.zeros_like(t)
    for e in range(N_EXPERTS):
        gu = t @ w_gate_up[e]
        y = (jax.nn.silu(gu[:, :D_EXPERT]) * gu[:, D_EXPERT:]) @ w_down[e]
        out = out + combine[:, e:e + 1] * y
    return out.reshape(B, S, D)

def setup_inputs(seed: int = 0) -> dict:
    key = jax.random.key(seed)
    ks = jax.random.split(key, 32)
    L, D, f32 = DEPTH, D_MODEL, jnp.float32

    def nrm(k, shape, fan_in):
        return jax.random.normal(k, shape, f32) * (fan_in ** -0.5)

    def gain(k, shape):
        return 1.0 + 0.05 * jax.random.normal(k, shape, f32)

    offsets = jax.random.randint(ks[1], (BATCH,), 0, 1024, dtype=jnp.int32)
    positions = offsets[:, None] + jnp.arange(SEQ, dtype=jnp.int32)[None, :]
    return {
        "x": jax.random.normal(ks[0], (BATCH, SEQ, D), f32),
        "positions": positions,
        "norm_mix": gain(ks[2], (L, D)),
        "w_in": nrm(ks[3], (L, D, D_IN), D),
        "q_norm": gain(ks[4], (L, Q_RANK)),
        "w_q_up": nrm(ks[5], (L, Q_RANK, MLA_HEADS * QK_HEAD), Q_RANK),
        "kv_norm": gain(ks[6], (L, KV_RANK)),
        "w_kv_up": nrm(ks[7], (L, KV_RANK, MLA_HEADS * (QK_NOPE + V_HEAD)), KV_RANK),
        "sg_norm": gain(ks[8], (L, SG_WIDTH)),
        "w_s": nrm(ks[9], (L, SG_GROUPS, CHUNK, CHUNK), CHUNK),
        "b_s": 1.0 + 0.1 * jax.random.normal(ks[10], (L, SG_GROUPS, CHUNK), f32),
        "conv_w": nrm(ks[11], (L, CONV_K, CONV_WIDTH), CONV_K),
        "w_a_out": nrm(ks[12], (L, MLA_WIDTH, D), MLA_WIDTH),
        "w_b_out": nrm(ks[13], (L, SG_WIDTH, D), SG_WIDTH),
        "w_c_out": nrm(ks[14], (L, CONV_WIDTH, D), CONV_WIDTH),
        "w_o": nrm(ks[15], (L, D, D), D),
        "norm_ffn": gain(ks[16], (L, D)),
        "w_group_router": nrm(ks[17], (L, D, N_GROUPS), D),
        "b_group_router": 0.01 * jax.random.normal(ks[18], (L, N_GROUPS), f32),
        "w_expert_router": nrm(ks[19], (L, D, N_EXPERTS), D),
        "b_expert_router": 0.01 * jax.random.normal(ks[20], (L, N_EXPERTS), f32),
        "w_gate_up": nrm(ks[21], (L, N_EXPERTS, D, 2 * D_EXPERT), D),
        "w_down": nrm(ks[22], (L, N_EXPERTS, D_EXPERT, D), D_EXPERT),
        "final_norm": gain(ks[23], (D,)),
    }

def reference(x, positions, norm_mix, w_in, q_norm, w_q_up, kv_norm, w_kv_up, sg_norm, w_s, b_s,
              conv_w, w_a_out, w_b_out, w_c_out, w_o, norm_ffn, w_group_router, b_group_router,
              w_expert_router, b_expert_router, w_gate_up, w_down, final_norm):
    cos, sin = rope_tables(positions)
    for l in range(DEPTH):
        h = rmsnorm(x, norm_mix[l])
        (c_q, c_kv, k_r, sg_u, sg_v, cb, cc, ch, ga, gb, gc) = split_cols(h @ w_in[l], IN_SIZES)
        y_a = mla_branch(c_q, c_kv, k_r, cos, sin, q_norm[l], w_q_up[l], kv_norm[l], w_kv_up[l]) @ w_a_out[l]
        y_b = spatial_gating_branch(sg_u, sg_v, sg_norm[l], w_s[l], b_s[l]) @ w_b_out[l]
        y_c = short_conv_branch(cb, cc, ch, conv_w[l]) @ w_c_out[l]
        merged = jax.nn.sigmoid(ga) * y_a + jax.nn.sigmoid(gb) * y_b + jax.nn.sigmoid(gc) * y_c
        x = x + merged @ w_o[l]
        h = rmsnorm(x, norm_ffn[l])
        x = x + hier_moe(h, w_group_router[l], b_group_router[l], w_expert_router[l],
                         b_expert_router[l], w_gate_up[l], w_down[l])
    return rmsnorm(x, final_norm)


_drawn_inputs = setup_inputs


def setup_inputs(seed=0):
    import zlib

    import numpy as np

    out = dict(_drawn_inputs(seed))
    spreads = {}
    factors = {'q_norm': 4.251,
     'kv_norm': 4.546,
     'sg_norm': 9.334,
     'b_group_router': 18.072,
     'b_expert_router': 18.73,
     'b_s': 3.021,
     'norm_ffn': 3.927}
    for name, (base, spread) in spreads.items():
        noise = np.random.default_rng([zlib.crc32(name.encode()), seed]).standard_normal(out[name].shape)
        drawn = base * np.exp(spread * noise) if base else spread * noise
        out[name] = __import__('jax').numpy.asarray(drawn.astype(out[name].dtype))
    for name, factor in factors.items():
        out[name] = (out[name] * factor).astype(out[name].dtype)
    return out
```

```python
from contextlib import ExitStack

import numpy as np
import concourse.bass as bass
from concourse import mybir

F32 = mybir.dt.float32
F32R = mybir.dt.float32r
I32 = mybir.dt.int32
ALU = mybir.AluOpType
ACT = mybir.ActivationFunctionType
AX_X = mybir.AxisListType.X

P = 128
D = 1024
SEQ = 256
T = SEQ // P
KD = D // P
EPS = 1e-6
HEADS, NOPE, ROPE, VH = 8, 64, 32, 64
QK = NOPE + ROPE
R2 = ROPE // 2
QR, KVR = 384, 256
KQ, KKV = QR // P, KVR // P
KC = KQ + KKV
SG, SGG = 512, 4
CW, TAPS = 512, 3
NG, EPG = 4, 8
NE = NG * EPG
DE = 256
NR = NG + NE
SCALE = float(QK) ** -0.5
NEG = -1.0e30
BIG = 64.0
LOWEST = -3.0e38
MAGIC = 12582912.0
IN_SIZES = (QR, KVR, ROPE, SG, SG, CW, CW, CW, D, D, D)
C_Q, C_KV, C_KR, C_SGU, C_SGV, C_CB, C_CC, C_CH, C_GA, C_GB, C_GC = (
    sum(IN_SIZES[:i]) for i in range(len(IN_SIZES)))

HALF = 2048
RAW = 6
SPLIT = 3
AHEAD = SPLIT - 1
BANK = 512

H_CQ, H_CKV, H_CB, H_CC, H_QUP, H_KVUP, H_CH, H_SGV, H_SGU = 0, 2, 4, 6, 8, 10, 11, 13, 15
H_GATE = 17
H_WO = H_GATE + 18
N_MIX = H_WO + 4
H_ATT = H_SGU
UNITS = T * HEADS // 2
PER_GROUP = 3 * EPG
SLOTS = (NG + 1) * P


def two_pi_parts():
    rest, parts = 2 * np.pi, []
    for _ in range(4):
        m, e = np.frexp(rest)
        part = float(np.ldexp(np.round(m * 256) / 256, int(e)))
        parts.append(part)
        rest -= part
    return parts


def trunk(nc, x, positions, norm_mix, w_in, q_norm, w_q_up, kv_norm, w_kv_up, sg_norm, w_s, b_s,
          conv_w, w_a_out, w_b_out, w_c_out, w_o, norm_ffn, w_group_router, b_group_router,
          w_expert_router, b_expert_router, w_gate_up, w_down, final_norm, out):
    x_d = x[0].rearrange("(t p) d -> p t d", p=P)
    out_d = out[0].rearrange("(t p) d -> p t d", p=P)
    win_d = w_in[0].rearrange("(p k) n -> p k n", k=KD)
    qup_d = w_q_up[0].rearrange("(p k) n -> p k n", k=KQ)
    kvup_d = w_kv_up[0].rearrange("(p k) n -> p k n", k=KKV)
    wout_d = [w[0].rearrange("(k p) n -> p k n", p=P) for w in (w_c_out, w_b_out, w_a_out)]
    wo_d = w_o[0].rearrange("(k p) n -> p k n", p=P)
    gu_d = w_gate_up[0].rearrange("e (p k) n -> e p (k n)", k=KD)
    dn_d = w_down[0].rearrange("e (p k) n -> e p (k n)", k=DE // P)

    with ExitStack() as ctx:
        def sb(name, shape, dt=F32, stack=ctx):
            return stack.enter_context(nc.sbuf_tensor(name, shape, dt))

        def sem(name):
            return ctx.enter_context(nc.semaphore(name))

        ps = ctx.enter_context(nc.psum_tensor("ps", [P, 8, BANK], F32))

        raw = sb("raw", [P, RAW, HALF])
        w_hi = sb("w_hi", [P, SPLIT, HALF], F32R)
        w_lo = sb("w_lo", [P, SPLIT, HALF], F32R)
        xs = sb("xs", [P, T, D])
        ident = sb("ident", [P, P])
        ident_r = sb("ident_r", [P, P], F32R)
        ones = sb("ones", [P, P])
        before = sb("before", [P, P])
        causal = sb("causal", [P, SEQ])
        g_mix = sb("g_mix", [P, KD])
        g_ffn = sb("g_ffn", [P, KD])
        g_c = sb("g_c", [P, KC])
        g_fin = sb("g_fin", [P, D])
        w_rt = sb("w_rt", [P, KD, NR])
        rt_raw = sb("rt_raw", [P, KD, NG])
        b_rt = sb("b_rt", [P, NR])
        stat = sb("stat", [P, 6, 4, T])
        neg_half = sb("neg_half", [P, T])

        mix = ExitStack()
        hT_hi = sb("hT_hi", [P, KD, SEQ], F32R, mix)
        hT_lo = sb("hT_lo", [P, KD, SEQ], F32R, mix)
        v_sb = sb("v_sb", [P, T, HEADS, VH], F32, mix)
        qT = sb("qT", [QK, HEADS, SEQ], F32, mix)
        kT = sb("kT", [QK, HEADS, SEQ], F32, mix)
        cb_sb = sb("cb_sb", [P, 4, SEQ], F32, mix)
        z_sb = sb("z_sb", [P, 4, SEQ + TAPS - 1], F32, mix)
        pr = sb("pr", [P, 2, 2, SEQ], F32, mix)
        pT = sb("pT", [P, 2, 4, P], F32, mix)
        o_sb = sb("o_sb", [P, T, HEADS * VH], F32, mix)
        rot = sb("rot", [P, 2, T, R2], F32, mix)
        g_sg = sb("g_sg", [P, SG], F32, mix)
        wsT = sb("wsT", [P, SGG, P], F32, mix)
        taps = sb("taps", [P, 4 * TAPS + SGG], F32, mix)
        rmax = sb("rmax", [P, T * HEADS], F32, mix)
        nmax = sb("nmax", [P, T * HEADS], F32, mix)
        rsum = sb("rsum", [P, T * HEADS], F32, mix)
        rinv = sb("rinv", [P, T * HEADS], F32, mix)
        early = ExitStack()
        cn = sb("cn", [P, T, QR + KVR], F32, early)
        cT_f = sb("cT_f", [P, KC, SEQ], F32, early)
        cT_hi = sb("cT_hi", [P, KC, SEQ], F32R, early)
        cT_lo = sb("cT_lo", [P, KC, SEQ], F32R, early)
        q9 = sb("q9", [P, T, HEADS + 1, QK], F32, early)
        kk = sb("kk", [P, T, HEADS, QK], F32, early)
        rt = cn[:].rearrange("p t n -> p (t n)")[:, 0:4 * T * (HEADS + 1) * R2]\
            .rearrange("p (i t h n) -> p i t h n", i=4, t=T, n=R2)
        early.close()
        late = ExitStack()
        merged = sb("merged", [P, T, D], F32, late)
        bT_f = sb("bT_f", [P, 4, SEQ], F32, late)
        bT_hi = sb("bT_hi", [P, 4, SEQ], F32R, late)
        bT_lo = sb("bT_lo", [P, 4, SEQ], F32R, late)
        gv = sb("gv", [P, T, SG], F32, late)
        gu_s = sb("gu_s", [P, T, SG], F32, late)
        late.close()
        start = ExitStack()
        xn = sb("xn", [P, T, D], F32, start)
        ws_raw = sb("ws_raw", [P, SGG, P], F32, start)
        cw_raw = sb("cw_raw", [4 * TAPS + SGG, P], F32, start)
        h_f = sb("h_f", [P, KD, SEQ], F32, start)
        pos_i = sb("pos_i", [P, T], I32, start)
        pos_f = sb("pos_f", [P, T], F32, start)
        inv_f = sb("inv_f", [P, R2], F32, start)
        ang = sb("ang", [P, 4, T, R2], F32, start)
        start.close()
        mix.close()

        xn_hi = sb("xn_hi", [P, T, D], F32R)
        xn_lo = sb("xn_lo", [P, T, D], F32R)
        sel = sb("sel", [P, T, SLOTS], F32R)
        selT = sb("selT", [P, NG + 1, SEQ], F32R)
        selT_g = sb("selT_g", [P, SEQ], F32R)
        comb = sb("comb", [P, NG + 1, EPG])
        y_hi = sb("y_hi", [P, D], F32R)
        y_lo = sb("y_lo", [P, D], F32R)
        ctl = sb("ctl", [P, 2], I32)
        router = ExitStack()
        xn2 = sb("xn2", [P, T, D], F32, router)
        h2T = sb("h2T", [P, KD, SEQ], F32, router)
        lg = sb("lg", [P, T, NR], F32, router)
        gt = sb("gt", [P, 5, T, NG], F32, router)
        et = sb("et", [P, 8, T, EPG], F32, router)
        eg = sb("eg", [P, T, NG, EPG], F32, router)
        sc = sb("sc", [P, 14, T, 1], F32, router)
        c_hi = sb("c_hi", [P, T, EPG], F32R, router)
        c_lo = sb("c_lo", [P, T, EPG], F32R, router)
        slot_i = sb("slot_i", [P, P], I32, router)
        slot_f = sb("slot_f", [P, P], F32, router)
        idx_g = sb("idx_g", [P, NG], F32, router)
        idx_e = sb("idx_e", [P, EPG], F32, router)
        cnt = sb("cnt", [P, 3, NG], F32, router)
        ctl_f = sb("ctl_f", [P, 3], F32, router)
        router.close()
        xg_f = sb("xg_f", [P, KD, P])
        xg_hi = sb("xg_hi", [P, KD, P], F32R)
        xg_lo = sb("xg_lo", [P, KD, P], F32R)
        silu = sb("silu", [P, 2, DE])
        hid = sb("hid", [P, 2, DE])
        hidT_hi = sb("hidT_hi", [P, 2, 2, P], F32R)
        hidT_lo = sb("hidT_lo", [P, 2, 2, P], F32R)
        x2 = sb("x2", [P, T, D])
        sq = sb("sq", [P, T, D])

        raw_landed = [sem(f"raw_landed{i}") for i in range(RAW)]
        hi_ready = sem("hi_ready")
        lo_ready = sem("lo_ready")
        half_used = sem("half_used")
        pos_in = sem("pos_in")
        x_in = sem("x_in")
        small_in = sem("small_in")
        mix_gain_in = sem("mix_gain_in")
        inv_ready = sem("inv_ready")
        ang_ready = sem("ang_ready")
        rot_ready = sem("rot_ready")
        consts_ready = sem("consts_ready")
        router_w_ready = sem("router_w_ready")
        dve_chain = sem("dve_chain")
        pool_chain = sem("pool_chain")
        ssq_ready = sem("ssq_ready")
        ms_ready = sem("ms_ready")
        root_ready = sem("root_ready")
        xn_ready = sem("xn_ready")
        h_turned = sem("h_turned")
        hf_ready = sem("hf_ready")
        hThi_ready = sem("hThi_ready")
        hTlo_ready = sem("hTlo_ready")
        small_turned = sem("small_turned")
        taps_ready = sem("taps_ready")
        wsT_ready = sem("wsT_ready")
        wsT_masked = sem("wsT_masked")
        cn_ready = sem("cn_ready")
        c_turned = sem("c_turned")
        cTf_ready = sem("cTf_ready")
        cThi_ready = sem("cThi_ready")
        cTlo_ready = sem("cTlo_ready")
        zpad_ready = sem("zpad_ready")
        cb_ready = sem("cb_ready")
        cc_ready = sem("cc_ready")
        z_ready = sem("z_ready")
        q_ready = sem("q_ready")
        kv_ready = sem("kv_ready")
        rope_ready = sem("rope_ready")
        qk_turned = sem("qk_turned")
        qT_ready = sem("qT_ready")
        kT_ready = sem("kT_ready")
        bTf_ready = sem("bTf_ready")
        bThi_ready = sem("bThi_ready")
        bTlo_ready = sem("bTlo_ready")
        branch_turned = sem("branch_turned")
        gv_ready = sem("gv_ready")
        gvn_ready = sem("gvn_ready")
        gu_ready = sem("gu_ready")
        mixed_done = sem("mixed_done")
        sgy_ready = sem("sgy_ready")
        scored = sem("scored")
        rowmax_ready = sem("rowmax_ready")
        exp_ready = sem("exp_ready")
        p_turned = sem("p_turned")
        pT_ready = sem("pT_ready")
        pv_done = sem("pv_done")
        o_ready = sem("o_ready")
        gate_ready = sem("gate_ready")
        merged_ready = sem("merged_ready")
        m_turned = sem("m_turned")
        mhi_ready = sem("mhi_ready")
        mlo_ready = sem("mlo_ready")
        x1_ready = sem("x1_ready")
        xn2_ready = sem("xn2_ready")
        xnhi_ready = sem("xnhi_ready")
        xnlo_ready = sem("xnlo_ready")
        x_turned = sem("x_turned")
        h2T_ready = sem("h2T_ready")
        logits_done = sem("logits_done")
        gmax_ready = sem("gmax_ready")
        gexp_ready = sem("gexp_ready")
        d_ready = sem("d_ready")
        eexp_ready = sem("eexp_ready")
        goh_ready = sem("goh_ready")
        ranked = sem("ranked")
        sel_ready = sem("sel_ready")
        comb_split = sem("comb_split")
        comb_hi = sem("comb_hi")
        comb_lo = sem("comb_lo")
        selT_done = sem("selT_done")
        selT_ready = sem("selT_ready")
        comb_done = sem("comb_done")
        comb_ready = sem("comb_ready")
        ctl_ready = sem("ctl_ready")
        slot_ready = sem("slot_ready")
        index_ready = sem("index_ready")
        selTg_ready = sem("selTg_ready")
        tokens_gathered = sem("tokens_gathered")
        xgf_ready = sem("xgf_ready")
        xghi_ready = sem("xghi_ready")
        xglo_ready = sem("xglo_ready")
        silu_ready = sem("silu_ready")
        hid_ready = sem("hid_ready")
        hid_turned = sem("hid_turned")
        hidThi_ready = sem("hidThi_ready")
        hidTlo_ready = sem("hidTlo_ready")
        yhi_ready = sem("yhi_ready")
        ylo_ready = sem("ylo_ready")
        scattered = sem("scattered")
        x2_ready = sem("x2_ready")
        y_ready = sem("y_ready")
        stored = sem("stored")

        block = ctx.enter_context(nc.Block())

        halves = {}
        for h0, c0, n in ((H_CQ, C_Q, QR), (H_CKV, C_KV, KVR + ROPE), (H_CB, C_CB, CW), (H_CC, C_CC, CW),
                          (H_CH, C_CH, CW), (H_SGV, C_SGV, SG), (H_SGU, C_SGU, SG)):
            for j in range(2):
                halves[h0 + j] = (win_d[:, 4 * j:4 * j + 4, c0:c0 + n], 4, n)
        halves[H_QUP] = (qup_d[:, 0:2, :], 2, HEADS * QK)
        halves[H_QUP + 1] = (qup_d[:, 2:3, :], 1, HEADS * QK)
        halves[H_KVUP] = (kvup_d[:, :, :], 2, HEADS * (NOPE + VH))
        for b, gcol in enumerate((C_GC, C_GB, C_GA)):
            for c in range(2):
                n, c0 = H_GATE + 6 * b + 3 * c, gcol + BANK * c
                for j in range(2):
                    halves[n + j] = (win_d[:, 4 * j:4 * j + 4, c0:c0 + BANK], 4, BANK)
                halves[n + 2] = (wout_d[b][:, :, BANK * c:BANK * c + BANK], 4, BANK)
        for j in range(2):
            for c in range(2):
                halves[H_WO + 2 * j + c] = (wo_d[:, 4 * j:4 * j + 4, BANK * c:BANK * c + BANK], 4, BANK)

        def half_view(buf, slots, n):
            _, blocks, cols = halves[n]
            return buf[:, n % slots, 0:blocks * cols].rearrange("p (k n) -> p k n", n=cols)

        def joined(banks):
            return banks.rearrange("p a b -> p (a b)")

        order = []
        for e in range(EPG):
            order += [("up0", e), ("up1", e)]
            if e:
                order.append(("down", e - 1))
        order.append(("down", EPG - 1))

        @block.sync
        def _(sp):
            for n in range(N_MIX):
                if n >= RAW:
                    sp.wait_ge(lo_ready, n - RAW + 1)
                sp.dma_start(half_view(raw, RAW, n), halves[n][0]).then_inc(raw_landed[n % RAW], 16)

            def load_group(first_expert, g):
                for j, (what, e) in enumerate(order):
                    n = N_MIX + j
                    if what == "down":
                        src = dn_d[bass.ds(first_expert + e, 1), :, :]
                    else:
                        k = int(what[2]) * HALF
                        src = gu_d[bass.ds(first_expert + e, 1), :, k:k + HALF]
                    sp.wait_ge(lo_ready, PER_GROUP * g + n - RAW + 1)
                    sp.dma_start(raw[:, n % RAW, :], src.rearrange("a p n -> (a p) n"))\
                      .then_inc(raw_landed[n % RAW], 16)

            with sp.Fori(0, NG) as g:
                load_group(g * EPG, g)
            sp.wait_ge(ctl_ready, 1)
            over = sp.value_load(ctl[0:1, 0:1], min_val=0, max_val=1)
            full = sp.value_load(ctl[0:1, 1:2], min_val=0, max_val=NG - 1)
            with sp.If(over > 0):
                load_group(full * EPG, NG)
            for t in range(T):
                sp.wait_ge(y_ready, t + 1)
                sp.dma_start(out_d[:, t, :], xs[:, t, :]).then_inc(stored, 16)
            sp.wait_ge(stored, 16 * T)

        @block.gpsimd
        def _(pool):
            count = [0]

            def then(ins):
                count[0] += 1
                ins.then_inc(pool_chain, 1)
                pool.wait_ge(pool_chain, count[0])

            pool.dma_start(g_mix[:], norm_mix[0].rearrange("(p k) -> p k", k=KD)).then_inc(mix_gain_in, 16)
            for i in range(R2):
                last = pool.memset(inv_f[:, i:i + 1], float(np.float32(10000.0 ** (-2 * i / ROPE))))
            last.then_inc(inv_ready, 1)
            then(pool.memset(neg_half[:], -0.5))
            then(pool.memset(ident[:], 0.0))
            then(pool.affine_select(ident[:], ident[:], [[-1, P]], ALU.not_equal, 1.0, base=0, channel_multiplier=1))
            pool.tensor_copy(ident_r[:], ident[:]).then_inc(consts_ready, 1)
            small = [
                (cw_raw[0:4 * TAPS, :], conv_w[0].rearrange("j (b p) -> (j b) p", p=P)),
                (cw_raw[4 * TAPS:, :], b_s[0]),
                (ws_raw[:], w_s[0].rearrange("g t s -> t g s")),
                (g_c[:, 0:KQ], q_norm[0].rearrange("(p k) -> p k", k=KQ)),
                (g_c[:, KQ:KC], kv_norm[0].rearrange("(p k) -> p k", k=KKV)),
                (g_sg[:], sg_norm[0].partition_broadcast(P)),
                (g_ffn[:], norm_ffn[0].rearrange("(p k) -> p k", k=KD)),
                (rt_raw[:], w_group_router[0].rearrange("(p k) n -> p k n", k=KD)),
                (w_rt[:, :, NG:], w_expert_router[0].rearrange("(p k) n -> p k n", k=KD)),
                (b_rt[:, 0:NG], b_group_router[0].partition_broadcast(P)),
                (b_rt[:, NG:], b_expert_router[0].partition_broadcast(P)),
                (g_fin[:], final_norm.partition_broadcast(P)),
            ]
            for dst, src in small:
                pool.dma_start(dst, src).then_inc(small_in, 16)

            def root(norm):
                pool.wait_ge(ms_ready, norm + 1)
                pool.tensor_tensor(stat[:, norm, 2, :], stat[:, norm, 1, :], neg_half[:], ALU.pow)\
                    .then_inc(root_ready, 1)

            root(0)
            then(pool.memset(ones[:], 1.0))
            then(pool.memset(causal[:], 0.0))
            pool.affine_select(causal[:, P:], causal[:, P:], [[-1, P]], ALU.is_ge, NEG, base=0, channel_multiplier=1)
            pool.affine_select(before[:], ones[:], [[1, P]], ALU.is_gt, 0.0, base=0, channel_multiplier=-1)
            pool.memset(z_sb[:, :, 0:TAPS - 1], 0.0).then_inc(zpad_ready, 1)
            root(1)
            pool.wait_ge(small_in, 16 * len(small))
            pool.tensor_copy(w_rt[:, :, 0:NG], rt_raw[:]).then_inc(router_w_ready, 1)
            root(2)
            pool.wait_ge(wsT_ready, 1)
            pool.affine_select(wsT[:], wsT[:], [[0, SGG], [1, P]], ALU.is_ge, 0.0, base=0, channel_multiplier=-1)\
                .then_inc(wsT_masked, 1)
            root(3)
            root(4)
            pool.iota(slot_i[:], [[1, P]], base=0, channel_multiplier=0).then_inc(slot_ready, 1)
            pool.wait_ge(slot_ready, 1)
            then(pool.tensor_copy(slot_f[:], slot_i[:]))
            then(pool.tensor_scalar(idx_g[:], slot_f[:, 0:NG], BIG, None, ALU.add))
            pool.tensor_scalar(idx_e[:], slot_f[:, 0:EPG], BIG, None, ALU.add).then_inc(index_ready, 1)
            then(pool.memset(y_hi[:].bitcast(F32), 0.0))
            pool.memset(y_lo[:].bitcast(F32), 0.0).then_inc(ylo_ready, 1)
            pool.memset(selT_g[:].bitcast(F32), 0.0).then_inc(selTg_ready, 1)

            pool.wait_ge(selT_ready, 1)
            with pool.Fori(0, NG) as g:
                pool.wait_ge(scattered, g + 1)
                pool.tensor_copy(selT_g[:], selT[:, bass.ds(g, 1), :].rearrange("p a n -> p (a n)"))\
                    .then_inc(selTg_ready, 1)
            pool.wait_ge(ctl_ready, 1)
            over = pool.value_load(ctl[0:1, 0:1], min_val=0, max_val=1)
            with pool.If(over > 0):
                pool.wait_ge(scattered, NG + 1)
                pool.tensor_copy(selT_g[:], selT[:, NG, :]).then_inc(selTg_ready, 1)
            root(5)

        @block.scalar
        def _(act):
            def split_hi(n, g=None):
                shift, slots = (0, 0) if g is None else (PER_GROUP * g, 16 * (PER_GROUP // RAW) * g)
                act.wait_ge(raw_landed[n % RAW], slots + 16 * (n // RAW + 1))
                if n >= SPLIT:
                    act.wait_ge(half_used, shift + n - SPLIT + 1)
                if n < N_MIX:
                    dst, src = half_view(w_hi, SPLIT, n), half_view(raw, RAW, n)
                else:
                    dst, src = w_hi[:, n % SPLIT, :], raw[:, n % RAW, :]
                act.activation(dst, src, ACT.Copy).then_inc(hi_ready, 1)

            def squares(norm, t, src, junk):
                act.activation(junk, src, ACT.Square, accum_out=stat[:, norm, 0, t:t + 1]).then_inc(ssq_ready, 1)

            for t in range(T):
                act.dma_start(pos_i[:, t:t + 1], positions[0, P * t:P * t + P].rearrange("(p a) -> p a", a=1))\
                   .then_inc(pos_in, 16)
            for t in range(T):
                act.dma_start(xs[:, t, :], x_d[:, t, :]).then_inc(x_in, 16)
            split_hi(0)
            act.wait_ge(x_in, 16 * T)
            for t in range(T):
                squares(0, t, xs[:, t, :], h_f[:, 4 * t:4 * t + 4, :].rearrange("p a b -> p (a b)"))
            act.wait_ge(ang_ready, 1)
            act.activation(rot[:], ang[:, 0:2, :, :], ACT.Sin).then_inc(rot_ready, 1)
            split_hi(1)
            for b in range(2 * T):
                t, k = b // 2, 4 * (b % 2)
                v = slice(P * t, P * t + P)
                act.wait_ge(hf_ready, b + 1)
                act.activation(hT_hi[:, k:k + 4, v], h_f[:, k:k + 4, v], ACT.Copy).then_inc(hThi_ready, 1)

            def attention_exp(u):
                t, pair = divmod(u, HEADS // 2)
                act.wait_ge(rowmax_ready, u + 1)
                for h in range(2):
                    i = HEADS * t + 2 * pair + h
                    row = pr[:, u % 2, h, 0:P * (t + 1)]
                    act.activation(row, row, ACT.Exp, bias=nmax[:, i:i + 1], scale=SCALE,
                                   accum_out=rsum[:, i:i + 1]).then_inc(exp_ready, 1)

            def attention_pT(u):
                n = 2 * (u // (HEADS // 2) + 1)
                act.wait_ge(p_turned, u + 1)
                act.activation(pT[:, u % 2, 0:n, :], ps[:, 6, 0:n * P].rearrange("p (a b) -> p a b", b=P), ACT.Copy)\
                    .then_inc(pT_ready, 1)

            def branch_turned_hi(i, t):
                act.wait_ge(branch_turned, i + 1)
                act.activation(bT_hi[:, :, P * t:P * t + P], ps[:, 5, :].rearrange("p (a b) -> p a b", b=P), ACT.Copy)\
                    .then_inc(bThi_ready, 1)

            for n in range(N_MIX):
                if n + AHEAD < N_MIX:
                    split_hi(n + AHEAD)
                else:
                    split_hi(n + AHEAD, 0)
                if n == H_CKV:
                    act.wait_ge(half_used, H_CKV)
                    for t in range(T):
                        squares(1, t, ps[:, t, 0:QR], xn[:, t, 0:QR])
                if n == H_CB:
                    act.wait_ge(half_used, H_CB)
                    for t in range(T):
                        squares(2, t, ps[:, 2 + t, 0:KVR], xn[:, t, QR:QR + KVR])
                if n == H_CC:
                    act.wait_ge(half_used, H_CC)
                    act.activation(cb_sb[:].rearrange("p a b -> p (a b)"), joined(ps[:, 0:2, :]), ACT.Copy)\
                        .then_inc(cb_ready, 1)
                    act.wait_ge(cTf_ready, 1)
                    act.activation(cT_hi[:], cT_f[:], ACT.Copy).then_inc(cThi_ready, 1)
                if n == H_QUP:
                    act.wait_ge(half_used, H_QUP)
                    act.activation(z_sb[:, :, TAPS - 1:], joined(ps[:, 2:4, :]).rearrange("p (a b) -> p a b", b=SEQ),
                                   ACT.Copy).then_inc(cc_ready, 1)
                if n == H_KVUP:
                    act.wait_ge(half_used, H_KVUP)
                    for t in range(T):
                        act.activation(q9[:, t, 0:HEADS, :].rearrange("p h d -> p (h d)"),
                                       joined(ps[:, 2 * t:2 * t + 2, :])[:, 0:HEADS * QK],
                                       ACT.Copy).then_inc(q_ready, 1)
                if n == H_CH:
                    act.wait_ge(half_used, H_CH)
                    for t in range(T):
                        kv = joined(ps[:, 4 + 2 * t:6 + 2 * t, :]).rearrange("p (h d) -> p h d", d=NOPE + VH)
                        act.activation(kk[:, t, :, 0:NOPE], kv[:, :, 0:NOPE], ACT.Copy).then_inc(kv_ready, 1)
                        act.activation(v_sb[:, t, :, :], kv[:, :, NOPE:], ACT.Copy).then_inc(kv_ready, 1)
                if n in (H_SGV, H_SGV + 1):
                    t = n - H_SGV
                    act.wait_ge(qk_turned, t + 1)
                    act.activation(qT[:, :, P * t:P * t + P],
                                   joined(ps[0:QK, 4:6, :]).rearrange("p (a b) -> p a b", b=P), ACT.Copy)\
                        .then_inc(qT_ready, 1)
                if n == H_SGU:
                    act.wait_ge(half_used, H_SGU)
                    for t in range(T):
                        act.activation(gv[:, t, :], ps[:, 2 + t, :], ACT.Gelu_apprx_tanh).then_inc(gv_ready, 1)
                    act.wait_ge(gv_ready, T)
                    for t in range(T):
                        squares(3, t, gv[:, t, :], merged[:, t, 0:SG])
                    act.wait_ge(bTf_ready, 1)
                    act.activation(bT_hi[:], bT_f[:], ACT.Copy).then_inc(bThi_ready, 1)
                if n == H_GATE:
                    act.wait_ge(half_used, H_GATE)
                    for t in range(T):
                        act.activation(gu_s[:, t, :], ps[:, t, :], ACT.Gelu_apprx_tanh).then_inc(gu_ready, 1)
                if 0 <= n - H_ATT - 2 < UNITS:
                    attention_pT(n - H_ATT - 2)
                if 0 <= n - H_ATT - 1 < UNITS:
                    attention_exp(n - H_ATT - 1)
                for b in (1, 2):
                    for t in range(T):
                        if n == H_GATE + 6 * b + t:
                            branch_turned_hi(T * (b - 1) + t, t)
                for c in range(6):
                    if n == H_GATE + 3 * c + 2:
                        act.wait_ge(half_used, H_GATE + 3 * c + 2)
                        act.wait_ge(gvn_ready if not c else merged_ready, T * max(c, 1))
                        if not c:
                            act.wait_ge(mixed_done, T)
                        for t in range(T):
                            act.activation(gv[:, t, :], ps[:, 2 + t, :], ACT.Tanh, scale=0.5).then_inc(gate_ready, 1)
                if n in (H_WO - 1, H_WO + 1):
                    for b in ((0, 1) if n < H_WO else (2, 3)):
                        t, k = b % 2, 4 * (b // 2)
                        act.wait_ge(m_turned, b + 1)
                        act.activation(hT_hi[:, k:k + 4, P * t:P * t + P],
                                       ps[:, 4 + b, :].rearrange("p (a b) -> p a b", b=P), ACT.Copy, scale=0.5)\
                            .then_inc(mhi_ready, 1)

            for t in range(T):
                act.wait_ge(x1_ready, T + t + 1)
                squares(4, t, xs[:, t, :], sq[:, t, :])
            for t in range(T):
                act.wait_ge(xn2_ready, t + 1)
                act.activation(xn_hi[:, t, :], xn2[:, t, :], ACT.Copy).then_inc(xnhi_ready, 1)
            act.wait_ge(gmax_ready, 1)
            act.activation(gt[:, 1, :, :], gt[:, 0, :, :], ACT.Exp).then_inc(gexp_ready, 1)
            act.wait_ge(d_ready, 1)
            act.activation(sc[:, 8, :, :], sc[:, 7, :, :], ACT.Exp).then_inc(eexp_ready, 1)
            act.wait_ge(comb_split, 1)
            act.activation(c_hi[:], et[:, 7, :, :], ACT.Copy).then_inc(comb_hi, 1)
            act.wait_ge(selT_done, 1)
            act.activation(selT[:].rearrange("p a b -> p (a b)"), joined(ps[:, 2:5, :])[:, 0:(NG + 1) * SEQ], ACT.Copy)\
                .then_inc(selT_ready, 1)

            def gathered_hi(g, h):
                act.wait_ge(xgf_ready, 2 * g + h + 1)
                act.activation(xg_hi[:, 4 * h:4 * h + 4, :], xg_f[:, 4 * h:4 * h + 4, :], ACT.Copy)\
                    .then_inc(xghi_ready, 1)

            def turned_hi(e, g):
                act.wait_ge(hid_turned, EPG * g + e + 1)
                act.activation(hidT_hi[:, e % 2, :, :], ps[:, e % 2, 0:DE].rearrange("p (a b) -> p a b", b=P),
                               ACT.Copy).then_inc(hidThi_ready, 1)

            def gate(e, g):
                act.wait_ge(half_used, PER_GROUP * g + N_MIX + order.index(("up1", e)) + 1)
                act.activation(silu[:, e % 2, :], ps[:, e % 2, 0:DE], ACT.Silu).then_inc(silu_ready, 1)

            def group(g, first, more):
                if first:
                    for j in range(AHEAD):
                        split_hi(N_MIX + j, g)
                for j, (what, e) in enumerate(order):
                    if what == "up0" and e == 1:
                        gate(0, g)
                    if what == "up1" and e:
                        turned_hi(e - 1, g)
                    if what == "down" and e < EPG - 1:
                        gate(e + 1, g)
                    if what == "down" and e == EPG - 1:
                        turned_hi(e, g)
                        if more:
                            gathered_hi(g + 1, 0)
                    if more or j + AHEAD < PER_GROUP:
                        split_hi(N_MIX + j + AHEAD, g)
                if more:
                    gathered_hi(g + 1, 1)
                act.wait_ge(half_used, PER_GROUP * g + N_MIX + PER_GROUP)
                act.wait_ge(scattered, g + 1)
                act.activation(y_hi[:], joined(ps[:, 2:4, :]), ACT.Copy).then_inc(yhi_ready, 1)

            gathered_hi(0, 0)
            gathered_hi(0, 1)
            with act.Fori(0, NG - 1) as g:
                group(g, False, True)
            group(NG - 1, False, False)
            act.wait_ge(ctl_ready, 1)
            over = act.value_load(ctl[0:1, 0:1], min_val=0, max_val=1)
            with act.If(over > 0):
                gathered_hi(NG, 0)
                gathered_hi(NG, 1)
                group(NG, True, False)
            for t in range(T):
                act.wait_ge(x2_ready, t + 1)
                squares(5, t, x2[:, t, :], sq[:, t, :])

        @block.vector
        def _(dve):
            counts = {}

            def then(ins, signal=dve_chain):
                counts[id(signal)] = counts.get(id(signal), 0) + 1
                ins.then_inc(signal, 1)
                dve.wait_ge(signal, counts[id(signal)])

            def split_lo(n, g=None):
                shift = 0 if g is None else PER_GROUP * g
                dve.wait_ge(hi_ready, shift + n + 1)
                if n < N_MIX:
                    dst, src, hi = half_view(w_lo, SPLIT, n), half_view(raw, RAW, n), half_view(w_hi, SPLIT, n)
                else:
                    dst, src, hi = w_lo[:, n % SPLIT, :], raw[:, n % RAW, :], w_hi[:, n % SPLIT, :]
                dve.tensor_tensor(dst, src, hi, ALU.subtract).then_inc(lo_ready, 1)

            def mean_square(norm, width):
                dve.wait_ge(ssq_ready, T * (norm + 1))
                dve.tensor_scalar(stat[:, norm, 1, :], stat[:, norm, 0, :], 1.0 / width, EPS, ALU.mult, ALU.add)\
                   .then_inc(ms_ready, 1)

            def refine(norm):
                ms, r, a = (stat[:, norm, i, :] for i in (1, 2, 3))
                dve.wait_ge(root_ready, norm + 1)
                dve.wait_ge(ms_ready, norm + 1)
                then(dve.tensor_tensor(a, r, r, ALU.mult))
                then(dve.scalar_tensor_tensor(a, a, -0.5, ms, ALU.mult, ALU.mult))
                then(dve.scalar_tensor_tensor(r, a, 1.5, r, ALU.add, ALU.mult))
                return r

            dve.wait_ge(pos_in, 16 * T)
            then(dve.tensor_copy(pos_f[:], pos_i[:]))
            dve.wait_ge(inv_ready, 1)
            a0, a1, turns, far = (ang[:, i, :, :] for i in range(4))
            for t in range(T):
                last = dve.tensor_scalar(ang[:, 0, t, :], inv_f[:], pos_f[:, t:t + 1], None, ALU.mult)
            then(last)
            then(dve.tensor_scalar(turns, a0, 1.0 / (2 * np.pi), MAGIC, ALU.mult, ALU.add))
            then(dve.tensor_scalar(turns, turns, -MAGIC, None, ALU.add))
            for part in two_pi_parts():
                then(dve.scalar_tensor_tensor(a0, turns, -part, a0, ALU.mult, ALU.add))
            then(dve.tensor_scalar(a1, a0, np.pi / 2, None, ALU.add))
            then(dve.tensor_scalar(far, a1, np.pi, 2 * np.pi, ALU.is_gt, ALU.mult))
            then(dve.tensor_tensor(a1, a1, far, ALU.subtract))
            limit = float(np.nextafter(np.float32(np.pi), np.float32(0)))
            dve.tensor_scalar(ang[:, 0:2, :, :], ang[:, 0:2, :, :], limit, -limit, ALU.min, ALU.max)\
               .then_inc(ang_ready, 1)

            mean_square(0, D)
            split_lo(0)
            r = refine(0)
            for t in range(T):
                dve.tensor_scalar(xn[:, t, :], xs[:, t, :], r[:, t:t + 1], None, ALU.mult).then_inc(xn_ready, 1)
            dve.wait_ge(mix_gain_in, 16)
            for b in range(2 * T):
                t, k = b // 2, 4 * (b % 2)
                dve.wait_ge(h_turned, b + 1)
                dve.tensor_tensor(h_f[:, k:k + 4, P * t:P * t + P], ps[:, 4 + b, :].rearrange("p (a b) -> p a b", b=P),
                                  g_mix[:, k:k + 4].unsqueeze(2).to_broadcast([P, 4, P]), ALU.mult)\
                   .then_inc(hf_ready, 1)
            for b in range(2 * T):
                t, k = b // 2, 4 * (b % 2)
                v = slice(P * t, P * t + P)
                dve.wait_ge(hThi_ready, b + 1)
                dve.tensor_tensor(hT_lo[:, k:k + 4, v], h_f[:, k:k + 4, v], hT_hi[:, k:k + 4, v], ALU.subtract)\
                   .then_inc(hTlo_ready, 1)
            split_lo(1)

            def attention_scores(u):
                t, pair = divmod(u, HEADS // 2)
                keys = P * (t + 1)
                i = HEADS * t + 2 * pair
                dve.wait_ge(scored, u + 1)
                then(dve.tensor_tensor(pr[:, u % 2, :, 0:keys], ps[:, 4, 0:2 * keys].rearrange("p (h k) -> p h k", k=keys),
                                       causal[:, SEQ - keys:].unsqueeze(1).to_broadcast([P, 2, keys]), ALU.add))
                then(dve.tensor_reduce(rmax[:, i:i + 2], pr[:, u % 2, :, 0:keys], AX_X, ALU.max))
                dve.tensor_scalar(nmax[:, i:i + 2], rmax[:, i:i + 2], -SCALE, None, ALU.mult)\
                   .then_inc(rowmax_ready, 1)

            def attention_out(t):
                v = slice(HEADS * t, HEADS * t + HEADS)
                dve.wait_ge(exp_ready, HEADS * (t + 1))
                then(dve.reciprocal(rinv[:, v], rsum[:, v]))
                dve.wait_ge(pv_done, UNITS // T * (t + 1))
                dve.tensor_tensor(o_sb[:, t, :].rearrange("p (h d) -> p h d", d=VH),
                                  ps[:, 7, :].rearrange("p (h d) -> p h d", d=VH),
                                  rinv[:, v].unsqueeze(2).to_broadcast([P, HEADS, VH]), ALU.mult)\
                   .then_inc(o_ready, 1)

            def branch_turned_lo(i, t):
                v = slice(P * t, P * t + P)
                dve.wait_ge(bThi_ready, 1 + i + 1)
                dve.tensor_tensor(bT_lo[:, :, v], ps[:, 5, :].rearrange("p (a b) -> p a b", b=P), bT_hi[:, :, v],
                                  ALU.subtract).then_inc(bTlo_ready, 1)

            def merge(c):
                b, cols = c // 2, slice(BANK * (c % 2), BANK * (c % 2) + BANK)
                dve.wait_ge(half_used, H_GATE + 3 * c + 3)
                dve.wait_ge(gate_ready, T * (c + 1))
                if b:
                    for t in range(T):
                        last = dve.scalar_tensor_tensor(gv[:, t, :], gv[:, t, :], 1.0, ps[:, t, :], ALU.add, ALU.mult)
                    then(last)
                for t in range(T):
                    if b:
                        ins = dve.tensor_tensor(merged[:, t, cols], merged[:, t, cols], gv[:, t, :], ALU.add)
                    else:
                        ins = dve.scalar_tensor_tensor(merged[:, t, cols], gv[:, t, :], 1.0, ps[:, t, :],
                                                       ALU.add, ALU.mult)
                    ins.then_inc(merged_ready, 1)

            for n in range(N_MIX):
                if n == H_CKV:
                    mean_square(1, QR)
                if n == H_CB:
                    mean_square(2, KVR)
                if n == H_SGV:
                    dve.wait_ge(qk_turned, 1)
                    dve.tensor_copy(kT[:, :, 0:P], joined(ps[0:QK, 6:8, :]).rearrange("p (a b) -> p a b", b=P))\
                       .then_inc(kT_ready, 1)
                if n + AHEAD < N_MIX:
                    split_lo(n + AHEAD)
                else:
                    split_lo(n + AHEAD, 0)
                if n == H_CKV:
                    r = refine(1)
                    for t in range(T):
                        dve.tensor_scalar(cn[:, t, 0:QR], ps[:, t, 0:QR], r[:, t:t + 1], None, ALU.mult)\
                           .then_inc(cn_ready, 1)
                if n == H_CB:
                    r = refine(2)
                    for t in range(T):
                        dve.tensor_copy(q9[:, t, HEADS, NOPE:], ps[:, 2 + t, KVR:KVR + ROPE])
                        dve.tensor_scalar(cn[:, t, QR:], ps[:, 2 + t, 0:KVR], r[:, t:t + 1], None, ALU.mult)\
                           .then_inc(cn_ready, 1)
                    dve.wait_ge(small_turned, 1)
                    dve.tensor_copy(taps[:], ps[:, 4, 0:4 * TAPS + SGG]).then_inc(taps_ready, 1)
                    dve.tensor_copy(wsT[:], ps[:, 5, :].rearrange("p (a b) -> p a b", b=P)).then_inc(wsT_ready, 1)
                if n == H_CC:
                    dve.wait_ge(small_in, 16 * 12)
                    dve.wait_ge(c_turned, 1)
                    dve.tensor_tensor(cT_f[:], joined(ps[:, 4:7, :])[:, 0:KC * SEQ].rearrange("p (a b) -> p a b", b=SEQ),
                                      g_c[:].unsqueeze(2).to_broadcast([P, KC, SEQ]), ALU.mult).then_inc(cTf_ready, 1)
                if n == H_CC + 1:
                    dve.wait_ge(cThi_ready, 1)
                    dve.tensor_tensor(cT_lo[:], cT_f[:], cT_hi[:], ALU.subtract).then_inc(cTlo_ready, 1)
                if n == H_CH:
                    dve.wait_ge(q_ready, T)
                    dve.wait_ge(rot_ready, 1)
                    one, two = q9[:, :, :, NOPE:NOPE + R2], q9[:, :, :, NOPE + R2:]
                    sin, cos = (rot[:, i, :, :].unsqueeze(2).to_broadcast([P, T, HEADS + 1, R2]) for i in range(2))
                    dve.tensor_tensor(rt[:, 0, :, :, :], one, cos, ALU.mult)
                    dve.tensor_tensor(rt[:, 1, :, :, :], two, sin, ALU.mult)
                    dve.tensor_tensor(rt[:, 2, :, :, :], two, cos, ALU.mult)
                    then(dve.tensor_tensor(rt[:, 3, :, :, :], one, sin, ALU.mult))
                    dve.tensor_tensor(one, rt[:, 0, :, :, :], rt[:, 1, :, :, :], ALU.subtract)
                    then(dve.tensor_tensor(two, rt[:, 2, :, :, :], rt[:, 3, :, :, :], ALU.add))
                    for t in range(T):
                        dve.tensor_copy(kk[:, t, :, NOPE:], q9[:, t, HEADS:, NOPE:].to_broadcast([P, HEADS, ROPE]))\
                           .then_inc(rope_ready, 1)
                if n == H_SGV:
                    dve.wait_ge(half_used, H_SGV)
                    dve.wait_ge(cc_ready, 1)
                    dve.wait_ge(zpad_ready, 1)
                    z = z_sb[:, :, TAPS - 1:]
                    then(dve.tensor_tensor(z, joined(ps[:, 0:2, :]).rearrange("p (a b) -> p a b", b=SEQ), z, ALU.mult),
                         z_ready)
                if n == H_SGV + 1:
                    dve.wait_ge(qk_turned, 2)
                    dve.tensor_copy(kT[:, :, P:], joined(ps[0:QK, 6:8, :]).rearrange("p (a b) -> p a b", b=P))\
                       .then_inc(kT_ready, 1)
                    dve.wait_ge(cb_ready, 1)
                    for j in range(TAPS):
                        for b in range(4):
                            w, zj = taps[:, 4 * j + b:4 * j + b + 1], z_sb[:, b, j:j + SEQ]
                            if j == 0:
                                last = dve.tensor_scalar(bT_f[:, b, :], zj, w, None, ALU.mult)
                            else:
                                last = dve.scalar_tensor_tensor(bT_f[:, b, :], zj, w, bT_f[:, b, :], ALU.mult, ALU.add)
                        then(last)
                    dve.tensor_tensor(bT_f[:], bT_f[:], cb_sb[:], ALU.mult).then_inc(bTf_ready, 1)
                if n == H_SGU:
                    dve.wait_ge(bThi_ready, 1)
                    dve.tensor_tensor(bT_lo[:], bT_f[:], bT_hi[:], ALU.subtract).then_inc(bTlo_ready, 1)
                    mean_square(3, SG)
                if 0 <= n - H_ATT - 1 < UNITS:
                    attention_scores(n - H_ATT - 1)
                if n == H_SGU + 1:
                    r = refine(3)
                    for t in range(T):
                        dve.scalar_tensor_tensor(gv[:, t, :], gv[:, t, :], r[:, t:t + 1], g_sg[:], ALU.mult, ALU.mult)\
                           .then_inc(gvn_ready, 1)
                for t in range(T):
                    if n == H_GATE + 1 + t:
                        dve.wait_ge(mixed_done, t + 1)
                        dve.wait_ge(gu_ready, T)
                        for g in range(SGG):
                            v = slice(P * g, P * g + P)
                            last = dve.scalar_tensor_tensor(gu_s[:, t, v], ps[:, 5, v],
                                                            taps[:, 4 * TAPS + g:4 * TAPS + g + 1],
                                                            gu_s[:, t, v], ALU.add, ALU.mult)
                        last.then_inc(sgy_ready, 1)
                for t in range(T):
                    if n == H_ATT + UNITS // T * (t + 1) + 2:
                        attention_out(t)
                for b in (1, 2):
                    for t in range(T):
                        if n == H_GATE + 6 * b + t:
                            branch_turned_lo(T * (b - 1) + t, t)
                for c in range(6):
                    if n == H_GATE + 3 * c + 3:
                        merge(c)
                if n in (H_WO - 1, H_WO + 1):
                    for b in ((0, 1) if n < H_WO else (2, 3)):
                        t, k = b % 2, 4 * (b // 2)
                        v = slice(P * t, P * t + P)
                        dve.wait_ge(mhi_ready, b + 1)
                        dve.scalar_tensor_tensor(hT_lo[:, k:k + 4, v], ps[:, 4 + b, :].rearrange("p (a b) -> p a b", b=P),
                                                 0.5, hT_hi[:, k:k + 4, v], ALU.mult, ALU.subtract)\
                           .then_inc(mlo_ready, 1)

            for c in range(2):
                dve.wait_ge(half_used, H_WO + 3 + c)
                for t in range(T):
                    v = slice(BANK * c, BANK * c + BANK)
                    dve.tensor_tensor(xs[:, t, v], xs[:, t, v], ps[:, 2 - 2 * c + t, :], ALU.add)\
                       .then_inc(x1_ready, 1)
            mean_square(4, D)
            r = refine(4)
            for t in range(T):
                dve.tensor_scalar(xn2[:, t, :], xs[:, t, :], r[:, t:t + 1], None, ALU.mult).then_inc(xn2_ready, 1)
            for b in range(2 * T):
                t, k = b // 2, 4 * (b % 2)
                dve.wait_ge(x_turned, b + 1)
                dve.tensor_tensor(h2T[:, k:k + 4, P * t:P * t + P], ps[:, 4 + b, :].rearrange("p (a b) -> p a b", b=P),
                                  g_ffn[:, k:k + 4].unsqueeze(2).to_broadcast([P, 4, P]), ALU.mult)\
                   .then_inc(h2T_ready, 1)
            for t in range(T):
                dve.wait_ge(xnhi_ready, t + 1)
                dve.tensor_tensor(xn_lo[:, t, :], xn2[:, t, :], xn_hi[:, t, :], ALU.subtract).then_inc(xnlo_ready, 1)

            def over(ap, n):
                return ap.to_broadcast([P, T, n])

            def one_hot(out, values, best, index, n, tmp, low):
                then(dve.tensor_reduce(best, values, AX_X, ALU.max))
                then(dve.tensor_tensor(tmp, values, over(best, n), ALU.is_equal))
                then(dve.scalar_tensor_tensor(tmp, tmp, -BIG, index[:].unsqueeze(1).to_broadcast([P, T, n]),
                                              ALU.mult, ALU.add))
                then(dve.tensor_reduce(low, tmp, AX_X, ALU.min))
                return dve.tensor_tensor(out, tmp, over(low, n), ALU.is_equal)

            scal = [sc[:, i, :, :] for i in range(14)]
            dve.wait_ge(logits_done, 1)
            then(dve.tensor_tensor(lg[:], ps[:, 0, 0:T * NR].rearrange("p (t n) -> p t n", n=NR),
                                   b_rt[:].unsqueeze(1).to_broadcast([P, T, NR]), ALU.add))
            dve.wait_ge(index_ready, 1)
            goh = gt[:, 3, :, :]
            then(one_hot(goh, lg[:, :, 0:NG], scal[0], idx_g, NG, gt[:, 2, :, :], scal[1]), goh_ready)
            dve.tensor_tensor(gt[:, 0, :, :], lg[:, :, 0:NG], over(scal[0], NG), ALU.subtract).then_inc(gmax_ready, 1)
            then(dve.tensor_tensor(eg[:], lg[:, :, NG:].rearrange("p t (g e) -> p t g e", e=EPG),
                                   goh.unsqueeze(3).to_broadcast([P, T, NG, EPG]), ALU.mult))
            chosen = et[:, 0, :, :]
            then(dve.tensor_reduce(chosen, eg[:].rearrange("p t g e -> p t e g"), AX_X, ALU.add))
            first, rest, second = et[:, 2, :, :], et[:, 3, :, :], et[:, 4, :, :]
            then(one_hot(first, chosen, scal[2], idx_e, EPG, et[:, 1, :, :], scal[3]))
            then(dve.scalar_tensor_tensor(rest, first, LOWEST, chosen, ALU.mult, ALU.add))
            then(one_hot(second, rest, scal[4], idx_e, EPG, et[:, 1, :, :], scal[5]))
            dve.tensor_tensor(scal[7], scal[4], scal[2], ALU.subtract).then_inc(d_ready, 1)
            dve.wait_ge(ranked, 1)
            then(dve.tensor_tensor(gt[:, 4, :, :], ps[:, 1, 0:T * NG].rearrange("p (t g) -> p t g", g=NG), goh, ALU.mult))
            then(dve.tensor_reduce(scal[6], gt[:, 4, :, :], AX_X, ALU.add))
            then(dve.tensor_scalar(scal[12], scal[6], -float(P), None, ALU.add))
            for t in range(T):
                for g in range(NG):
                    dve.tensor_scalar(sel[:, t, P * g:P * g + P], slot_f[:], scal[6][:, t, :], goh[:, t, g:g + 1],
                                      ALU.is_equal, ALU.mult).then_inc(sel_ready, 1)
                dve.tensor_scalar(sel[:, t, P * NG:], slot_f[:], scal[12][:, t, :], None, ALU.is_equal)\
                   .then_inc(sel_ready, 1)
            dve.wait_ge(gexp_ready, 1)
            then(dve.tensor_reduce(scal[9], gt[:, 1, :, :], AX_X, ALU.add))
            dve.wait_ge(eexp_ready, 1)
            then(dve.scalar_tensor_tensor(scal[10], scal[8], 1.0, scal[9], ALU.add, ALU.mult))
            then(dve.reciprocal(scal[11], scal[10]))
            then(dve.tensor_tensor(scal[13], scal[11], scal[8], ALU.mult))
            dve.tensor_tensor(et[:, 5, :, :], first, over(scal[11], EPG), ALU.mult)
            then(dve.tensor_tensor(et[:, 6, :, :], second, over(scal[13], EPG), ALU.mult))
            then(dve.tensor_tensor(et[:, 7, :, :], et[:, 5, :, :], et[:, 6, :, :], ALU.add), comb_split)
            dve.wait_ge(comb_hi, 1)
            dve.tensor_tensor(c_lo[:], et[:, 7, :, :], c_hi[:], ALU.subtract).then_inc(comb_lo, 1)
            counted = ps[:, 1, T * NG:T * NG + NG]
            then(dve.tensor_scalar(cnt[:, 0, :], counted, float(P), None, ALU.is_gt))
            then(dve.scalar_tensor_tensor(cnt[:, 1, :], idx_g[:], -BIG, cnt[:, 0, :], ALU.add, ALU.mult))
            dve.tensor_reduce(ctl_f[:, 0:1], cnt[:, 0, :], AX_X, ALU.add)
            then(dve.tensor_reduce(ctl_f[:, 1:2], cnt[:, 1, :], AX_X, ALU.add))
            dve.tensor_copy(ctl[:], ctl_f[:, 0:2]).then_inc(ctl_ready, 1)
            dve.wait_ge(comb_done, 1)
            dve.tensor_copy(comb[:].rearrange("p g e -> p (g e)"), ps[:, 5, 0:(NG + 1) * EPG]).then_inc(comb_ready, 1)

            def gathered(g, h):
                dve.wait_ge(tokens_gathered, 2 * g + h + 1)
                dve.tensor_tensor(xg_f[:, 4 * h:4 * h + 4, :], ps[:, h, :].rearrange("p (a b) -> p a b", b=P),
                                  g_ffn[:, 4 * h:4 * h + 4].unsqueeze(2).to_broadcast([P, 4, P]), ALU.mult)\
                   .then_inc(xgf_ready, 1)

            def gathered_lo(g, h):
                dve.wait_ge(xghi_ready, 2 * g + h + 1)
                dve.wait_ge(xgf_ready, 2 * g + h + 1)
                v = slice(4 * h, 4 * h + 4)
                dve.tensor_tensor(xg_lo[:, v, :], xg_f[:, v, :], xg_hi[:, v, :], ALU.subtract).then_inc(xglo_ready, 1)

            def turned_lo(e, g):
                dve.wait_ge(hidThi_ready, EPG * g + e + 1)
                dve.tensor_tensor(hidT_lo[:, e % 2, :, :], ps[:, e % 2, 0:DE].rearrange("p (a b) -> p a b", b=P),
                                  hidT_hi[:, e % 2, :, :], ALU.subtract).then_inc(hidTlo_ready, 1)

            def hidden(e, g):
                dve.wait_ge(silu_ready, EPG * g + e + 1)
                dve.scalar_tensor_tensor(hid[:, e % 2, :], silu[:, e % 2, :],
                                         comb[:, bass.ds(g, 1), e:e + 1].rearrange("p a b -> p (a b)"),
                                         ps[:, e % 2, DE:2 * DE], ALU.mult, ALU.mult).then_inc(hid_ready, 1)

            def group(g, first, more):
                if first:
                    for j in range(AHEAD):
                        split_lo(N_MIX + j, g)
                for j, (what, e) in enumerate(order):
                    if what == "up0" and e == 1:
                        hidden(0, g)
                    if what == "up1" and e:
                        turned_lo(e - 1, g)
                    if what == "down" and e < EPG - 1:
                        hidden(e + 1, g)
                    if what == "down" and e == EPG - 1:
                        turned_lo(e, g)
                        if more:
                            gathered(g + 1, 0)
                            gathered_lo(g + 1, 0)
                    if more or j + AHEAD < PER_GROUP:
                        split_lo(N_MIX + j + AHEAD, g)
                if more:
                    gathered(g + 1, 1)
                    gathered_lo(g + 1, 1)
                dve.wait_ge(yhi_ready, g + 1)
                dve.tensor_tensor(y_lo[:], joined(ps[:, 2:4, :]), y_hi[:], ALU.subtract).then_inc(ylo_ready, 1)

            gathered(0, 0)
            gathered(0, 1)
            gathered_lo(0, 0)
            gathered_lo(0, 1)
            with dve.Fori(0, NG - 1) as g:
                group(g, False, True)
            group(NG - 1, False, False)
            dve.wait_ge(ctl_ready, 1)
            more_tokens = dve.value_load(ctl[0:1, 0:1], min_val=0, max_val=1)
            with dve.If(more_tokens > 0):
                gathered(NG, 0)
                gathered(NG, 1)
                gathered_lo(NG, 0)
                gathered_lo(NG, 1)
                group(NG, True, False)
            dve.wait_ge(scattered, more_tokens + NG + 1)
            for t in range(T):
                dve.tensor_tensor(x2[:, t, :], xs[:, t, :], joined(ps[:, 4 + 2 * t:6 + 2 * t, :]), ALU.add)\
                   .then_inc(x2_ready, 1)
            mean_square(5, D)
            r = refine(5)
            for t in range(T):
                dve.scalar_tensor_tensor(xs[:, t, :], x2[:, t, :], r[:, t:t + 1], g_fin[:], ALU.mult, ALU.mult)\
                   .then_inc(y_ready, 1)

        @block.tensor
        def _(pe):
            def three(dst, x_hi, x_lo, hi, lo, first, last, weights_stand=False):
                for i, (x_part, w_part) in enumerate(((x_hi, hi), (x_hi, lo), (x_lo, hi))):
                    a, b = (w_part, x_part) if weights_stand else (x_part, w_part)
                    ins = pe.matmul(dst, a, b, start=first and i == 0, stop=last and i == 2, skip_group_check=True)
                return ins

            def use(n):
                pe.wait_ge(lo_ready, n + 1)
                return half_view(w_hi, SPLIT, n), half_view(w_lo, SPLIT, n)

            def by_token(n, k0, banks, a_hi, a_lo, first, last):
                hi, lo = use(n)
                _, blocks, cols = halves[n]
                for k in range(blocks):
                    for t in range(T):
                        v = slice(P * t, P * t + P)
                        ins = three(ps[:, banks + t, 0:cols], a_hi[:, k0 + k, v], a_lo[:, k0 + k, v],
                                    hi[:, k, :], lo[:, k, :], first and k == 0, last and k == blocks - 1)
                ins.then_inc(half_used, 1)

            def by_channel(n, k0, banks, first, last):
                hi, lo = use(n)
                for k in range(4):
                    for j in range(4):
                        ins = three(ps[:, banks + j // 2, SEQ * (j % 2):SEQ * (j % 2) + SEQ],
                                    hT_hi[:, k0 + k, :], hT_lo[:, k0 + k, :], hi[:, k, P * j:P * j + P],
                                    lo[:, k, P * j:P * j + P], first and k == 0 and j % 2 == 0, last and k == 3,
                                    weights_stand=True)
                ins.then_inc(half_used, 1)

            def wide(n, k0, a_k0, banks, first, last):
                hi, lo = use(n)
                _, blocks, cols = halves[n]
                for k in range(blocks):
                    for t in range(T):
                        v = slice(P * t, P * t + P)
                        for c in range(0, cols, BANK):
                            w = min(BANK, cols - c)
                            ins = three(ps[:, banks + 2 * t + c // BANK, 0:w], cT_hi[:, a_k0 + k0 + k, v],
                                        cT_lo[:, a_k0 + k0 + k, v], hi[:, k, c:c + w], lo[:, k, c:c + w],
                                        first and k == 0, last and k == blocks - 1)
                ins.then_inc(half_used, 1)
            def place(u):
                t, pair = divmod(u, HEADS // 2)
                return t, 2 * pair, P * (t + 1)

            def attention_s(u):
                t, h0, keys = place(u)
                pe.wait_ge(qT_ready, t + 1)
                pe.wait_ge(kT_ready, T if u == 0 else t + 1)
                if u == 0:
                    pe.wait_ge(qT_ready, T)
                else:
                    pe.wait_ge(rowmax_ready, u)
                for h in range(2):
                    ins = pe.matmul(ps[:, 4, keys * h:keys * h + keys], qT[:, h0 + h, P * t:P * t + P],
                                    kT[:, h0 + h, 0:keys], start=True, stop=True)
                ins.then_inc(scored, 1)

            def attention_t(u):
                t, _, _ = place(u)
                pe.wait_ge(exp_ready, 2 * (u + 1))
                if u:
                    pe.wait_ge(pT_ready, u)
                for h in range(2):
                    for b in range(t + 1):
                        i = h * (t + 1) + b
                        ins = pe.transpose(ps[:, 6, P * i:P * i + P], pr[:, u % 2, h, P * b:P * b + P], ident[:])
                ins.then_inc(p_turned, 1)

            def attention_pv(u):
                t, h0, _ = place(u)
                pe.wait_ge(pT_ready, u + 1)
                if u == UNITS // T:
                    pe.wait_ge(o_ready, 1)
                for h in range(2):
                    for b in range(t + 1):
                        ins = pe.matmul(ps[:, 7, VH * (h0 + h):VH * (h0 + h) + VH], pT[:, u % 2, h * (t + 1) + b, :],
                                        v_sb[:, b, h0 + h, :], start=b == 0, stop=b == t)
                ins.then_inc(pv_done, 1)

            def turn_branch(src, i, t):
                if i:
                    pe.wait_ge(bTlo_ready, 1 + i)
                for b in range(4):
                    ins = pe.transpose(ps[:, 5, P * b:P * b + P], src[:, t, P * b:P * b + P], ident[:])
                ins.then_inc(branch_turned, 1)

            def turn_merged(b):
                t, k0 = b % 2, 4 * (b // 2)
                for k in range(4):
                    ins = pe.transpose(ps[:, 4 + b, P * k:P * k + P], merged[:, t, P * (k0 + k):P * (k0 + k) + P],
                                       ident[:])
                ins.then_inc(m_turned, 1)

            pe.wait_ge(consts_ready, 1)
            for b in range(2 * T):
                t, k0 = b // 2, 4 * (b % 2)
                pe.wait_ge(xn_ready, t + 1)
                for k in range(4):
                    ins = pe.transpose(ps[:, 4 + b, P * k:P * k + P], xn[:, t, k0 + k:D:KD], ident[:])
                ins.then_inc(h_turned, 1)

            pe.wait_ge(hTlo_ready, 2 * T)
            for n in (H_CQ, H_CQ + 1):
                by_token(n, 4 * (n - H_CQ), 0, hT_hi, hT_lo, n == H_CQ, n != H_CQ)
            for n in (H_CKV, H_CKV + 1):
                by_token(n, 4 * (n - H_CKV), 2, hT_hi, hT_lo, n == H_CKV, n != H_CKV)
            pe.wait_ge(small_in, 16 * 12)
            rows = 4 * TAPS + SGG
            pe.transpose(ps[:, 4, 0:rows], cw_raw[:], ident[0:rows, 0:rows])
            for g in range(SGG):
                ins = pe.transpose(ps[:, 5, P * g:P * g + P], ws_raw[:, g, :], ident[:])
            ins.then_inc(small_turned, 1)
            pe.wait_ge(cn_ready, T)
            for n in (H_CB, H_CB + 1):
                by_channel(n, 4 * (n - H_CB), 0, n == H_CB, n != H_CB)
            pe.wait_ge(cn_ready, 2 * T)
            pe.wait_ge(taps_ready, 1)
            pe.wait_ge(wsT_ready, 1)
            for b in range(KC):
                c0, step, end = (b, KQ, QR) if b < KQ else (QR + b - KQ, KKV, QR + KVR)
                for t in range(T):
                    c = SEQ * (b % 2) + P * t
                    ins = pe.transpose(ps[:, 4 + b // 2, c:c + P], cn[:, t, c0:end:step], ident[:])
            ins.then_inc(c_turned, 1)
            for n in (H_CC, H_CC + 1):
                by_channel(n, 4 * (n - H_CC), 2, n == H_CC, n != H_CC)
            pe.wait_ge(cTlo_ready, 1)
            pe.wait_ge(cb_ready, 1)
            pe.wait_ge(cc_ready, 1)
            wide(H_QUP, 0, 0, 0, True, False)
            wide(H_QUP + 1, 2, 0, 0, False, True)
            wide(H_KVUP, 0, KQ, 4, True, True)
            pe.wait_ge(q_ready, 1)
            for n in (H_CH, H_CH + 1):
                by_channel(n, 4 * (n - H_CH), 0, n == H_CH, n != H_CH)

            def turn_qk(t):
                pe.wait_ge(rope_ready, T)
                if t == 0:
                    pe.wait_ge(kv_ready, 2 * T)
                else:
                    pe.wait_ge(qT_ready, t)
                    pe.wait_ge(kT_ready, t)
                for i, src in enumerate((q9, kk)):
                    for h in range(HEADS):
                        ins = pe.transpose(ps[0:QK, 4 + 2 * i + h // 4, P * (h % 4):P * (h % 4) + P],
                                           src[:, t, h, :], ident[:])
                ins.then_inc(qk_turned, 1)

            turn_qk(0)
            pe.wait_ge(q_ready, T)
            by_token(H_SGV, 0, 2, hT_hi, hT_lo, True, False)
            turn_qk(1)
            by_token(H_SGV + 1, 4, 2, hT_hi, hT_lo, False, True)
            pe.wait_ge(z_ready, 1)

            for n in range(H_SGU, N_MIX):
                if n < H_GATE:
                    by_token(n, 4 * (n - H_SGU), 0, hT_hi, hT_lo, n == H_SGU, n != H_SGU)
                elif n < H_WO:
                    c, j = divmod(n - H_GATE, 3)
                    if j == 0:
                        if c == 0:
                            pe.wait_ge(gv_ready, T)
                        else:
                            pe.wait_ge(gate_ready, T * c)
                    if j < 2:
                        by_token(n, 4 * j, 2, hT_hi, hT_lo, j == 0, j == 1)
                    else:
                        b = c // 2
                        if c == 0:
                            pe.wait_ge(gu_ready, T)
                        else:
                            pe.wait_ge(merged_ready, T * c)
                        pe.wait_ge(bTlo_ready, 1 + T * b)
                        by_token(n, 0, 0, bT_hi, bT_lo, True, True)
                else:
                    j, c = divmod(n - H_WO, 2)
                    if n == H_WO:
                        pe.wait_ge(gate_ready, 6 * T)
                        pe.wait_ge(mlo_ready, 2)
                    if n == H_WO + 1:
                        pe.wait_ge(merged_ready, 6 * T)
                    if n == H_WO + 2:
                        pe.wait_ge(mlo_ready, 4)
                    by_token(n, 4 * j, 2 - 2 * c, hT_hi, hT_lo, j == 0, j == 1)
                if 0 <= n - H_ATT < UNITS:
                    attention_s(n - H_ATT)
                if 0 <= n - H_ATT - 1 < UNITS:
                    attention_t(n - H_ATT - 1)
                if 0 <= n - H_ATT - 2 < UNITS:
                    attention_pv(n - H_ATT - 2)
                for t in range(T):
                    if n == H_GATE + t:
                        pe.wait_ge(gvn_ready, t + 1)
                        pe.wait_ge(wsT_masked, 1)
                        if t:
                            pe.wait_ge(sgy_ready, t)
                        for g in range(SGG):
                            v = slice(P * g, P * g + P)
                            ins = pe.matmul(ps[:, 5, v], wsT[:, g, :], gv[:, t, v], start=True, stop=True)
                        ins.then_inc(mixed_done, 1)
                    if n == H_GATE + 5 + t:
                        pe.wait_ge(sgy_ready, T)
                        turn_branch(gu_s, t, t)
                    if n == H_GATE + 11 + t:
                        pe.wait_ge(o_ready, t + 1)
                        turn_branch(o_sb, T + t, t)
                if n == H_WO - 2:
                    pe.wait_ge(merged_ready, 5 * T)
                    turn_merged(0)
                    turn_merged(1)
                if n == H_WO:
                    pe.wait_ge(merged_ready, 6 * T)
                    turn_merged(2)
                    turn_merged(3)

            for b in range(2 * T):
                t, k0 = b // 2, 4 * (b % 2)
                pe.wait_ge(xn2_ready, t + 1)
                for k in range(4):
                    ins = pe.transpose(ps[:, 4 + b, P * k:P * k + P], xn2[:, t, k0 + k:D:KD], ident[:])
                ins.then_inc(x_turned, 1)
            pe.wait_ge(router_w_ready, 1)
            pe.wait_ge(x1_ready, 2 * T)
            for t in range(T):
                pe.wait_ge(h2T_ready, 2 * (t + 1))
                for k in range(KD):
                    ins = pe.matmul(ps[:, 0, NR * t:NR * t + NR], h2T[:, k, P * t:P * t + P], w_rt[:, k, :],
                                    start=k == 0, stop=k == KD - 1)
            ins.then_inc(logits_done, 1)
            pe.wait_ge(goh_ready, 1)
            goh = gt[:, 3, :, :]
            pe.matmul(ps[:, 1, 0:NG], before[:], goh[:, 0, :], start=True, stop=True)
            pe.matmul(ps[:, 1, NG:2 * NG], before[:], goh[:, 1, :], start=True, stop=False)
            pe.matmul(ps[:, 1, NG:2 * NG], ones[:], goh[:, 0, :], start=False, stop=True)
            pe.matmul(ps[:, 1, 2 * NG:3 * NG], ones[:], goh[:, 0, :], start=True, stop=False)
            pe.matmul(ps[:, 1, 2 * NG:3 * NG], ones[:], goh[:, 1, :], start=False, stop=True).then_inc(ranked, 1)
            pe.wait_ge(sel_ready, T * (NG + 1))
            for g in range(NG + 1):
                for t in range(T):
                    c = SEQ * (g % 2) + P * t
                    ins = pe.matmul(ps[:, 2 + g // 2, c:c + P], sel[:, t, P * g:P * g + P], ident_r[:],
                                    start=True, stop=True)
            ins.then_inc(selT_done, 1)

            def gather(g, h):
                for k in range(4):
                    cols = slice(4 * h + k, D, KD)
                    for i in range(2 * T):
                        part, t = (xn_hi, xn_lo)[i // T], i % T
                        ins = pe.matmul(ps[:, h, P * k:P * k + P], part[:, t, cols],
                                        sel[:, t, bass.ds(g * P, P)], start=i == 0, stop=i == 2 * T - 1)
                ins.then_inc(tokens_gathered, 1)

            pe.wait_ge(xnlo_ready, T)
            gather(0, 0)
            pe.wait_ge(ctl_ready, 1)
            gather(0, 1)
            pe.wait_ge(comb_lo, 1)
            for g in range(NG + 1):
                for i in range(2 * T):
                    part, t = (c_hi, c_lo)[i // T], i % T
                    ins = pe.matmul(ps[:, 5, EPG * g:EPG * g + EPG], sel[:, t, P * g:P * g + P], part[:, t, :],
                                    start=i == 0, stop=i == 2 * T - 1)
            ins.then_inc(comb_done, 1)

            def scatter(start, g):
                pe.wait_ge(selTg_ready, g + 1)
                for t in range(T):
                    for c in range(2):
                        for i, part in enumerate((y_hi, y_lo)):
                            ins = pe.matmul(ps[:, 4 + 2 * t + c, :], selT_g[:, P * t:P * t + P],
                                            part[:, BANK * c:BANK * c + BANK], start=start and i == 0, stop=i == 1,
                                            skip_group_check=True)
                return ins

            pe.wait_ge(ylo_ready, 1)
            pe.wait_ge(selT_ready, 1)
            pe.wait_ge(comb_ready, 1)
            scatter(True, 0)

            def turn_hidden(e, g):
                pe.wait_ge(hid_ready, EPG * g + e + 1)
                for k in range(2):
                    ins = pe.transpose(ps[:, e % 2, P * k:P * k + P], hid[:, e % 2, k:DE:2], ident[:])
                ins.then_inc(hid_turned, 1)

            def expert_half(j, g):
                what, e = order[j]
                n = N_MIX + j
                pe.wait_ge(lo_ready, PER_GROUP * g + n + 1)
                cols = BANK if what != "down" else D
                hi, lo = (w[:, n % SPLIT, :].rearrange("p (k n) -> p k n", n=cols) for w in (w_hi, w_lo))
                if what != "down":
                    k0 = 4 * int(what[2])
                    if e == 0:
                        pe.wait_ge(xglo_ready, 2 * g + 1 + int(what[2]))
                    for k in range(4):
                        ins = three(ps[:, e % 2, :], xg_hi[:, k0 + k, :], xg_lo[:, k0 + k, :], hi[:, k, :], lo[:, k, :],
                                    k0 + k == 0, k0 + k == KD - 1)
                else:
                    pe.wait_ge(hidTlo_ready, EPG * g + e + 1)
                    for k in range(2):
                        for c in range(2):
                            v = slice(BANK * c, BANK * c + BANK)
                            ins = three(ps[:, 2 + c, :], hidT_hi[:, e % 2, k, :], hidT_lo[:, e % 2, k, :],
                                        hi[:, k, v], lo[:, k, v], e == 0 and k == 0, e == EPG - 1 and k == 1)
                ins.then_inc(half_used, 1)

            def group(g, more):
                for j, (what, e) in enumerate(order):
                    if what == "up1" and e:
                        turn_hidden(e - 1, g)
                    if what == "down" and e == EPG - 1:
                        if more:
                            gather(g + 1, 0)
                        turn_hidden(e, g)
                    expert_half(j, g)
                    if what == "up1" and e == 0:
                        pe.wait_ge(ylo_ready, g + 1)
                        scatter(False, g).then_inc(scattered, 1)
                if more:
                    gather(g + 1, 1)

            with pe.Fori(0, NG - 1) as g:
                group(g, True)
            group(NG - 1, False)
            pe.wait_ge(ctl_ready, 1)
            over = pe.value_load(ctl[0:1, 0:1], min_val=0, max_val=1)
            with pe.If(over > 0):
                pe.wait_ge(hidTlo_ready, EPG * NG)
                gather(NG, 0)
                gather(NG, 1)
                group(NG, False)
            pe.wait_ge(ylo_ready, over + NG + 1)
            scatter(False, over + NG).then_inc(scattered, 1)


_INS = ["x", "positions", "norm_mix", "w_in", "q_norm", "w_q_up", "kv_norm", "w_kv_up", "sg_norm", "w_s", "b_s",
        "conv_w", "w_a_out", "w_b_out", "w_c_out", "w_o", "norm_ffn", "w_group_router", "b_group_router",
        "w_expert_router", "b_expert_router", "w_gate_up", "w_down", "final_norm"]


def kernel(**inputs):
    import concourse.bacc as bacc
    from concourse.bass_utils import run_bass_kernel_spmd

    nc = bacc.Bacc("TRN2", target_bir_lowering=False, num_devices=1)
    arrays, args = {}, []
    for name in _INS:
        a = np.ascontiguousarray(inputs[name])
        arrays[f"in_{name}"] = a
        args.append(nc.dram_tensor(f"in_{name}", a.shape, mybir.dt.from_np(a.dtype), kind="ExternalInput").ap())
    args.append(nc.dram_tensor("out_0", (1, SEQ, D), F32, kind="ExternalOutput").ap())
    trunk(nc, *args)
    r = run_bass_kernel_spmd(nc, [arrays], core_ids=[0])
    return r.results[0]["out_0"]
```

```python
from contextlib import ExitStack

import numpy as np
import concourse.bass as bass
from concourse import mybir

F32 = mybir.dt.float32
F32R = mybir.dt.float32r
I32 = mybir.dt.int32
ALU = mybir.AluOpType
ACT = mybir.ActivationFunctionType
AX_X = mybir.AxisListType.X

P = 128
D = 1024
SEQ = 256
T = SEQ // P
KD = D // P
EPS = 1e-6
HEADS, NOPE, ROPE, VH = 8, 64, 32, 64
QK = NOPE + ROPE
R2 = ROPE // 2
QR, KVR = 384, 256
KQ, KKV = QR // P, KVR // P
KC = KQ + KKV
SG, SGG = 512, 4
CW, TAPS = 512, 3
NG, EPG = 4, 8
NE = NG * EPG
DE = 256
NR = NG + NE
SCALE = float(QK) ** -0.5
NEG = -1.0e30
BIG = 64.0
NOWHERE = 1024.0
LOWEST = -3.0e38
MAGIC = 12582912.0
IN_SIZES = (QR, KVR, ROPE, SG, SG, CW, CW, CW, D, D, D)
C_Q, C_KV, C_KR, C_SGU, C_SGV, C_CB, C_CC, C_CH, C_GA, C_GB, C_GC = (
    sum(IN_SIZES[:i]) for i in range(len(IN_SIZES)))

HALF = 2048
RAW = 6
SPLIT = 3
AHEAD = SPLIT - 1
BANK = 512

H_CQ, H_CKV, H_CB, H_CC, H_QUP, H_KVUP, H_CH, H_SGV, H_SGU = 0, 2, 4, 6, 8, 10, 11, 13, 15
H_GATE = 17
H_WO = H_GATE + 18
N_MIX = H_WO + 4
H_ATT = H_SGU
UNITS = T * HEADS // 2
PER_GROUP = 3 * EPG
SMALL = 13
ROWS = 4 * TAPS + SGG + KD
COMB_COLS = (NG + 1) * 2 * (EPG + 1)
SLOTS = (NG + 1) * P


def two_pi_parts():
    rest, parts = 2 * np.pi, []
    for _ in range(4):
        m, e = np.frexp(rest)
        part = float(np.ldexp(np.round(m * 256) / 256, int(e)))
        parts.append(part)
        rest -= part
    return parts


def trunk(nc, x, positions, norm_mix, w_in, q_norm, w_q_up, kv_norm, w_kv_up, sg_norm, w_s, b_s,
          conv_w, w_a_out, w_b_out, w_c_out, w_o, norm_ffn, w_group_router, b_group_router,
          w_expert_router, b_expert_router, w_gate_up, w_down, final_norm, out):
    x_d = x[0].rearrange("(t p) d -> p t d", p=P)
    out_d = out[0].rearrange("(t p) d -> p t d", p=P)
    win_d = w_in[0].rearrange("(p k) n -> p k n", k=KD)
    qup_d = w_q_up[0].rearrange("(p k) n -> p k n", k=KQ)
    kvup_d = w_kv_up[0].rearrange("(p k) n -> p k n", k=KKV)
    wout_d = [w[0].rearrange("(k p) n -> p k n", p=P) for w in (w_c_out, w_b_out, w_a_out)]
    wo_d = w_o[0].rearrange("(k p) n -> p k n", p=P)
    gu_d = w_gate_up[0].rearrange("e (p k) n -> e p (k n)", k=KD)
    dn_d = w_down[0].rearrange("e (p k) n -> e p (k n)", k=DE // P)

    with ExitStack() as ctx:
        def sb(name, shape, dt=F32, stack=ctx):
            return stack.enter_context(nc.sbuf_tensor(name, shape, dt))

        def sem(name):
            return ctx.enter_context(nc.semaphore(name))

        ps = ctx.enter_context(nc.psum_tensor("ps", [P, 8, BANK], F32))

        raw = sb("raw", [P, RAW, HALF])
        w_hi = sb("w_hi", [P, SPLIT, HALF], F32R)
        w_lo = sb("w_lo", [P, SPLIT, HALF], F32R)
        xs = sb("xs", [P, T, D])
        ident = sb("ident", [P, P])
        ident_r = sb("ident_r", [P, P], F32R)
        mask = sb("mask", [P, P])
        ones = sb("ones", [P, P], F32R)
        before = sb("before", [P, P], F32R)
        causal = sb("causal", [P, SEQ])
        g_mix = sb("g_mix", [P, KD])
        g_ffn = sb("g_ffn", [P, KD])
        g_c = sb("g_c", [P, KC])
        g_fin = sb("g_fin", [P, D])
        w_rt = sb("w_rt", [P, KD, NR])
        rt_raw = sb("rt_raw", [P, KD, NG])
        b_rt = sb("b_rt", [P, NR])
        stat = sb("stat", [P, 6, 4, T])
        neg_half = sb("neg_half", [P, T])

        mix = ExitStack()
        hT_hi = sb("hT_hi", [P, KD, SEQ], F32R, mix)
        hT_lo = sb("hT_lo", [P, KD, SEQ], F32R, mix)
        v_sb = sb("v_sb", [P, T, HEADS, VH], F32, mix)
        qT = sb("qT", [QK, HEADS, SEQ], F32, mix)
        kT = sb("kT", [QK, HEADS, SEQ], F32, mix)
        cb_sb = sb("cb_sb", [P, 4, SEQ], F32, mix)
        z_sb = sb("z_sb", [P, 4, SEQ + TAPS - 1], F32, mix)
        pr = sb("pr", [P, 2, 2, SEQ], F32, mix)
        pT = sb("pT", [P, 2, 4, P], F32, mix)
        o_sb = sb("o_sb", [P, T, HEADS * VH], F32, mix)
        rot = sb("rot", [P, 2, T, R2], F32, mix)
        g_sg = sb("g_sg", [P, SG], F32, mix)
        wsT = sb("wsT", [P, SGG, P], F32, mix)
        taps = sb("taps", [P, ROWS], F32, mix)
        rmax = sb("rmax", [P, T * HEADS], F32, mix)
        nmax = sb("nmax", [P, T * HEADS], F32, mix)
        rsum = sb("rsum", [P, T * HEADS], F32, mix)
        rinv = sb("rinv", [P, T * HEADS], F32, mix)
        early = ExitStack()
        cn = sb("cn", [P, T, QR + KVR], F32, early)
        cT_f = sb("cT_f", [P, KC, SEQ], F32, early)
        cT_hi = sb("cT_hi", [P, KC, SEQ], F32R, early)
        cT_lo = sb("cT_lo", [P, KC, SEQ], F32R, early)
        q9 = sb("q9", [P, T, HEADS + 1, QK], F32, early)
        kk = sb("kk", [P, T, HEADS, QK], F32, early)
        rt = cn[:].rearrange("p t n -> p (t n)")[:, 0:4 * T * (HEADS + 1) * R2]\
            .rearrange("p (i t h n) -> p i t h n", i=4, t=T, n=R2)
        early.close()
        late = ExitStack()
        merged = sb("merged", [P, T, D], F32, late)
        bT_f = sb("bT_f", [P, 4, SEQ], F32, late)
        bT_hi = sb("bT_hi", [P, 4, SEQ], F32R, late)
        bT_lo = sb("bT_lo", [P, 4, SEQ], F32R, late)
        gv = sb("gv", [P, T, SG], F32, late)
        gu_s = sb("gu_s", [P, T, SG], F32, late)
        late.close()
        start = ExitStack()
        xn = sb("xn", [P, T, D], F32, start)
        ws_raw = sb("ws_raw", [P, SGG, P], F32, start)
        cw_raw = sb("cw_raw", [ROWS, P], F32, start)
        h_f = sb("h_f", [P, KD, SEQ], F32, start)
        pos_i = sb("pos_i", [P, T], I32, start)
        pos_f = sb("pos_f", [P, T], F32, start)
        inv_f = sb("inv_f", [P, R2], F32, start)
        ang = sb("ang", [P, 4, T, R2], F32, start)
        start.close()
        mix.close()

        x_hi = sb("x_hi", [P, T, D], F32R)
        x_lo = sb("x_lo", [P, T, D], F32R)
        sel = sb("sel", [P, T, SLOTS], F32R)
        selT = sb("selT", [P, NG + 1, SEQ], F32R)
        selT_g = sb("selT_g", [P, SEQ], F32R)
        comb = sb("comb", [P, NG + 1, EPG + 1])
        root_g = sb("root_g", [P, 1])
        y_hi = sb("y_hi", [P, D], F32R)
        y_lo = sb("y_lo", [P, D], F32R)
        cw_parts = sb("cw_parts", [P, T, 2, EPG + 1], F32R)
        ctl = sb("ctl", [P, 2], I32)
        router = ExitStack()
        x1T = sb("x1T", [P, KD, SEQ], F32, router)
        lg = sb("lg", [P, T, NR], F32, router)
        gt = sb("gt", [P, 6, T, NG], F32, router)
        goh = sb("goh", [P, T, NG], F32R, router)
        et = sb("et", [P, 8, T, EPG], F32, router)
        eg = sb("eg", [P, T, NG, EPG], F32, router)
        sc = sb("sc", [P, 14, T, 1], F32, router)
        cw = sb("cw", [P, T, EPG + 1], F32, router)
        slot_i = sb("slot_i", [P, P], I32, router)
        slot_f = sb("slot_f", [P, P], F32, router)
        idx_g = sb("idx_g", [P, NG], F32, router)
        idx_e = sb("idx_e", [P, EPG], F32, router)
        cnt = sb("cnt", [P, 3, NG], F32, router)
        ctl_f = sb("ctl_f", [P, 3], F32, router)
        router.close()
        xg_f = sb("xg_f", [P, KD, P])
        xg_hi = sb("xg_hi", [P, KD, P], F32R)
        xg_lo = sb("xg_lo", [P, KD, P], F32R)
        silu = sb("silu", [P, 2, DE])
        hid = sb("hid", [P, 2, DE])
        hidT_hi = sb("hidT_hi", [P, 2, 2, P], F32R)
        hidT_lo = sb("hidT_lo", [P, 2, 2, P], F32R)
        x2 = sb("x2", [P, T, D])
        sq = sb("sq", [P, T, D])

        raw_landed = [sem(f"raw_landed{i}") for i in range(RAW)]
        hi_ready = sem("hi_ready")
        lo_ready = sem("lo_ready")
        half_used = sem("half_used")
        pos_in = sem("pos_in")
        x_in = sem("x_in")
        small_in = sem("small_in")
        mix_gain_in = sem("mix_gain_in")
        inv_ready = sem("inv_ready")
        ang_ready = sem("ang_ready")
        rot_ready = sem("rot_ready")
        consts_ready = sem("consts_ready")
        router_w_ready = sem("router_w_ready")
        dve_chain = sem("dve_chain")
        pool_chain = sem("pool_chain")
        ssq_ready = sem("ssq_ready")
        ms_ready = sem("ms_ready")
        root_ready = sem("root_ready")
        xn_ready = sem("xn_ready")
        h_turned = sem("h_turned")
        hf_ready = sem("hf_ready")
        hThi_ready = sem("hThi_ready")
        hTlo_ready = sem("hTlo_ready")
        small_turned = sem("small_turned")
        taps_ready = sem("taps_ready")
        wsT_ready = sem("wsT_ready")
        wsT_masked = sem("wsT_masked")
        cn_ready = sem("cn_ready")
        c_turned = sem("c_turned")
        cTf_ready = sem("cTf_ready")
        cThi_ready = sem("cThi_ready")
        cTlo_ready = sem("cTlo_ready")
        zpad_ready = sem("zpad_ready")
        cb_ready = sem("cb_ready")
        cc_ready = sem("cc_ready")
        z_ready = sem("z_ready")
        q_ready = sem("q_ready")
        kv_ready = sem("kv_ready")
        rope_ready = sem("rope_ready")
        qk_turned = sem("qk_turned")
        qT_ready = sem("qT_ready")
        kT_ready = sem("kT_ready")
        bTf_ready = sem("bTf_ready")
        bThi_ready = sem("bThi_ready")
        bTlo_ready = sem("bTlo_ready")
        branch_turned = sem("branch_turned")
        gv_ready = sem("gv_ready")
        gvn_ready = sem("gvn_ready")
        gu_ready = sem("gu_ready")
        mixed_done = sem("mixed_done")
        sgy_ready = sem("sgy_ready")
        scored = sem("scored")
        rowmax_ready = sem("rowmax_ready")
        exp_ready = sem("exp_ready")
        p_turned = sem("p_turned")
        pT_ready = sem("pT_ready")
        pv_done = sem("pv_done")
        o_ready = sem("o_ready")
        gate_ready = sem("gate_ready")
        merged_ready = sem("merged_ready")
        m_turned = sem("m_turned")
        mhi_ready = sem("mhi_ready")
        mlo_ready = sem("mlo_ready")
        x1_ready = sem("x1_ready")
        xhi_ready = sem("xhi_ready")
        xlo_ready = sem("xlo_ready")
        x_turned = sem("x_turned")
        x1T_ready = sem("x1T_ready")
        logits_done = sem("logits_done")
        gmax_ready = sem("gmax_ready")
        gexp_ready = sem("gexp_ready")
        d_ready = sem("d_ready")
        eexp_ready = sem("eexp_ready")
        goh_ready = sem("goh_ready")
        ranked = sem("ranked")
        counted = sem("counted")
        sel_ready = sem("sel_ready")
        comb_split = sem("comb_split")
        comb_hi = sem("comb_hi")
        comb_lo = sem("comb_lo")
        selT_done = sem("selT_done")
        selT_ready = sem("selT_ready")
        comb_done = sem("comb_done")
        comb_ready = sem("comb_ready")
        rootg_ready = sem("rootg_ready")
        ctl_ready = sem("ctl_ready")
        slot_ready = sem("slot_ready")
        index_ready = sem("index_ready")
        selTg_ready = sem("selTg_ready")
        tokens_gathered = sem("tokens_gathered")
        xgf_ready = sem("xgf_ready")
        xghi_ready = sem("xghi_ready")
        xglo_ready = sem("xglo_ready")
        silu_ready = sem("silu_ready")
        hid_ready = sem("hid_ready")
        hid_turned = sem("hid_turned")
        hidThi_ready = sem("hidThi_ready")
        hidTlo_ready = sem("hidTlo_ready")
        yhi_ready = sem("yhi_ready")
        ylo_ready = sem("ylo_ready")
        scattered = sem("scattered")
        x2_ready = sem("x2_ready")
        y_ready = sem("y_ready")
        stored = sem("stored")

        block = ctx.enter_context(nc.Block())

        halves = {}
        for h0, c0, n in ((H_CQ, C_Q, QR), (H_CKV, C_KV, KVR + ROPE), (H_CB, C_CB, CW), (H_CC, C_CC, CW),
                          (H_CH, C_CH, CW), (H_SGV, C_SGV, SG), (H_SGU, C_SGU, SG)):
            for j in range(2):
                halves[h0 + j] = (win_d[:, 4 * j:4 * j + 4, c0:c0 + n], 4, n)
        halves[H_QUP] = (qup_d[:, 0:2, :], 2, HEADS * QK)
        halves[H_QUP + 1] = (qup_d[:, 2:3, :], 1, HEADS * QK)
        halves[H_KVUP] = (kvup_d[:, :, :], 2, HEADS * (NOPE + VH))
        for b, gcol in enumerate((C_GC, C_GB, C_GA)):
            for c in range(2):
                n, c0 = H_GATE + 6 * b + 3 * c, gcol + BANK * c
                for j in range(2):
                    halves[n + j] = (win_d[:, 4 * j:4 * j + 4, c0:c0 + BANK], 4, BANK)
                halves[n + 2] = (wout_d[b][:, :, BANK * c:BANK * c + BANK], 4, BANK)
        for j in range(2):
            for c in range(2):
                halves[H_WO + 2 * j + c] = (wo_d[:, 4 * j:4 * j + 4, BANK * c:BANK * c + BANK], 4, BANK)

        def half_view(buf, slots, n):
            _, blocks, cols = halves[n]
            return buf[:, n % slots, 0:blocks * cols].rearrange("p (k n) -> p k n", n=cols)

        def joined(banks):
            return banks.rearrange("p a b -> p (a b)")

        order = []
        for e in range(EPG):
            order += [("up0", e), ("up1", e)]
            if e:
                order.append(("down", e - 1))
        order.append(("down", EPG - 1))

        @block.sync
        def _(sp):
            for n in range(N_MIX):
                if n >= RAW:
                    sp.wait_ge(lo_ready, n - RAW + 1)
                sp.dma_start(half_view(raw, RAW, n), halves[n][0]).then_inc(raw_landed[n % RAW], 16)

            def load_group(first_expert, g):
                for j, (what, e) in enumerate(order):
                    n = N_MIX + j
                    if what == "down":
                        src = dn_d[bass.ds(first_expert + e, 1), :, :]
                    else:
                        k = int(what[2]) * HALF
                        src = gu_d[bass.ds(first_expert + e, 1), :, k:k + HALF]
                    sp.wait_ge(lo_ready, PER_GROUP * g + n - RAW + 1)
                    sp.dma_start(raw[:, n % RAW, :], src.rearrange("a p n -> (a p) n"))\
                      .then_inc(raw_landed[n % RAW], 16)

            with sp.Fori(0, NG) as g:
                load_group(g * EPG, g)
            sp.wait_ge(ctl_ready, 1)
            over = sp.value_load(ctl[0:1, 0:1], min_val=0, max_val=1)
            full = sp.value_load(ctl[0:1, 1:2], min_val=0, max_val=NG - 1)
            with sp.If(over > 0):
                load_group(full * EPG, NG)
            for t in range(T):
                sp.wait_ge(y_ready, t + 1)
                sp.dma_start(out_d[:, t, :], xs[:, t, :]).then_inc(stored, 16)
            sp.wait_ge(stored, 16 * T)

        @block.gpsimd
        def _(pool):
            count = [0]

            def then(ins):
                count[0] += 1
                ins.then_inc(pool_chain, 1)
                pool.wait_ge(pool_chain, count[0])

            pool.dma_start(g_mix[:], norm_mix[0].rearrange("(p k) -> p k", k=KD)).then_inc(mix_gain_in, 16)
            for i in range(R2):
                last = pool.memset(inv_f[:, i:i + 1], float(np.float32(10000.0 ** (-2 * i / ROPE))))
            last.then_inc(inv_ready, 1)
            then(pool.memset(neg_half[:], -0.5))
            then(pool.memset(ident[:], 0.0))
            then(pool.affine_select(ident[:], ident[:], [[-1, P]], ALU.not_equal, 1.0, base=0, channel_multiplier=1))
            pool.tensor_copy(ident_r[:], ident[:]).then_inc(consts_ready, 1)
            small = [
                (cw_raw[0:4 * TAPS, :], conv_w[0].rearrange("j (b p) -> (j b) p", p=P)),
                (cw_raw[4 * TAPS:4 * TAPS + SGG, :], b_s[0]),
                (ws_raw[:], w_s[0].rearrange("g t s -> t g s")),
                (g_c[:, 0:KQ], q_norm[0].rearrange("(p k) -> p k", k=KQ)),
                (g_c[:, KQ:KC], kv_norm[0].rearrange("(p k) -> p k", k=KKV)),
                (g_sg[:], sg_norm[0].partition_broadcast(P)),
                (g_ffn[:], norm_ffn[0].rearrange("(p k) -> p k", k=KD)),
                (cw_raw[4 * TAPS + SGG:, :], norm_ffn[0].rearrange("(k p) -> k p", p=P)),
                (rt_raw[:], w_group_router[0].rearrange("(k p) n -> p k n", p=P)),
                (w_rt[:, :, NG:], w_expert_router[0].rearrange("(k p) n -> p k n", p=P)),
                (b_rt[:, 0:NG], b_group_router[0].partition_broadcast(P)),
                (b_rt[:, NG:], b_expert_router[0].partition_broadcast(P)),
                (g_fin[:], final_norm.partition_broadcast(P)),
            ]
            for dst, src in small:
                pool.dma_start(dst, src).then_inc(small_in, 16)

            def root(norm):
                pool.wait_ge(ms_ready, norm + 1)
                pool.tensor_tensor(stat[:, norm, 2, :], stat[:, norm, 1, :], neg_half[:], ALU.pow)\
                    .then_inc(root_ready, 1)

            root(0)
            then(pool.memset(mask[:], 1.0))
            pool.tensor_copy(ones[:], mask[:])
            then(pool.memset(causal[:], 0.0))
            pool.affine_select(causal[:, P:], causal[:, P:], [[-1, P]], ALU.is_ge, NEG, base=0, channel_multiplier=1)
            then(pool.affine_select(mask[:], mask[:], [[1, P]], ALU.is_gt, 0.0, base=0, channel_multiplier=-1))
            pool.tensor_copy(before[:], mask[:])
            pool.memset(z_sb[:, :, 0:TAPS - 1], 0.0).then_inc(zpad_ready, 1)
            root(1)
            root(2)
            pool.wait_ge(small_in, 16 * SMALL)
            pool.wait_ge(taps_ready, 1)
            gains = taps[:, 4 * TAPS + SGG:].unsqueeze(2)
            pool.tensor_tensor(w_rt[:, :, NG:], w_rt[:, :, NG:], gains.to_broadcast([P, KD, NE]), ALU.mult)
            pool.tensor_tensor(w_rt[:, :, 0:NG], rt_raw[:], gains.to_broadcast([P, KD, NG]), ALU.mult)\
                .then_inc(router_w_ready, 1)
            pool.wait_ge(wsT_ready, 1)
            pool.affine_select(wsT[:], wsT[:], [[0, SGG], [1, P]], ALU.is_ge, 0.0, base=0, channel_multiplier=-1)\
                .then_inc(wsT_masked, 1)
            root(3)
            pool.wait_ge(half_used, H_WO + 3)
            pool.iota(slot_i[:], [[1, P]], base=0, channel_multiplier=0).then_inc(slot_ready, 1)
            pool.wait_ge(slot_ready, 1)
            then(pool.tensor_copy(slot_f[:], slot_i[:]))
            then(pool.tensor_scalar(idx_g[:], slot_f[:, 0:NG], BIG, None, ALU.add))
            pool.tensor_scalar(idx_e[:], slot_f[:, 0:EPG], BIG, None, ALU.add).then_inc(index_ready, 1)
            pool.memset(y_hi[:].bitcast(F32), 0.0).then_inc(ylo_ready, 1)
            pool.memset(selT_g[:].bitcast(F32), 0.0).then_inc(selTg_ready, 1)
            root(4)

            pool.wait_ge(selT_ready, 1)
            with pool.Fori(0, NG) as g:
                pool.wait_ge(scattered, g + 1)
                pool.tensor_copy(selT_g[:], selT[:, bass.ds(g, 1), :].rearrange("p a n -> p (a n)"))\
                    .then_inc(selTg_ready, 1)
            pool.wait_ge(ctl_ready, 1)
            over = pool.value_load(ctl[0:1, 0:1], min_val=0, max_val=1)
            with pool.If(over > 0):
                pool.wait_ge(scattered, NG + 1)
                pool.tensor_copy(selT_g[:], selT[:, NG, :]).then_inc(selTg_ready, 1)
            root(5)

        @block.scalar
        def _(act):
            def split_hi(n, g=None):
                shift, slots = (0, 0) if g is None else (PER_GROUP * g, 16 * (PER_GROUP // RAW) * g)
                act.wait_ge(raw_landed[n % RAW], slots + 16 * (n // RAW + 1))
                if n >= SPLIT:
                    act.wait_ge(half_used, shift + n - SPLIT + 1)
                if n < N_MIX:
                    dst, src = half_view(w_hi, SPLIT, n), half_view(raw, RAW, n)
                else:
                    dst, src = w_hi[:, n % SPLIT, :], raw[:, n % RAW, :]
                act.activation(dst, src, ACT.Copy).then_inc(hi_ready, 1)

            def squares(norm, t, src, junk):
                act.activation(junk, src, ACT.Square, accum_out=stat[:, norm, 0, t:t + 1]).then_inc(ssq_ready, 1)

            for t in range(T):
                act.dma_start(pos_i[:, t:t + 1], positions[0, P * t:P * t + P].rearrange("(p a) -> p a", a=1))\
                   .then_inc(pos_in, 16)
            for t in range(T):
                act.dma_start(xs[:, t, :], x_d[:, t, :]).then_inc(x_in, 16)
            split_hi(0)
            act.wait_ge(x_in, 16 * T)
            for t in range(T):
                squares(0, t, xs[:, t, :], h_f[:, 4 * t:4 * t + 4, :].rearrange("p a b -> p (a b)"))
            act.wait_ge(ang_ready, 1)
            act.activation(rot[:], ang[:, 0:2, :, :], ACT.Sin).then_inc(rot_ready, 1)
            split_hi(1)
            for b in range(2 * T):
                t, k = b // 2, 4 * (b % 2)
                v = slice(P * t, P * t + P)
                act.wait_ge(hf_ready, b + 1)
                act.activation(hT_hi[:, k:k + 4, v], h_f[:, k:k + 4, v], ACT.Copy).then_inc(hThi_ready, 1)

            def attention_exp(u):
                t, pair = divmod(u, HEADS // 2)
                act.wait_ge(rowmax_ready, u + 1)
                for h in range(2):
                    i = HEADS * t + 2 * pair + h
                    row = pr[:, u % 2, h, 0:P * (t + 1)]
                    act.activation(row, row, ACT.Exp, bias=nmax[:, i:i + 1], scale=SCALE,
                                   accum_out=rsum[:, i:i + 1]).then_inc(exp_ready, 1)

            def attention_pT(u):
                n = 2 * (u // (HEADS // 2) + 1)
                act.wait_ge(p_turned, u + 1)
                act.activation(pT[:, u % 2, 0:n, :], ps[:, 6, 0:n * P].rearrange("p (a b) -> p a b", b=P), ACT.Copy)\
                    .then_inc(pT_ready, 1)

            def branch_turned_hi(i, t):
                act.wait_ge(branch_turned, i + 1)
                act.activation(bT_hi[:, :, P * t:P * t + P], ps[:, 5, :].rearrange("p (a b) -> p a b", b=P), ACT.Copy)\
                    .then_inc(bThi_ready, 1)

            for n in range(N_MIX):
                if n + AHEAD < N_MIX:
                    split_hi(n + AHEAD)
                else:
                    split_hi(n + AHEAD, 0)
                if n == H_CKV:
                    act.wait_ge(half_used, H_CKV)
                    for t in range(T):
                        squares(1, t, ps[:, t, 0:QR], xn[:, t, 0:QR])
                if n == H_CB:
                    act.wait_ge(half_used, H_CB)
                    for t in range(T):
                        squares(2, t, ps[:, 2 + t, 0:KVR], xn[:, t, QR:QR + KVR])
                if n == H_CC:
                    act.wait_ge(half_used, H_CC)
                    act.activation(cb_sb[:].rearrange("p a b -> p (a b)"), joined(ps[:, 0:2, :]), ACT.Copy)\
                        .then_inc(cb_ready, 1)
                    act.wait_ge(cTf_ready, 1)
                    act.activation(cT_hi[:], cT_f[:], ACT.Copy).then_inc(cThi_ready, 1)
                if n == H_QUP:
                    act.wait_ge(half_used, H_QUP)
                    act.activation(z_sb[:, :, TAPS - 1:], joined(ps[:, 2:4, :]).rearrange("p (a b) -> p a b", b=SEQ),
                                   ACT.Copy).then_inc(cc_ready, 1)
                if n == H_KVUP:
                    act.wait_ge(half_used, H_KVUP)
                    for t in range(T):
                        act.activation(q9[:, t, 0:HEADS, :].rearrange("p h d -> p (h d)"),
                                       joined(ps[:, 2 * t:2 * t + 2, :])[:, 0:HEADS * QK],
                                       ACT.Copy).then_inc(q_ready, 1)
                if n == H_CH:
                    act.wait_ge(half_used, H_CH)
                    for t in range(T):
                        kv = joined(ps[:, 4 + 2 * t:6 + 2 * t, :]).rearrange("p (h d) -> p h d", d=NOPE + VH)
                        act.activation(kk[:, t, :, 0:NOPE], kv[:, :, 0:NOPE], ACT.Copy).then_inc(kv_ready, 1)
                        act.activation(v_sb[:, t, :, :], kv[:, :, NOPE:], ACT.Copy).then_inc(kv_ready, 1)
                if n in (H_SGV, H_SGV + 1):
                    t = n - H_SGV
                    act.wait_ge(qk_turned, t + 1)
                    act.activation(qT[:, :, P * t:P * t + P],
                                   joined(ps[0:QK, 4:6, :]).rearrange("p (a b) -> p a b", b=P), ACT.Copy)\
                        .then_inc(qT_ready, 1)
                if n == H_SGU:
                    act.wait_ge(half_used, H_SGU)
                    for t in range(T):
                        act.activation(gv[:, t, :], ps[:, 2 + t, :], ACT.Gelu_apprx_tanh).then_inc(gv_ready, 1)
                    act.wait_ge(gv_ready, T)
                    for t in range(T):
                        squares(3, t, gv[:, t, :], merged[:, t, 0:SG])
                    act.wait_ge(bTf_ready, 1)
                    act.activation(bT_hi[:], bT_f[:], ACT.Copy).then_inc(bThi_ready, 1)
                if n == H_GATE:
                    act.wait_ge(half_used, H_GATE)
                    for t in range(T):
                        act.activation(gu_s[:, t, :], ps[:, t, :], ACT.Gelu_apprx_tanh).then_inc(gu_ready, 1)
                if 0 <= n - H_ATT - 2 < UNITS:
                    attention_pT(n - H_ATT - 2)
                if 0 <= n - H_ATT - 1 < UNITS:
                    attention_exp(n - H_ATT - 1)
                for b in (1, 2):
                    for t in range(T):
                        if n == H_GATE + 6 * b + t:
                            branch_turned_hi(T * (b - 1) + t, t)
                for c in range(6):
                    if n == H_GATE + 3 * c + 2:
                        act.wait_ge(half_used, H_GATE + 3 * c + 2)
                        act.wait_ge(gvn_ready if not c else merged_ready, T * max(c, 1))
                        if not c:
                            act.wait_ge(mixed_done, T)
                        for t in range(T):
                            act.activation(gv[:, t, :], ps[:, 2 + t, :], ACT.Tanh, scale=0.5).then_inc(gate_ready, 1)
                if n in (H_WO - 1, H_WO + 1):
                    for b in ((0, 1) if n < H_WO else (2, 3)):
                        t, k = b % 2, 4 * (b // 2)
                        act.wait_ge(m_turned, b + 1)
                        act.activation(hT_hi[:, k:k + 4, P * t:P * t + P],
                                       ps[:, 4 + b, :].rearrange("p (a b) -> p a b", b=P), ACT.Copy, scale=0.5)\
                            .then_inc(mhi_ready, 1)

            for t in range(T):
                act.wait_ge(x1_ready, T + t + 1)
                squares(4, t, xs[:, t, :], sq[:, t, :])
            for t in range(T):
                act.activation(x_hi[:, t, :], xs[:, t, :], ACT.Copy).then_inc(xhi_ready, 1)
            act.wait_ge(gmax_ready, 1)
            act.activation(gt[:, 1, :, :], gt[:, 0, :, :], ACT.Exp).then_inc(gexp_ready, 1)
            act.wait_ge(d_ready, 1)
            act.activation(sc[:, 8, :, :], sc[:, 7, :, :], ACT.Exp).then_inc(eexp_ready, 1)
            act.wait_ge(comb_split, 1)
            act.activation(cw_parts[:, :, 0, :], cw[:], ACT.Copy).then_inc(comb_hi, 1)

            def gathered_hi(g, h):
                act.wait_ge(xgf_ready, 2 * g + h + 1)
                act.activation(xg_hi[:, 4 * h:4 * h + 4, :], xg_f[:, 4 * h:4 * h + 4, :], ACT.Copy)\
                    .then_inc(xghi_ready, 1)

            def turned_hi(e, g):
                act.wait_ge(hid_turned, EPG * g + e + 1)
                act.activation(hidT_hi[:, e % 2, :, :], ps[:, e % 2, 0:DE].rearrange("p (a b) -> p a b", b=P),
                               ACT.Copy).then_inc(hidThi_ready, 1)

            def gate(e, g):
                act.wait_ge(half_used, PER_GROUP * g + N_MIX + order.index(("up1", e)) + 1)
                if e == 0:
                    act.wait_ge(rootg_ready, g + 1)
                act.activation(silu[:, e % 2, :], ps[:, e % 2, 0:DE], ACT.Silu,
                               scale=root_g[:]).then_inc(silu_ready, 1)

            def group(g, more, opening=False, again=False):
                if again:
                    for j in range(AHEAD):
                        split_hi(N_MIX + j, g)
                for j, (what, e) in enumerate(order):
                    if opening and j == 1:
                        act.wait_ge(selT_done, 1)
                        act.activation(selT[:].rearrange("p a b -> p (a b)"), joined(ps[:, 1:4, :])[:, 0:(NG + 1) * SEQ],
                                       ACT.Copy).then_inc(selT_ready, 1)
                    if what == "up0" and e == 1:
                        gate(0, g)
                    if what == "up1" and e:
                        turned_hi(e - 1, g)
                    if what == "down" and e < EPG - 1:
                        gate(e + 1, g)
                    if what == "down" and e == EPG - 1:
                        turned_hi(e, g)
                        if more:
                            gathered_hi(g + 1, 0)
                    if more or j + AHEAD < PER_GROUP:
                        split_hi(N_MIX + j + AHEAD, g)
                if more:
                    gathered_hi(g + 1, 1)
                act.wait_ge(half_used, PER_GROUP * g + N_MIX + PER_GROUP)
                act.wait_ge(scattered, g + 1)
                act.activation(y_hi[:], joined(ps[:, 2:4, :]), ACT.Copy).then_inc(yhi_ready, 1)

            gathered_hi(0, 0)
            gathered_hi(0, 1)
            group(0, True, opening=True)
            with act.Fori(1, NG - 1) as g:
                group(g, True)
            group(NG - 1, False)
            act.wait_ge(ctl_ready, 1)
            over = act.value_load(ctl[0:1, 0:1], min_val=0, max_val=1)
            with act.If(over > 0):
                gathered_hi(NG, 0)
                gathered_hi(NG, 1)
                group(NG, False, again=True)
            for t in range(T):
                act.wait_ge(x2_ready, t + 1)
                squares(5, t, x2[:, t, :], sq[:, t, :])

        @block.vector
        def _(dve):
            counts = {}

            def then(ins, signal=dve_chain):
                counts[id(signal)] = counts.get(id(signal), 0) + 1
                ins.then_inc(signal, 1)
                dve.wait_ge(signal, counts[id(signal)])

            def split_lo(n, g=None):
                shift = 0 if g is None else PER_GROUP * g
                dve.wait_ge(hi_ready, shift + n + 1)
                if n < N_MIX:
                    dst, src, hi = half_view(w_lo, SPLIT, n), half_view(raw, RAW, n), half_view(w_hi, SPLIT, n)
                else:
                    dst, src, hi = w_lo[:, n % SPLIT, :], raw[:, n % RAW, :], w_hi[:, n % SPLIT, :]
                dve.tensor_tensor(dst, src, hi, ALU.subtract).then_inc(lo_ready, 1)

            def mean_square(norm, width):
                dve.wait_ge(ssq_ready, T * (norm + 1))
                dve.tensor_scalar(stat[:, norm, 1, :], stat[:, norm, 0, :], 1.0 / width, EPS, ALU.mult, ALU.add)\
                   .then_inc(ms_ready, 1)

            def refine(norm):
                ms, r, a = (stat[:, norm, i, :] for i in (1, 2, 3))
                dve.wait_ge(root_ready, norm + 1)
                dve.wait_ge(ms_ready, norm + 1)
                then(dve.tensor_tensor(a, r, r, ALU.mult))
                then(dve.scalar_tensor_tensor(a, a, -0.5, ms, ALU.mult, ALU.mult))
                then(dve.scalar_tensor_tensor(r, a, 1.5, r, ALU.add, ALU.mult))
                return r

            dve.wait_ge(pos_in, 16 * T)
            then(dve.tensor_copy(pos_f[:], pos_i[:]))
            dve.wait_ge(inv_ready, 1)
            a0, a1, turns, far = (ang[:, i, :, :] for i in range(4))
            for t in range(T):
                last = dve.tensor_scalar(ang[:, 0, t, :], inv_f[:], pos_f[:, t:t + 1], None, ALU.mult)
            then(last)
            then(dve.tensor_scalar(turns, a0, 1.0 / (2 * np.pi), MAGIC, ALU.mult, ALU.add))
            then(dve.tensor_scalar(turns, turns, -MAGIC, None, ALU.add))
            for part in two_pi_parts():
                then(dve.scalar_tensor_tensor(a0, turns, -part, a0, ALU.mult, ALU.add))
            then(dve.tensor_scalar(a1, a0, np.pi / 2, None, ALU.add))
            then(dve.tensor_scalar(far, a1, np.pi, 2 * np.pi, ALU.is_gt, ALU.mult))
            then(dve.tensor_tensor(a1, a1, far, ALU.subtract))
            limit = float(np.nextafter(np.float32(np.pi), np.float32(0)))
            dve.tensor_scalar(ang[:, 0:2, :, :], ang[:, 0:2, :, :], limit, -limit, ALU.min, ALU.max)\
               .then_inc(ang_ready, 1)

            mean_square(0, D)
            split_lo(0)
            r = refine(0)
            for t in range(T):
                dve.tensor_scalar(xn[:, t, :], xs[:, t, :], r[:, t:t + 1], None, ALU.mult).then_inc(xn_ready, 1)
            dve.wait_ge(mix_gain_in, 16)
            for b in range(2 * T):
                t, k = b // 2, 4 * (b % 2)
                dve.wait_ge(h_turned, b + 1)
                dve.tensor_tensor(h_f[:, k:k + 4, P * t:P * t + P], ps[:, 4 + b, :].rearrange("p (a b) -> p a b", b=P),
                                  g_mix[:, k:k + 4].unsqueeze(2).to_broadcast([P, 4, P]), ALU.mult)\
                   .then_inc(hf_ready, 1)
            for b in range(2 * T):
                t, k = b // 2, 4 * (b % 2)
                v = slice(P * t, P * t + P)
                dve.wait_ge(hThi_ready, b + 1)
                dve.tensor_tensor(hT_lo[:, k:k + 4, v], h_f[:, k:k + 4, v], hT_hi[:, k:k + 4, v], ALU.subtract)\
                   .then_inc(hTlo_ready, 1)
            split_lo(1)

            def attention_scores(u):
                t, pair = divmod(u, HEADS // 2)
                keys = P * (t + 1)
                i = HEADS * t + 2 * pair
                dve.wait_ge(scored, u + 1)
                then(dve.tensor_tensor(pr[:, u % 2, :, 0:keys], ps[:, 4, 0:2 * keys].rearrange("p (h k) -> p h k", k=keys),
                                       causal[:, SEQ - keys:].unsqueeze(1).to_broadcast([P, 2, keys]), ALU.add))
                then(dve.tensor_reduce(rmax[:, i:i + 2], pr[:, u % 2, :, 0:keys], AX_X, ALU.max))
                dve.tensor_scalar(nmax[:, i:i + 2], rmax[:, i:i + 2], -SCALE, None, ALU.mult)\
                   .then_inc(rowmax_ready, 1)

            def attention_out(t):
                v = slice(HEADS * t, HEADS * t + HEADS)
                dve.wait_ge(exp_ready, HEADS * (t + 1))
                then(dve.reciprocal(rinv[:, v], rsum[:, v]))
                dve.wait_ge(pv_done, UNITS // T * (t + 1))
                dve.tensor_tensor(o_sb[:, t, :].rearrange("p (h d) -> p h d", d=VH),
                                  ps[:, 7, :].rearrange("p (h d) -> p h d", d=VH),
                                  rinv[:, v].unsqueeze(2).to_broadcast([P, HEADS, VH]), ALU.mult)\
                   .then_inc(o_ready, 1)

            def branch_turned_lo(i, t):
                v = slice(P * t, P * t + P)
                dve.wait_ge(bThi_ready, 1 + i + 1)
                dve.tensor_tensor(bT_lo[:, :, v], ps[:, 5, :].rearrange("p (a b) -> p a b", b=P), bT_hi[:, :, v],
                                  ALU.subtract).then_inc(bTlo_ready, 1)

            def merge(c):
                b, cols = c // 2, slice(BANK * (c % 2), BANK * (c % 2) + BANK)
                dve.wait_ge(half_used, H_GATE + 3 * c + 3)
                dve.wait_ge(gate_ready, T * (c + 1))
                if b:
                    for t in range(T):
                        last = dve.scalar_tensor_tensor(gv[:, t, :], gv[:, t, :], 1.0, ps[:, t, :], ALU.add, ALU.mult)
                    then(last)
                for t in range(T):
                    if b:
                        ins = dve.tensor_tensor(merged[:, t, cols], merged[:, t, cols], gv[:, t, :], ALU.add)
                    else:
                        ins = dve.scalar_tensor_tensor(merged[:, t, cols], gv[:, t, :], 1.0, ps[:, t, :],
                                                       ALU.add, ALU.mult)
                    ins.then_inc(merged_ready, 1)

            def residual(c):
                dve.wait_ge(half_used, H_WO + 3 + c)
                v = slice(BANK * c, BANK * c + BANK)
                for t in range(T):
                    dve.tensor_tensor(xs[:, t, v], xs[:, t, v], ps[:, 2 - 2 * c + t, :], ALU.add)\
                       .then_inc(x1_ready, 1)

            def x1_turned(c):
                for t in range(T):
                    b = T * c + t
                    dve.wait_ge(x_turned, b + 1)
                    dve.tensor_copy(x1T[:, 4 * c:4 * c + 4, P * t:P * t + P],
                                    ps[:, 4 + b, :].rearrange("p (a b) -> p a b", b=P)).then_inc(x1T_ready, 1)

            for n in range(N_MIX):
                if n == N_MIX - 1:
                    residual(0)
                if n == H_CKV:
                    mean_square(1, QR)
                if n == H_CB:
                    mean_square(2, KVR)
                if n == H_SGV:
                    dve.wait_ge(qk_turned, 1)
                    dve.tensor_copy(kT[:, :, 0:P], joined(ps[0:QK, 6:8, :]).rearrange("p (a b) -> p a b", b=P))\
                       .then_inc(kT_ready, 1)
                if n + AHEAD < N_MIX:
                    split_lo(n + AHEAD)
                else:
                    split_lo(n + AHEAD, 0)
                if n == H_CKV:
                    r = refine(1)
                    for t in range(T):
                        dve.tensor_scalar(cn[:, t, 0:QR], ps[:, t, 0:QR], r[:, t:t + 1], None, ALU.mult)\
                           .then_inc(cn_ready, 1)
                if n == H_CB:
                    r = refine(2)
                    for t in range(T):
                        dve.tensor_copy(q9[:, t, HEADS, NOPE:], ps[:, 2 + t, KVR:KVR + ROPE])
                        dve.tensor_scalar(cn[:, t, QR:], ps[:, 2 + t, 0:KVR], r[:, t:t + 1], None, ALU.mult)\
                           .then_inc(cn_ready, 1)
                    dve.wait_ge(small_turned, 1)
                    dve.tensor_copy(taps[:], ps[:, 4, 0:ROWS]).then_inc(taps_ready, 1)
                    dve.tensor_copy(wsT[:], ps[:, 5, :].rearrange("p (a b) -> p a b", b=P)).then_inc(wsT_ready, 1)
                if n == H_CC:
                    dve.wait_ge(small_in, 16 * SMALL)
                    dve.wait_ge(c_turned, 1)
                    dve.tensor_tensor(cT_f[:], joined(ps[:, 4:7, :])[:, 0:KC * SEQ].rearrange("p (a b) -> p a b", b=SEQ),
                                      g_c[:].unsqueeze(2).to_broadcast([P, KC, SEQ]), ALU.mult).then_inc(cTf_ready, 1)
                if n == H_CC + 1:
                    dve.wait_ge(cThi_ready, 1)
                    dve.tensor_tensor(cT_lo[:], cT_f[:], cT_hi[:], ALU.subtract).then_inc(cTlo_ready, 1)
                if n == H_CH:
                    dve.wait_ge(q_ready, T)
                    dve.wait_ge(rot_ready, 1)
                    one, two = q9[:, :, :, NOPE:NOPE + R2], q9[:, :, :, NOPE + R2:]
                    sin, cos = (rot[:, i, :, :].unsqueeze(2).to_broadcast([P, T, HEADS + 1, R2]) for i in range(2))
                    dve.tensor_tensor(rt[:, 0, :, :, :], one, cos, ALU.mult)
                    dve.tensor_tensor(rt[:, 1, :, :, :], two, sin, ALU.mult)
                    dve.tensor_tensor(rt[:, 2, :, :, :], two, cos, ALU.mult)
                    then(dve.tensor_tensor(rt[:, 3, :, :, :], one, sin, ALU.mult))
                    dve.tensor_tensor(one, rt[:, 0, :, :, :], rt[:, 1, :, :, :], ALU.subtract)
                    then(dve.tensor_tensor(two, rt[:, 2, :, :, :], rt[:, 3, :, :, :], ALU.add))
                    for t in range(T):
                        dve.tensor_copy(kk[:, t, :, NOPE:], q9[:, t, HEADS:, NOPE:].to_broadcast([P, HEADS, ROPE]))\
                           .then_inc(rope_ready, 1)
                if n == H_SGV:
                    dve.wait_ge(half_used, H_SGV)
                    dve.wait_ge(cc_ready, 1)
                    dve.wait_ge(zpad_ready, 1)
                    z = z_sb[:, :, TAPS - 1:]
                    then(dve.tensor_tensor(z, joined(ps[:, 0:2, :]).rearrange("p (a b) -> p a b", b=SEQ), z, ALU.mult),
                         z_ready)
                if n == H_SGV + 1:
                    dve.wait_ge(qk_turned, 2)
                    dve.tensor_copy(kT[:, :, P:], joined(ps[0:QK, 6:8, :]).rearrange("p (a b) -> p a b", b=P))\
                       .then_inc(kT_ready, 1)
                    dve.wait_ge(cb_ready, 1)
                    for j in range(TAPS):
                        for b in range(4):
                            w, zj = taps[:, 4 * j + b:4 * j + b + 1], z_sb[:, b, j:j + SEQ]
                            if j == 0:
                                last = dve.tensor_scalar(bT_f[:, b, :], zj, w, None, ALU.mult)
                            else:
                                last = dve.scalar_tensor_tensor(bT_f[:, b, :], zj, w, bT_f[:, b, :], ALU.mult, ALU.add)
                        then(last)
                    dve.tensor_tensor(bT_f[:], bT_f[:], cb_sb[:], ALU.mult).then_inc(bTf_ready, 1)
                if n == H_SGU:
                    dve.wait_ge(bThi_ready, 1)
                    dve.tensor_tensor(bT_lo[:], bT_f[:], bT_hi[:], ALU.subtract).then_inc(bTlo_ready, 1)
                    mean_square(3, SG)
                if 0 <= n - H_ATT - 1 < UNITS:
                    attention_scores(n - H_ATT - 1)
                if n == H_SGU + 1:
                    r = refine(3)
                    for t in range(T):
                        dve.scalar_tensor_tensor(gv[:, t, :], gv[:, t, :], r[:, t:t + 1], g_sg[:], ALU.mult, ALU.mult)\
                           .then_inc(gvn_ready, 1)
                for t in range(T):
                    if n == H_GATE + 1 + t:
                        dve.wait_ge(mixed_done, t + 1)
                        dve.wait_ge(gu_ready, T)
                        for g in range(SGG):
                            v = slice(P * g, P * g + P)
                            last = dve.scalar_tensor_tensor(gu_s[:, t, v], ps[:, 5, v],
                                                            taps[:, 4 * TAPS + g:4 * TAPS + g + 1],
                                                            gu_s[:, t, v], ALU.add, ALU.mult)
                        last.then_inc(sgy_ready, 1)
                for t in range(T):
                    if n == H_ATT + UNITS // T * (t + 1) + 2:
                        attention_out(t)
                for b in (1, 2):
                    for t in range(T):
                        if n == H_GATE + 6 * b + t:
                            branch_turned_lo(T * (b - 1) + t, t)
                for c in range(6):
                    if n == H_GATE + 3 * c + 3:
                        merge(c)
                if n in (H_WO - 1, H_WO + 1):
                    for b in ((0, 1) if n < H_WO else (2, 3)):
                        t, k = b % 2, 4 * (b // 2)
                        v = slice(P * t, P * t + P)
                        dve.wait_ge(mhi_ready, b + 1)
                        dve.scalar_tensor_tensor(hT_lo[:, k:k + 4, v], ps[:, 4 + b, :].rearrange("p (a b) -> p a b", b=P),
                                                 0.5, hT_hi[:, k:k + 4, v], ALU.mult, ALU.subtract)\
                           .then_inc(mlo_ready, 1)

            x1_turned(0)
            residual(1)
            x1_turned(1)
            mean_square(4, D)
            r = refine(4)
            for t in range(T):
                dve.wait_ge(xhi_ready, t + 1)
                dve.tensor_tensor(x_lo[:, t, :], xs[:, t, :], x_hi[:, t, :], ALU.subtract).then_inc(xlo_ready, 1)

            def over(ap, n):
                return ap.to_broadcast([P, T, n])

            def one_hot(out, values, best, index, n, tmp, low):
                if best is not scal[4]:
                    then(dve.tensor_reduce(best, values, AX_X, ALU.max))
                then(dve.tensor_tensor(tmp, values, over(best, n), ALU.is_equal))
                then(dve.scalar_tensor_tensor(tmp, tmp, -BIG, index[:].unsqueeze(1).to_broadcast([P, T, n]),
                                              ALU.mult, ALU.add))
                then(dve.tensor_reduce(low, tmp, AX_X, ALU.min))
                return dve.tensor_tensor(out, tmp, over(low, n), ALU.is_equal)

            scal = [sc[:, i, :, :] for i in range(14)]
            dve.wait_ge(logits_done, 1)
            for t in range(T):
                last = dve.scalar_tensor_tensor(lg[:, t, :], ps[:, 2 + t, 0:NR], r[:, t:t + 1], b_rt[:], ALU.mult, ALU.add)
            then(last)
            dve.wait_ge(index_ready, 1)
            then(one_hot(goh[:], lg[:, :, 0:NG], scal[0], idx_g, NG, gt[:, 2, :, :], scal[1]), goh_ready)
            unchosen, place = gt[:, 3, :, :], gt[:, 4, :, :]
            dve.tensor_scalar(unchosen, goh[:], NOWHERE, -NOWHERE, ALU.mult, ALU.add)
            dve.tensor_tensor(gt[:, 0, :, :], lg[:, :, 0:NG], over(scal[0], NG), ALU.subtract).then_inc(gmax_ready, 1)
            then(dve.tensor_tensor(eg[:], lg[:, :, NG:].rearrange("p t (g e) -> p t g e", e=EPG),
                                   goh[:].unsqueeze(3).to_broadcast([P, T, NG, EPG]), ALU.mult))
            dve.wait_ge(ranked, 1)
            then(dve.tensor_tensor(place, ps[:, 2, 0:T * NG].rearrange("p (t g) -> p t g", g=NG), unchosen, ALU.add))
            for g in range(NG):
                for t in range(T):
                    dve.tensor_scalar(sel[:, t, P * g:P * g + P], slot_f[:], place[:, t, g:g + 1], None, ALU.is_equal)\
                       .then_inc(sel_ready, 1)
            chosen = et[:, 0, :, :]
            dve.tensor_reduce(chosen, eg[:].rearrange("p t g e -> p t e g"), AX_X, ALU.add)
            then(dve.tensor_reduce(scal[6], place, AX_X, ALU.max))
            then(dve.tensor_scalar(scal[12], scal[6], -float(P), None, ALU.add))
            for t in range(T):
                dve.tensor_scalar(sel[:, t, P * NG:], slot_f[:], scal[12][:, t, :], None, ALU.is_equal)\
                   .then_inc(sel_ready, 1)
            first, rest, second = et[:, 2, :, :], et[:, 3, :, :], et[:, 4, :, :]
            then(one_hot(first, chosen, scal[2], idx_e, EPG, et[:, 1, :, :], scal[3]))
            then(dve.scalar_tensor_tensor(rest, first, LOWEST, chosen, ALU.mult, ALU.add))
            then(dve.tensor_reduce(scal[4], rest, AX_X, ALU.max))
            dve.tensor_tensor(scal[7], scal[4], scal[2], ALU.subtract).then_inc(d_ready, 1)
            then(one_hot(second, rest, scal[4], idx_e, EPG, et[:, 1, :, :], scal[5]))
            root_r = r.unsqueeze(2)
            dve.wait_ge(gexp_ready, 1)
            then(dve.tensor_reduce(scal[9], gt[:, 1, :, :], AX_X, ALU.add))
            dve.wait_ge(eexp_ready, 1)
            then(dve.scalar_tensor_tensor(scal[10], scal[8], 1.0, scal[9], ALU.add, ALU.mult))
            then(dve.reciprocal(scal[11], scal[10]))
            then(dve.tensor_tensor(scal[11], scal[11], root_r, ALU.mult))
            then(dve.tensor_tensor(scal[13], scal[11], scal[8], ALU.mult))
            dve.tensor_tensor(et[:, 5, :, :], first, over(scal[11], EPG), ALU.mult)
            dve.tensor_copy(cw[:, :, EPG:], root_r)
            then(dve.tensor_tensor(et[:, 6, :, :], second, over(scal[13], EPG), ALU.mult))
            then(dve.tensor_tensor(cw[:, :, 0:EPG], et[:, 5, :, :], et[:, 6, :, :], ALU.add), comb_split)
            dve.wait_ge(comb_hi, 1)
            dve.tensor_tensor(cw_parts[:, :, 1, :], cw[:], cw_parts[:, :, 0, :], ALU.subtract).then_inc(comb_lo, 1)
            dve.wait_ge(counted, 1)
            then(dve.tensor_scalar(cnt[:, 0, :], ps[:, 3, 0:NG], float(P), None, ALU.is_gt))
            then(dve.scalar_tensor_tensor(cnt[:, 1, :], idx_g[:], -BIG, cnt[:, 0, :], ALU.add, ALU.mult))
            dve.tensor_reduce(ctl_f[:, 0:1], cnt[:, 0, :], AX_X, ALU.add)
            then(dve.tensor_reduce(ctl_f[:, 1:2], cnt[:, 1, :], AX_X, ALU.add))
            dve.tensor_copy(ctl[:], ctl_f[:, 0:2]).then_inc(ctl_ready, 1)

            def gathered(g, h):
                dve.wait_ge(tokens_gathered, 2 * g + h + 1)
                dve.tensor_tensor(xg_f[:, 4 * h:4 * h + 4, :], ps[:, h, :].rearrange("p (a b) -> p a b", b=P),
                                  g_ffn[:, 4 * h:4 * h + 4].unsqueeze(2).to_broadcast([P, 4, P]), ALU.mult)\
                   .then_inc(xgf_ready, 1)

            def gathered_lo(g, h):
                dve.wait_ge(xghi_ready, 2 * g + h + 1)
                dve.wait_ge(xgf_ready, 2 * g + h + 1)
                v = slice(4 * h, 4 * h + 4)
                dve.tensor_tensor(xg_lo[:, v, :], xg_f[:, v, :], xg_hi[:, v, :], ALU.subtract).then_inc(xglo_ready, 1)

            def turned_lo(e, g):
                dve.wait_ge(hidThi_ready, EPG * g + e + 1)
                dve.tensor_tensor(hidT_lo[:, e % 2, :, :], ps[:, e % 2, 0:DE].rearrange("p (a b) -> p a b", b=P),
                                  hidT_hi[:, e % 2, :, :], ALU.subtract).then_inc(hidTlo_ready, 1)

            def hidden(e, g):
                dve.wait_ge(silu_ready, EPG * g + e + 1)
                dve.scalar_tensor_tensor(hid[:, e % 2, :], silu[:, e % 2, :],
                                         comb[:, bass.ds(g, 1), e:e + 1].rearrange("p a b -> p (a b)"),
                                         ps[:, e % 2, DE:2 * DE], ALU.mult, ALU.mult).then_inc(hid_ready, 1)

            def group(g, more, opening=False, again=False):
                if again:
                    for j in range(AHEAD):
                        split_lo(N_MIX + j, g)
                for j, (what, e) in enumerate(order):
                    if opening and j == 1:
                        dve.wait_ge(comb_done, 1)
                        dve.tensor_reduce(comb[:], ps[:, 3, SEQ:SEQ + COMB_COLS].rearrange("p (g i e) -> p g e i", i=2, e=EPG + 1),
                                          AX_X, ALU.add).then_inc(comb_ready, 1)
                        dve.wait_ge(comb_ready, 1)
                    if j == 1:
                        dve.tensor_copy(root_g[:], comb[:, bass.ds(g, 1), EPG:].rearrange("p a b -> p (a b)"))\
                           .then_inc(rootg_ready, 1)
                    if what == "up0" and e == 1:
                        hidden(0, g)
                    if what == "up1" and e:
                        turned_lo(e - 1, g)
                    if what == "down" and e < EPG - 1:
                        hidden(e + 1, g)
                    if what == "down" and e == EPG - 1:
                        turned_lo(e, g)
                        if more:
                            gathered(g + 1, 0)
                            gathered_lo(g + 1, 0)
                    if more or j + AHEAD < PER_GROUP:
                        split_lo(N_MIX + j + AHEAD, g)
                if more:
                    gathered(g + 1, 1)
                    gathered_lo(g + 1, 1)
                dve.wait_ge(yhi_ready, g + 1)
                dve.tensor_tensor(y_lo[:], joined(ps[:, 2:4, :]), y_hi[:], ALU.subtract).then_inc(ylo_ready, 1)

            for h in range(2):
                gathered(0, h)
                gathered_lo(0, h)
            group(0, True, opening=True)
            with dve.Fori(1, NG - 1) as g:
                group(g, True)
            group(NG - 1, False)
            dve.wait_ge(ctl_ready, 1)
            more_tokens = dve.value_load(ctl[0:1, 0:1], min_val=0, max_val=1)
            with dve.If(more_tokens > 0):
                for h in range(2):
                    gathered(NG, h)
                    gathered_lo(NG, h)
                group(NG, False, again=True)
            dve.wait_ge(scattered, more_tokens + NG + 1)
            for t in range(T):
                dve.tensor_tensor(x2[:, t, :], xs[:, t, :], joined(ps[:, 4 + 2 * t:6 + 2 * t, :]), ALU.add)\
                   .then_inc(x2_ready, 1)
            mean_square(5, D)
            r = refine(5)
            for t in range(T):
                dve.scalar_tensor_tensor(xs[:, t, :], x2[:, t, :], r[:, t:t + 1], g_fin[:], ALU.mult, ALU.mult)\
                   .then_inc(y_ready, 1)

        @block.tensor
        def _(pe):
            def three(dst, x_hi, x_lo, hi, lo, first, last, weights_stand=False):
                for i, (x_part, w_part) in enumerate(((x_hi, hi), (x_hi, lo), (x_lo, hi))):
                    a, b = (w_part, x_part) if weights_stand else (x_part, w_part)
                    ins = pe.matmul(dst, a, b, start=first and i == 0, stop=last and i == 2, skip_group_check=True)
                return ins

            def use(n):
                pe.wait_ge(lo_ready, n + 1)
                return half_view(w_hi, SPLIT, n), half_view(w_lo, SPLIT, n)

            def by_token(n, k0, banks, a_hi, a_lo, first, last, part=None):
                hi, lo = use(n)
                _, blocks, cols = halves[n]
                for k in range(*(part or (0, blocks))):
                    for t in range(T):
                        v = slice(P * t, P * t + P)
                        ins = three(ps[:, banks + t, 0:cols], a_hi[:, k0 + k, v], a_lo[:, k0 + k, v],
                                    hi[:, k, :], lo[:, k, :], first and k == 0, last and k == blocks - 1)
                if k == blocks - 1:
                    ins.then_inc(half_used, 1)

            def by_channel(n, k0, banks, first, last):
                hi, lo = use(n)
                for k in range(4):
                    for j in range(4):
                        ins = three(ps[:, banks + j // 2, SEQ * (j % 2):SEQ * (j % 2) + SEQ],
                                    hT_hi[:, k0 + k, :], hT_lo[:, k0 + k, :], hi[:, k, P * j:P * j + P],
                                    lo[:, k, P * j:P * j + P], first and k == 0 and j % 2 == 0, last and k == 3,
                                    weights_stand=True)
                ins.then_inc(half_used, 1)

            def wide(n, k0, a_k0, banks, first, last):
                hi, lo = use(n)
                _, blocks, cols = halves[n]
                for k in range(blocks):
                    for t in range(T):
                        v = slice(P * t, P * t + P)
                        for c in range(0, cols, BANK):
                            w = min(BANK, cols - c)
                            ins = three(ps[:, banks + 2 * t + c // BANK, 0:w], cT_hi[:, a_k0 + k0 + k, v],
                                        cT_lo[:, a_k0 + k0 + k, v], hi[:, k, c:c + w], lo[:, k, c:c + w],
                                        first and k == 0, last and k == blocks - 1)
                ins.then_inc(half_used, 1)
            def place(u):
                t, pair = divmod(u, HEADS // 2)
                return t, 2 * pair, P * (t + 1)

            def attention_s(u):
                t, h0, keys = place(u)
                pe.wait_ge(qT_ready, t + 1)
                pe.wait_ge(kT_ready, T if u == 0 else t + 1)
                if u == 0:
                    pe.wait_ge(qT_ready, T)
                else:
                    pe.wait_ge(rowmax_ready, u)
                for h in range(2):
                    ins = pe.matmul(ps[:, 4, keys * h:keys * h + keys], qT[:, h0 + h, P * t:P * t + P],
                                    kT[:, h0 + h, 0:keys], start=True, stop=True)
                ins.then_inc(scored, 1)

            def attention_t(u):
                t, _, _ = place(u)
                pe.wait_ge(exp_ready, 2 * (u + 1))
                if u:
                    pe.wait_ge(pT_ready, u)
                for h in range(2):
                    for b in range(t + 1):
                        i = h * (t + 1) + b
                        ins = pe.transpose(ps[:, 6, P * i:P * i + P], pr[:, u % 2, h, P * b:P * b + P], ident[:])
                ins.then_inc(p_turned, 1)

            def attention_pv(u):
                t, h0, _ = place(u)
                pe.wait_ge(pT_ready, u + 1)
                if u == UNITS // T:
                    pe.wait_ge(o_ready, 1)
                for h in range(2):
                    for b in range(t + 1):
                        ins = pe.matmul(ps[:, 7, VH * (h0 + h):VH * (h0 + h) + VH], pT[:, u % 2, h * (t + 1) + b, :],
                                        v_sb[:, b, h0 + h, :], start=b == 0, stop=b == t)
                ins.then_inc(pv_done, 1)

            def turn_branch(src, i, t):
                if i:
                    pe.wait_ge(bTlo_ready, 1 + i)
                for b in range(4):
                    ins = pe.transpose(ps[:, 5, P * b:P * b + P], src[:, t, P * b:P * b + P], ident[:])
                ins.then_inc(branch_turned, 1)

            def turn_merged(b):
                t, k0 = b % 2, 4 * (b // 2)
                for k in range(4):
                    ins = pe.transpose(ps[:, 4 + b, P * k:P * k + P], merged[:, t, P * (k0 + k):P * (k0 + k) + P],
                                       ident[:])
                ins.then_inc(m_turned, 1)

            def turn_x1(c):
                for t in range(T):
                    pe.wait_ge(x1_ready, T * c + t + 1)
                    for k in range(4):
                        v = slice(P * (4 * c + k), P * (4 * c + k) + P)
                        ins = pe.transpose(ps[:, 4 + T * c + t, P * k:P * k + P], xs[:, t, v], ident[:])
                    ins.then_inc(x_turned, 1)

            def logits(c):
                for t in range(T):
                    pe.wait_ge(x1T_ready, T * c + t + 1)
                    for k in range(4 * c, 4 * c + 4):
                        ins = pe.matmul(ps[:, 2 + t, 0:NR], x1T[:, k, P * t:P * t + P], w_rt[:, k, :],
                                        start=k == 0, stop=k == KD - 1)
                return ins

            pe.wait_ge(consts_ready, 1)
            for b in range(2 * T):
                t, k0 = b // 2, 4 * (b % 2)
                pe.wait_ge(xn_ready, t + 1)
                for k in range(4):
                    ins = pe.transpose(ps[:, 4 + b, P * k:P * k + P], xn[:, t, k0 + k:D:KD], ident[:])
                ins.then_inc(h_turned, 1)

            pe.wait_ge(hTlo_ready, 2 * T)
            for n in (H_CQ, H_CQ + 1):
                by_token(n, 4 * (n - H_CQ), 0, hT_hi, hT_lo, n == H_CQ, n != H_CQ)
            for n in (H_CKV, H_CKV + 1):
                by_token(n, 4 * (n - H_CKV), 2, hT_hi, hT_lo, n == H_CKV, n != H_CKV)
            pe.wait_ge(small_in, 16 * SMALL)
            pe.transpose(ps[:, 4, 0:ROWS], cw_raw[:], ident[0:ROWS, 0:ROWS])
            for g in range(SGG):
                ins = pe.transpose(ps[:, 5, P * g:P * g + P], ws_raw[:, g, :], ident[:])
            ins.then_inc(small_turned, 1)
            pe.wait_ge(cn_ready, T)
            for n in (H_CB, H_CB + 1):
                by_channel(n, 4 * (n - H_CB), 0, n == H_CB, n != H_CB)
            pe.wait_ge(cn_ready, 2 * T)
            pe.wait_ge(taps_ready, 1)
            pe.wait_ge(wsT_ready, 1)
            for b in range(KC):
                c0, step, end = (b, KQ, QR) if b < KQ else (QR + b - KQ, KKV, QR + KVR)
                for t in range(T):
                    c = SEQ * (b % 2) + P * t
                    ins = pe.transpose(ps[:, 4 + b // 2, c:c + P], cn[:, t, c0:end:step], ident[:])
            ins.then_inc(c_turned, 1)
            for n in (H_CC, H_CC + 1):
                by_channel(n, 4 * (n - H_CC), 2, n == H_CC, n != H_CC)
            pe.wait_ge(cTlo_ready, 1)
            pe.wait_ge(cb_ready, 1)
            pe.wait_ge(cc_ready, 1)
            wide(H_QUP, 0, 0, 0, True, False)
            wide(H_QUP + 1, 2, 0, 0, False, True)
            wide(H_KVUP, 0, KQ, 4, True, True)
            pe.wait_ge(q_ready, 1)
            for n in (H_CH, H_CH + 1):
                by_channel(n, 4 * (n - H_CH), 0, n == H_CH, n != H_CH)

            def turn_qk(t):
                pe.wait_ge(rope_ready, T)
                if t == 0:
                    pe.wait_ge(kv_ready, 2 * T)
                else:
                    pe.wait_ge(qT_ready, t)
                    pe.wait_ge(kT_ready, t)
                for i, src in enumerate((q9, kk)):
                    for h in range(HEADS):
                        ins = pe.transpose(ps[0:QK, 4 + 2 * i + h // 4, P * (h % 4):P * (h % 4) + P],
                                           src[:, t, h, :], ident[:])
                ins.then_inc(qk_turned, 1)

            turn_qk(0)
            pe.wait_ge(q_ready, T)
            by_token(H_SGV, 0, 2, hT_hi, hT_lo, True, False)
            turn_qk(1)
            by_token(H_SGV + 1, 4, 2, hT_hi, hT_lo, False, True)
            pe.wait_ge(z_ready, 1)

            for n in range(H_SGU, N_MIX):
                if n < H_GATE:
                    by_token(n, 4 * (n - H_SGU), 0, hT_hi, hT_lo, n == H_SGU, n != H_SGU)
                elif n < H_WO:
                    c, j = divmod(n - H_GATE, 3)
                    if j == 0:
                        if c == 0:
                            pe.wait_ge(gv_ready, T)
                        else:
                            pe.wait_ge(gate_ready, T * c)
                    if j < 2:
                        by_token(n, 4 * j, 2, hT_hi, hT_lo, j == 0, j == 1)
                    else:
                        b = c // 2
                        if c == 0:
                            pe.wait_ge(gu_ready, T)
                        else:
                            pe.wait_ge(merged_ready, T * c)
                        pe.wait_ge(bTlo_ready, 1 + T * b)
                        by_token(n, 0, 0, bT_hi, bT_lo, True, True)
                else:
                    j, c = divmod(n - H_WO, 2)
                    if n == H_WO:
                        pe.wait_ge(gate_ready, 6 * T)
                        pe.wait_ge(mlo_ready, 2)
                    if n == H_WO + 1:
                        pe.wait_ge(merged_ready, 6 * T)
                    if n == H_WO + 2:
                        pe.wait_ge(mlo_ready, 4)
                    if n < N_MIX - 1:
                        by_token(n, 4 * j, 2 - 2 * c, hT_hi, hT_lo, j == 0, j == 1)
                    else:
                        by_token(n, 4 * j, 2 - 2 * c, hT_hi, hT_lo, False, True, (0, 2))
                        turn_x1(0)
                        by_token(n, 4 * j, 2 - 2 * c, hT_hi, hT_lo, False, True, (2, 4))
                if 0 <= n - H_ATT < UNITS:
                    attention_s(n - H_ATT)
                if 0 <= n - H_ATT - 1 < UNITS:
                    attention_t(n - H_ATT - 1)
                if 0 <= n - H_ATT - 2 < UNITS:
                    attention_pv(n - H_ATT - 2)
                for t in range(T):
                    if n == H_GATE + t:
                        pe.wait_ge(gvn_ready, t + 1)
                        pe.wait_ge(wsT_masked, 1)
                        if t:
                            pe.wait_ge(sgy_ready, t)
                        for g in range(SGG):
                            v = slice(P * g, P * g + P)
                            ins = pe.matmul(ps[:, 5, v], wsT[:, g, :], gv[:, t, v], start=True, stop=True)
                        ins.then_inc(mixed_done, 1)
                    if n == H_GATE + 5 + t:
                        pe.wait_ge(sgy_ready, T)
                        turn_branch(gu_s, t, t)
                    if n == H_GATE + 11 + t:
                        pe.wait_ge(o_ready, t + 1)
                        turn_branch(o_sb, T + t, t)
                if n == H_WO - 2:
                    pe.wait_ge(merged_ready, 5 * T)
                    turn_merged(0)
                    turn_merged(1)
                if n == H_WO:
                    pe.wait_ge(merged_ready, 6 * T)
                    turn_merged(2)
                    turn_merged(3)

            pe.wait_ge(router_w_ready, 1)
            logits(0)
            turn_x1(1)
            logits(1).then_inc(logits_done, 1)
            pe.wait_ge(x1T_ready, 2 * T)
            pe.wait_ge(ylo_ready, 1)
            pe.wait_ge(selTg_ready, 1)
            for b in range(4):
                ins = pe.matmul(ps[:, 4 + b, :], selT_g[:, 0:P], y_hi[:, 0:BANK], start=True, stop=True)
            ins.then_inc(scattered, 1)
            pe.wait_ge(goh_ready, 1)
            chosen = goh[:].rearrange("p t g -> p (t g)")
            pe.matmul(ps[:, 2, 0:2 * NG], before[:], chosen, start=True, stop=False, skip_group_check=True)
            pe.matmul(ps[:, 2, NG:2 * NG], ones[:], goh[:, 0, :], start=False, stop=True, skip_group_check=True)\
              .then_inc(ranked, 1)
            for t in range(T):
                ins = pe.matmul(ps[:, 3, 0:NG], ones[:], goh[:, t, :], start=t == 0, stop=t == 1)
            ins.then_inc(counted, 1)

            def gather(g, h):
                for k in range(4):
                    cols = slice(4 * h + k, D, KD)
                    for i in range(2 * T):
                        part, t = (x_hi, x_lo)[i // T], i % T
                        ins = pe.matmul(ps[:, h, P * k:P * k + P], part[:, t, cols],
                                        sel[:, t, bass.ds(g * P, P)], start=i == 0, stop=i == 2 * T - 1)
                ins.then_inc(tokens_gathered, 1)

            pe.wait_ge(xlo_ready, T)
            pe.wait_ge(sel_ready, T)
            gather(0, 0)
            gather(0, 1)

            def maps():
                pe.wait_ge(sel_ready, T * (NG + 1))
                pe.wait_ge(ctl_ready, 1)
                pe.wait_ge(comb_lo, 1)
                for g in range(NG + 1):
                    c = SEQ + 2 * (EPG + 1) * g
                    for t in range(T):
                        ins = pe.matmul(ps[:, 3, c:c + 2 * (EPG + 1)], sel[:, t, P * g:P * g + P],
                                        cw_parts[:, t, :, :].rearrange("p i e -> p (i e)"), start=t == 0, stop=t == T - 1)
                ins.then_inc(comb_done, 1)
                pe.wait_ge(xgf_ready, 2)
                for g in range(NG + 1):
                    if g == NG:
                        pe.wait_ge(comb_ready, 1)
                    for t in range(T):
                        c = SEQ * (g % 2) + P * t
                        ins = pe.matmul(ps[:, 1 + g // 2, c:c + P], sel[:, t, P * g:P * g + P], ident_r[:],
                                        start=True, stop=True)
                ins.then_inc(selT_done, 1)

            def scatter(g):
                pe.wait_ge(selTg_ready, g + 1)
                for t in range(T):
                    for c in range(2):
                        for i, part in enumerate((y_hi, y_lo)):
                            ins = pe.matmul(ps[:, 4 + 2 * t + c, :], selT_g[:, P * t:P * t + P],
                                            part[:, BANK * c:BANK * c + BANK], start=False, stop=i == 1,
                                            skip_group_check=True)
                return ins

            def turn_hidden(e, g):
                pe.wait_ge(hid_ready, EPG * g + e + 1)
                for k in range(2):
                    ins = pe.transpose(ps[:, e % 2, P * k:P * k + P], hid[:, e % 2, k:DE:2], ident[:])
                ins.then_inc(hid_turned, 1)

            def expert_half(j, g):
                what, e = order[j]
                n = N_MIX + j
                pe.wait_ge(lo_ready, PER_GROUP * g + n + 1)
                cols = BANK if what != "down" else D
                hi, lo = (w[:, n % SPLIT, :].rearrange("p (k n) -> p k n", n=cols) for w in (w_hi, w_lo))
                if what != "down":
                    k0 = 4 * int(what[2])
                    if e == 0:
                        pe.wait_ge(xglo_ready, 2 * g + 1 + int(what[2]))
                    for k in range(4):
                        ins = three(ps[:, e % 2, :], xg_hi[:, k0 + k, :], xg_lo[:, k0 + k, :], hi[:, k, :], lo[:, k, :],
                                    k0 + k == 0, k0 + k == KD - 1)
                else:
                    pe.wait_ge(hidTlo_ready, EPG * g + e + 1)
                    for k in range(2):
                        for c in range(2):
                            v = slice(BANK * c, BANK * c + BANK)
                            ins = three(ps[:, 2 + c, :], hidT_hi[:, e % 2, k, :], hidT_lo[:, e % 2, k, :],
                                        hi[:, k, v], lo[:, k, v], e == 0 and k == 0, e == EPG - 1 and k == 1)
                ins.then_inc(half_used, 1)

            def group(g, more, opening=False):
                for j, (what, e) in enumerate(order):
                    if opening and j == 1:
                        maps()
                    if opening and j == 2:
                        pe.wait_ge(selT_ready, 1)
                        pe.wait_ge(comb_ready, 1)
                    if what == "up1" and e:
                        turn_hidden(e - 1, g)
                    if what == "down" and e == EPG - 1:
                        if more:
                            gather(g + 1, 0)
                        turn_hidden(e, g)
                    expert_half(j, g)
                    if what == "up1" and e == 0 and not opening:
                        pe.wait_ge(ylo_ready, g + 1)
                        scatter(g).then_inc(scattered, 1)
                if more:
                    gather(g + 1, 1)

            group(0, True, opening=True)
            with pe.Fori(1, NG - 1) as g:
                group(g, True)
            group(NG - 1, False)
            pe.wait_ge(ctl_ready, 1)
            over = pe.value_load(ctl[0:1, 0:1], min_val=0, max_val=1)
            with pe.If(over > 0):
                pe.wait_ge(hidTlo_ready, EPG * NG)
                gather(NG, 0)
                gather(NG, 1)
                group(NG, False)
            pe.wait_ge(ylo_ready, over + NG + 1)
            scatter(over + NG).then_inc(scattered, 1)


_INS = ["x", "positions", "norm_mix", "w_in", "q_norm", "w_q_up", "kv_norm", "w_kv_up", "sg_norm", "w_s", "b_s",
        "conv_w", "w_a_out", "w_b_out", "w_c_out", "w_o", "norm_ffn", "w_group_router", "b_group_router",
        "w_expert_router", "b_expert_router", "w_gate_up", "w_down", "final_norm"]


def kernel(**inputs):
    import concourse.bacc as bacc
    from concourse.bass_utils import run_bass_kernel_spmd

    nc = bacc.Bacc("TRN2", target_bir_lowering=False, num_devices=1)
    arrays, args = {}, []
    for name in _INS:
        a = np.ascontiguousarray(inputs[name])
        arrays[f"in_{name}"] = a
        args.append(nc.dram_tensor(f"in_{name}", a.shape, mybir.dt.from_np(a.dtype), kind="ExternalInput").ap())
    args.append(nc.dram_tensor("out_0", (1, SEQ, D), F32, kind="ExternalOutput").ap())
    trunk(nc, *args)
    r = run_bass_kernel_spmd(nc, [arrays], core_ids=[0])
    return r.results[0]["out_0"]
```

```python
from contextlib import ExitStack

import numpy as np
import concourse.bass as bass
from concourse import mybir

F32 = mybir.dt.float32
F32R = mybir.dt.float32r
I32 = mybir.dt.int32
ALU = mybir.AluOpType
ACT = mybir.ActivationFunctionType
AX_X = mybir.AxisListType.X

P = 128
D = 1024
SEQ = 256
T = SEQ // P
KD = D // P
EPS = 1e-6
HEADS, NOPE, ROPE, VH = 8, 64, 32, 64
QK = NOPE + ROPE
R2 = ROPE // 2
QR, KVR = 384, 256
KQ, KKV = QR // P, KVR // P
KC = KQ + KKV
SG, SGG = 512, 4
CW, TAPS = 512, 3
NG, EPG = 4, 8
NE = NG * EPG
DE = 256
NR = NG + NE
SCALE = float(QK) ** -0.5
NEG = -1.0e30
BIG = 64.0
NOWHERE = 1024.0
LOWEST = -3.0e38
MAGIC = 12582912.0
IN_SIZES = (QR, KVR, ROPE, SG, SG, CW, CW, CW, D, D, D)
C_Q, C_KV, C_KR, C_SGU, C_SGV, C_CB, C_CC, C_CH, C_GA, C_GB, C_GC = (
    sum(IN_SIZES[:i]) for i in range(len(IN_SIZES)))

HALF = 2048
RAW = 6
RAW_E = 8
SPLIT = 3
AHEAD = SPLIT - 1
SPLIT_E = 4
AHEAD_E = SPLIT_E - 1
BANK = 512

H_CQ, H_CKV, H_CB, H_CC, H_QUP, H_KVUP, H_CH, H_SGV, H_SGU = 0, 2, 4, 6, 8, 10, 11, 13, 15
H_GATE = 17
H_WO = H_GATE + 18
N_MIX = H_WO + 4
H_ATT = H_SGU
UNITS = T * HEADS // 2
PER_GROUP = 3 * EPG
SMALL = 12
ROWS = 4 * TAPS + SGG + KD
COMB_COLS = (NG + 1) * 2 * (EPG + 1)
SLOTS = (NG + 1) * P


def two_pi_parts():
    rest, parts = 2 * np.pi, []
    for _ in range(4):
        m, e = np.frexp(rest)
        part = float(np.ldexp(np.round(m * 256) / 256, int(e)))
        parts.append(part)
        rest -= part
    return parts


def trunk(nc, x, positions, norm_mix, w_in, q_norm, w_q_up, kv_norm, w_kv_up, sg_norm, w_s, b_s,
          conv_w, w_a_out, w_b_out, w_c_out, w_o, norm_ffn, w_group_router, b_group_router,
          w_expert_router, b_expert_router, w_gate_up, w_down, final_norm, out):
    x_d = x[0].rearrange("(t p) d -> p t d", p=P)
    out_d = out[0].rearrange("(t p) d -> p t d", p=P)
    win_d = w_in[0].rearrange("(p k) n -> p k n", k=KD)
    qup_d = w_q_up[0].rearrange("(p k) n -> p k n", k=KQ)
    kvup_d = w_kv_up[0].rearrange("(p k) n -> p k n", k=KKV)
    wout_d = [w[0].rearrange("(k p) n -> p k n", p=P) for w in (w_c_out, w_b_out, w_a_out)]
    wo_d = w_o[0].rearrange("(k p) n -> p k n", p=P)
    gu_d = w_gate_up[0].rearrange("e (p k) n -> e p (k n)", k=KD)
    dn_d = w_down[0].rearrange("e (p k) n -> e p (k n)", k=DE // P)

    with ExitStack() as ctx:
        def sb(name, shape, dt=F32, stack=ctx):
            return stack.enter_context(nc.sbuf_tensor(name, shape, dt))

        def sem(name):
            return ctx.enter_context(nc.semaphore(name))

        ps = ctx.enter_context(nc.psum_tensor("ps", [P, 8, BANK], F32))

        raw = sb("raw", [P, RAW, HALF])
        w_hi = sb("w_hi", [P, SPLIT, HALF], F32R)
        w_lo = sb("w_lo", [P, SPLIT, HALF], F32R)
        xs = sb("xs", [P, T, D])
        ident = sb("ident", [P, P])
        ident_r = sb("ident_r", [P, P], F32R)
        mask = sb("mask", [P, P])
        ones = sb("ones", [P, P], F32R)
        before = sb("before", [P, P], F32R)
        causal = sb("causal", [P, SEQ])
        g_mix = sb("g_mix", [P, KD])
        g_c = sb("g_c", [P, KC])
        g_row = sb("g_row", [P, D])
        w_rt = sb("w_rt", [P, KD, NR])
        rt_raw = sb("rt_raw", [P, KD, NG])
        b_rt = sb("b_rt", [P, NR])
        stat = sb("stat", [P, 6, 4, T])
        neg_half = sb("neg_half", [P, T])

        mix = ExitStack()
        hT_hi = sb("hT_hi", [P, KD, SEQ], F32R, mix)
        hT_lo = sb("hT_lo", [P, KD, SEQ], F32R, mix)
        v_sb = sb("v_sb", [P, T, HEADS, VH], F32, mix)
        qT = sb("qT", [QK, HEADS, SEQ], F32, mix)
        kT = sb("kT", [QK, HEADS, SEQ], F32, mix)
        cb_sb = sb("cb_sb", [P, 4, SEQ], F32, mix)
        z_sb = sb("z_sb", [P, 4, SEQ + TAPS - 1], F32, mix)
        pr = sb("pr", [P, 2, 2, SEQ], F32, mix)
        pT = sb("pT", [P, 2, 4, P], F32, mix)
        o_sb = sb("o_sb", [P, T, HEADS * VH], F32, mix)
        rot = sb("rot", [P, 2, T, R2], F32, mix)
        g_sg = sb("g_sg", [P, SG], F32, mix)
        wsT = sb("wsT", [P, SGG, P], F32, mix)
        taps = sb("taps", [P, ROWS], F32, mix)
        rmax = sb("rmax", [P, T * HEADS], F32, mix)
        nmax = sb("nmax", [P, T * HEADS], F32, mix)
        rsum = sb("rsum", [P, T * HEADS], F32, mix)
        rinv = sb("rinv", [P, T * HEADS], F32, mix)
        early = ExitStack()
        cn = sb("cn", [P, T, QR + KVR], F32, early)
        cT_f = sb("cT_f", [P, KC, SEQ], F32, early)
        cT_hi = sb("cT_hi", [P, KC, SEQ], F32R, early)
        cT_lo = sb("cT_lo", [P, KC, SEQ], F32R, early)
        q9 = sb("q9", [P, T, HEADS + 1, QK], F32, early)
        kk = sb("kk", [P, T, HEADS, QK], F32, early)
        rt = cn[:].rearrange("p t n -> p (t n)")[:, 0:4 * T * (HEADS + 1) * R2]\
            .rearrange("p (i t h n) -> p i t h n", i=4, t=T, n=R2)
        early.close()
        late = ExitStack()
        merged = sb("merged", [P, T, D], F32, late)
        bT_f = sb("bT_f", [P, 4, SEQ], F32, late)
        bT_hi = sb("bT_hi", [P, 4, SEQ], F32R, late)
        bT_lo = sb("bT_lo", [P, 4, SEQ], F32R, late)
        gv = sb("gv", [P, T, SG], F32, late)
        gu_s = sb("gu_s", [P, T, SG], F32, late)
        late.close()
        start = ExitStack()
        xn = sb("xn", [P, T, D], F32, start)
        ws_raw = sb("ws_raw", [P, SGG, P], F32, start)
        cw_raw = sb("cw_raw", [ROWS, P], F32, start)
        h_f = sb("h_f", [P, KD, SEQ], F32, start)
        pos_i = sb("pos_i", [P, T], I32, start)
        pos_f = sb("pos_f", [P, T], F32, start)
        inv_f = sb("inv_f", [P, R2], F32, start)
        ang = sb("ang", [P, 4, T, R2], F32, start)
        start.close()
        mix.close()

        sel = sb("sel", [P, T, SLOTS], F32R)
        selT = sb("selT", [P, NG + 1, SEQ], F32R)
        silu = sb("silu", [P, 2, DE])
        hid = sb("hid", [P, 2, DE])
        comb = sb("comb", [P, NG + 1, EPG + 1])
        sb("unused", [P, 512])
        selT_g = sb("selT_g", [P, SEQ], F32R)
        hidT_hi = sb("hidT_hi", [P, 2, 2, P], F32R)
        hidT_lo = sb("hidT_lo", [P, 2, 2, P], F32R)
        last = ExitStack()
        x2 = sb("x2", [P, T, D], F32, last)
        x2g = sb("x2g", [P, T, D], F32, last)
        last.close()
        x_hi = sb("x_hi", [P, T, D], F32R)
        x_lo = sb("x_lo", [P, T, D], F32R)
        root_g = sb("root_g", [P, 1])
        y_hi = sb("y_hi", [P, D], F32R)
        y_lo = sb("y_lo", [P, D], F32R)
        cw_parts = sb("cw_parts", [P, T, 2, EPG + 1], F32R)
        ctl = sb("ctl", [P, 2], I32)
        squared = ExitStack()
        sq = sb("sq", [P, T, D], F32, squared)
        squared.close()
        xg_hi = sb("xg_hi", [P, KD, P], F32R)
        xg_lo = sb("xg_lo", [P, KD, P], F32R)
        raw_more = sb("raw_more", [P, RAW_E - RAW, HALF])
        more = ExitStack()
        w_more = sb("w_more", [P, 2, HALF], F32R, more)
        more.close()
        router = ExitStack()
        x1T = sb("x1T", [P, KD, SEQ], F32, router)
        xf = sb("xf", [P, T, D], F32, router)
        lg = sb("lg", [P, T, NR], F32, router)
        gt = sb("gt", [P, 6, T, NG], F32, router)
        goh = sb("goh", [P, T, NG], F32R, router)
        et = sb("et", [P, 8, T, EPG], F32, router)
        eg = sb("eg", [P, T, NG, EPG], F32, router)
        sc = sb("sc", [P, 14, T, 1], F32, router)
        cw = sb("cw", [P, T, EPG + 1], F32, router)
        slot_i = sb("slot_i", [P, P], I32, router)
        slot_f = sb("slot_f", [P, P], F32, router)
        idx_g = sb("idx_g", [P, NG], F32, router)
        idx_e = sb("idx_e", [P, EPG], F32, router)
        cnt = sb("cnt", [P, 3, NG], F32, router)
        ctl_f = sb("ctl_f", [P, 3], F32, router)
        router.close()
        ssq_half = sb("ssq_half", [P, 2, T])

        raw_landed = [sem(f"raw_landed{i}") for i in range(RAW_E)]
        hi_ready = sem("hi_ready")
        lo_ready = sem("lo_ready")
        half_used = sem("half_used")
        pos_in = sem("pos_in")
        final_gain_in = sem("final_gain_in")
        x_in = [sem(f"x_in{t}") for t in range(T)]
        r0_ready = sem("r0_ready")
        xn1_ready = sem("xn1_ready")
        small_in = sem("small_in")
        mix_gain_in = sem("mix_gain_in")
        inv_ready = sem("inv_ready")
        ang_ready = sem("ang_ready")
        rot_ready = sem("rot_ready")
        consts_ready = sem("consts_ready")
        router_w_ready = sem("router_w_ready")
        dve_chain = sem("dve_chain")
        pool_chain = sem("pool_chain")
        ssq_ready = sem("ssq_ready")
        ms_ready = sem("ms_ready")
        root_ready = sem("root_ready")
        xn0_ready = sem("xn0_ready")
        h_turned = sem("h_turned")
        hf_ready = sem("hf_ready")
        hThi_ready = sem("hThi_ready")
        hTlo_ready = sem("hTlo_ready")
        small_turned = sem("small_turned")
        taps_ready = sem("taps_ready")
        wsT_ready = sem("wsT_ready")
        wsT_masked = sem("wsT_masked")
        cn_ready = sem("cn_ready")
        c_turned = sem("c_turned")
        cTf_ready = sem("cTf_ready")
        cThi_ready = sem("cThi_ready")
        cTlo_ready = sem("cTlo_ready")
        zpad_ready = sem("zpad_ready")
        cb_ready = sem("cb_ready")
        cc_ready = sem("cc_ready")
        z_ready = sem("z_ready")
        q_ready = sem("q_ready")
        kv_ready = sem("kv_ready")
        rope_ready = sem("rope_ready")
        qk_turned = sem("qk_turned")
        qT_ready = sem("qT_ready")
        kT_ready = sem("kT_ready")
        bTf_ready = sem("bTf_ready")
        bThi_ready = sem("bThi_ready")
        bTlo_ready = sem("bTlo_ready")
        branch_turned = sem("branch_turned")
        gv_ready = sem("gv_ready")
        gvn_ready = sem("gvn_ready")
        gu_ready = sem("gu_ready")
        mixed_done = sem("mixed_done")
        sgy_ready = sem("sgy_ready")
        scored = sem("scored")
        rowmax_ready = sem("rowmax_ready")
        exp_ready = sem("exp_ready")
        p_turned = sem("p_turned")
        pT_ready = sem("pT_ready")
        pv_done = sem("pv_done")
        o_ready = sem("o_ready")
        gate_ready = sem("gate_ready")
        merged_ready = sem("merged_ready")
        m_turned = sem("m_turned")
        mhi_ready = sem("mhi_ready")
        mlo_ready = sem("mlo_ready")
        x1_ready = sem("x1_ready")
        xf0_ready = sem("xf0_ready")
        xf1_ready = sem("xf1_ready")
        xhi_ready = sem("xhi_ready")
        xlo0_ready = sem("xlo0_ready")
        xlo1_ready = sem("xlo1_ready")
        x_turned = sem("x_turned")
        x1T_ready = sem("x1T_ready")
        logits_done = sem("logits_done")
        gmax_ready = sem("gmax_ready")
        gexp_ready = sem("gexp_ready")
        d_ready = sem("d_ready")
        eexp_ready = sem("eexp_ready")
        goh_ready = sem("goh_ready")
        ranked = sem("ranked")
        counted = sem("counted")
        sel_ready = sem("sel_ready")
        comb_split = sem("comb_split")
        comb_hi = sem("comb_hi")
        comb_lo = sem("comb_lo")
        selT_done = sem("selT_done")
        selT_ready = sem("selT_ready")
        comb_done = sem("comb_done")
        comb_ready = sem("comb_ready")
        rootg_ready = sem("rootg_ready")
        ctl_ready = sem("ctl_ready")
        slot_ready = sem("slot_ready")
        index_ready = sem("index_ready")
        selTg_ready = sem("selTg_ready")
        tokens_gathered = sem("tokens_gathered")
        xghi_ready = sem("xghi_ready")
        xglo_ready = sem("xglo_ready")
        silu_ready = sem("silu_ready")
        hid_ready = sem("hid_ready")
        hid_turned = sem("hid_turned")
        hidThi_ready = sem("hidThi_ready")
        hidTlo_ready = sem("hidTlo_ready")
        sum_done = sem("sum_done")
        yhi_ready = sem("yhi_ready")
        ylo_ready = sem("ylo_ready")
        scattered = sem("scattered")
        output_done = sem("output_done")
        x2g_ready = sem("x2g_ready")
        r5_ready = sem("r5_ready")
        y1_ready = sem("y1_ready")
        x2_ready = sem("x2_ready")
        y0_ready = sem("y0_ready")
        stored = sem("stored")

        block = ctx.enter_context(nc.Block())

        halves = {}
        for h0, c0, n in ((H_CQ, C_Q, QR), (H_CKV, C_KV, KVR + ROPE), (H_CB, C_CB, CW), (H_CC, C_CC, CW),
                          (H_CH, C_CH, CW), (H_SGV, C_SGV, SG), (H_SGU, C_SGU, SG)):
            for j in range(2):
                halves[h0 + j] = (win_d[:, 4 * j:4 * j + 4, c0:c0 + n], 4, n)
        halves[H_QUP] = (qup_d[:, 0:2, :], 2, HEADS * QK)
        halves[H_QUP + 1] = (qup_d[:, 2:3, :], 1, HEADS * QK)
        halves[H_KVUP] = (kvup_d[:, :, :], 2, HEADS * (NOPE + VH))
        for b, gcol in enumerate((C_GC, C_GB, C_GA)):
            for c in range(2):
                n, c0 = H_GATE + 6 * b + 3 * c, gcol + BANK * c
                for j in range(2):
                    halves[n + j] = (win_d[:, 4 * j:4 * j + 4, c0:c0 + BANK], 4, BANK)
                halves[n + 2] = (wout_d[b][:, :, BANK * c:BANK * c + BANK], 4, BANK)
        for j in range(2):
            for c in range(2):
                halves[H_WO + 2 * j + c] = (wo_d[:, 4 * j:4 * j + 4, BANK * c:BANK * c + BANK], 4, BANK)

        def half_view(buf, slots, n):
            _, blocks, cols = halves[n]
            return buf[:, n % slots, 0:blocks * cols].rearrange("p (k n) -> p k n", n=cols)

        def expert_slot(j):
            s = j % RAW_E
            return (N_MIX + s) % RAW if s < RAW else s

        def expert_raw(j):
            s = expert_slot(j)
            return raw[:, s, :] if s < RAW else raw_more[:, s - RAW, :]

        def expert_split(j):
            s = j % SPLIT_E
            return (w_hi[:, s, :], w_lo[:, s, :]) if s < SPLIT else (w_more[:, 0, :], w_more[:, 1, :])

        def landed(j, g):
            s = expert_slot(j)
            mixer_loads = len([n for n in range(N_MIX) if n % RAW == s]) if s < RAW else 0
            return 16 * (PER_GROUP // RAW_E) * g + 16 * (mixer_loads + j // RAW_E + 1)

        def joined(banks):
            return banks.rearrange("p a b -> p (a b)")

        order = []
        for e in range(EPG):
            order += [("up0", e), ("up1", e)]
            if e:
                order.append(("down", e - 1))
        order.append(("down", EPG - 1))

        @block.sync
        def _(sp):
            for t in range(T):
                sp.dma_start(xs[:, t, :], x_d[:, t, :]).then_inc(x_in[t], 16)
            for n in range(N_MIX):
                if n >= RAW:
                    sp.wait_ge(lo_ready, n - RAW + 1)
                sp.dma_start(half_view(raw, RAW, n), halves[n][0]).then_inc(raw_landed[n % RAW], 16)

            def load_group(first_expert, g, opening=False):
                for j, (what, e) in enumerate(order):
                    n = N_MIX + j
                    if what == "down":
                        src = dn_d[bass.ds(first_expert + e, 1), :, :]
                    else:
                        k = int(what[2]) * HALF
                        src = gu_d[bass.ds(first_expert + e, 1), :, k:k + HALF]
                    if opening and j < RAW:
                        sp.wait_ge(lo_ready, n - RAW + 1)
                    elif opening and j < RAW_E:
                        sp.wait_ge(half_used, H_WO + 3)
                        sp.wait_ge(x1_ready, 1)
                    else:
                        sp.wait_ge(lo_ready, PER_GROUP * g + n - RAW_E + 1)
                    sp.dma_start(expert_raw(j), src.rearrange("a p n -> (a p) n"))\
                      .then_inc(raw_landed[expert_slot(j)], 16)

            load_group(0, 0, opening=True)
            with sp.Fori(1, NG) as g:
                load_group(g * EPG, g)
            sp.wait_ge(ctl_ready, 1)
            over = sp.value_load(ctl[0:1, 0:1], min_val=0, max_val=1)
            full = sp.value_load(ctl[0:1, 1:2], min_val=0, max_val=NG - 1)
            with sp.If(over > 0):
                load_group(full * EPG, NG)
            for t in range(T):
                sp.wait_ge(y1_ready if t else y0_ready, 1)
                sp.dma_start(out_d[:, t, :], xs[:, t, :]).then_inc(stored, 16)
            sp.wait_ge(stored, 16 * T)

        @block.gpsimd
        def _(pool):
            count = [0]

            def then(ins):
                count[0] += 1
                ins.then_inc(pool_chain, 1)
                pool.wait_ge(pool_chain, count[0])

            pool.dma_start(g_mix[:], norm_mix[0].rearrange("(p k) -> p k", k=KD)).then_inc(mix_gain_in, 16)
            for i in range(R2):
                last = pool.memset(inv_f[:, i:i + 1], float(np.float32(10000.0 ** (-2 * i / ROPE))))
            last.then_inc(inv_ready, 1)
            then(pool.memset(neg_half[:], -0.5))
            then(pool.memset(ident[:], 0.0))
            then(pool.affine_select(ident[:], ident[:], [[-1, P]], ALU.not_equal, 1.0, base=0, channel_multiplier=1))
            pool.tensor_copy(ident_r[:], ident[:]).then_inc(consts_ready, 1)
            small = [
                (cw_raw[0:4 * TAPS, :], conv_w[0].rearrange("j (b p) -> (j b) p", p=P)),
                (cw_raw[4 * TAPS:4 * TAPS + SGG, :], b_s[0]),
                (ws_raw[:], w_s[0].rearrange("g t s -> t g s")),
                (g_c[:, 0:KQ], q_norm[0].rearrange("(p k) -> p k", k=KQ)),
                (g_c[:, KQ:KC], kv_norm[0].rearrange("(p k) -> p k", k=KKV)),
                (g_sg[:], sg_norm[0].partition_broadcast(P)),
                (cw_raw[4 * TAPS + SGG:, :], norm_ffn[0].rearrange("(k p) -> k p", p=P)),
                (rt_raw[:], w_group_router[0].rearrange("(k p) n -> p k n", p=P)),
                (w_rt[:, :, NG:], w_expert_router[0].rearrange("(k p) n -> p k n", p=P)),
                (b_rt[:, 0:NG], b_group_router[0].partition_broadcast(P)),
                (b_rt[:, NG:], b_expert_router[0].partition_broadcast(P)),
                (g_row[:], norm_ffn[0].partition_broadcast(P)),
            ]
            def root(norm):
                pool.wait_ge(ms_ready, norm + 1)
                pool.tensor_tensor(stat[:, norm, 2, :], stat[:, norm, 1, :], neg_half[:], ALU.pow)\
                    .then_inc(root_ready, 1)

            root(0)
            for dst, src in small:
                pool.dma_start(dst, src).then_inc(small_in, 16)
            then(pool.memset(mask[:], 1.0))
            pool.tensor_copy(ones[:], mask[:])
            then(pool.memset(causal[:], 0.0))
            pool.affine_select(causal[:, P:], causal[:, P:], [[-1, P]], ALU.is_ge, NEG, base=0, channel_multiplier=1)
            then(pool.affine_select(mask[:], mask[:], [[1, P]], ALU.is_gt, 0.0, base=0, channel_multiplier=-1))
            pool.tensor_copy(before[:], mask[:])
            pool.memset(z_sb[:, :, 0:TAPS - 1], 0.0).then_inc(zpad_ready, 1)
            root(1)
            root(2)
            pool.wait_ge(small_in, 16 * SMALL)
            pool.wait_ge(taps_ready, 1)
            gains = taps[:, 4 * TAPS + SGG:].unsqueeze(2)
            pool.tensor_tensor(w_rt[:, :, NG:], w_rt[:, :, NG:], gains.to_broadcast([P, KD, NE]), ALU.mult)
            pool.tensor_tensor(w_rt[:, :, 0:NG], rt_raw[:], gains.to_broadcast([P, KD, NG]), ALU.mult)\
                .then_inc(router_w_ready, 1)
            pool.wait_ge(wsT_ready, 1)
            pool.affine_select(wsT[:], wsT[:], [[0, SGG], [1, P]], ALU.is_ge, 0.0, base=0, channel_multiplier=-1)\
                .then_inc(wsT_masked, 1)
            root(3)
            pool.wait_ge(half_used, H_WO + 3)
            pool.iota(slot_i[:], [[1, P]], base=0, channel_multiplier=0).then_inc(slot_ready, 1)
            pool.wait_ge(slot_ready, 1)
            then(pool.tensor_copy(slot_f[:], slot_i[:]))
            then(pool.tensor_scalar(idx_g[:], slot_f[:, 0:NG], BIG, None, ALU.add))
            pool.tensor_scalar(idx_e[:], slot_f[:, 0:EPG], BIG, None, ALU.add).then_inc(index_ready, 1)
            pool.memset(y_hi[:].bitcast(F32), 0.0).then_inc(ylo_ready, 1)
            pool.memset(selT_g[:].bitcast(F32), 0.0).then_inc(selTg_ready, 1)
            for c in range(2):
                v = slice(BANK * c, BANK * c + BANK)
                pool.wait_ge(x1_ready, T * c + 2)
                pool.tensor_tensor(xf[:, 1, v], xs[:, 1, v], g_row[:, v], ALU.mult).then_inc(xf1_ready, 1)
            root(4)
            pool.wait_ge(xhi_ready, 2 * T)
            for t in range(T):
                pool.tensor_tensor(x_lo[:, t, BANK:], xf[:, t, BANK:], x_hi[:, t, BANK:], ALU.subtract)\
                    .then_inc(xlo1_ready, 1)
            pool.wait_ge(xf0_ready, 2)
            pool.wait_ge(xf1_ready, 2)
            pool.dma_start(g_row[:], final_norm.partition_broadcast(P)).then_inc(final_gain_in, 16)

            pool.wait_ge(selT_ready, 1)
            with pool.Fori(0, NG) as g:
                pool.wait_ge(scattered, g + 1)
                pool.tensor_copy(selT_g[:], selT[:, bass.ds(g, 1), :].rearrange("p a n -> p (a n)"))\
                    .then_inc(selTg_ready, 1)
            pool.wait_ge(ctl_ready, 1)
            over = pool.value_load(ctl[0:1, 0:1], min_val=0, max_val=1)
            with pool.If(over > 0):
                pool.wait_ge(scattered, NG + 1)
                pool.tensor_copy(selT_g[:], selT[:, NG, :]).then_inc(selTg_ready, 1)
            pool.wait_ge(final_gain_in, 16)
            for c in range(2):
                v = slice(BANK * c, BANK * c + BANK)
                pool.wait_ge(x2_ready, T * c + 2)
                last = pool.tensor_tensor(x2g[:, 1, v], x2[:, 1, v], g_row[:, v], ALU.mult)
            last.then_inc(x2g_ready, 1)
            root(5)

        @block.scalar
        def _(act):
            def split_hi(n, g=None, opening=False):
                shift = 0 if g is None else PER_GROUP * g
                if n < N_MIX:
                    act.wait_ge(raw_landed[n % RAW], 16 * (n // RAW + 1))
                else:
                    act.wait_ge(raw_landed[expert_slot(n - N_MIX)], landed(n - N_MIX, g))
                if n - N_MIX == SPLIT and opening:
                    act.wait_ge(ctl_ready, 1)
                elif n - N_MIX >= SPLIT_E or n >= N_MIX and not opening:
                    act.wait_ge(half_used, shift + n - SPLIT_E + 1)
                elif n >= SPLIT:
                    act.wait_ge(half_used, n - SPLIT + 1)
                if n < N_MIX:
                    dst, src = half_view(w_hi, SPLIT, n), half_view(raw, RAW, n)
                else:
                    dst, src = expert_split(n - N_MIX)[0], expert_raw(n - N_MIX)
                act.activation(dst, src, ACT.Copy).then_inc(hi_ready, 1)

            def squares(norm, t, src, junk):
                act.activation(junk, src, ACT.Square, accum_out=stat[:, norm, 0, t:t + 1]).then_inc(ssq_ready, 1)

            for t in range(T):
                act.dma_start(pos_i[:, t:t + 1], positions[0, P * t:P * t + P].rearrange("(p a) -> p a", a=1))\
                   .then_inc(pos_in, 16)
            for t in range(T):
                act.wait_ge(x_in[t], 16)
                squares(0, t, xs[:, t, :], h_f[:, 4 * t:4 * t + 4, :].rearrange("p a b -> p (a b)"))
            split_hi(0)
            act.wait_ge(r0_ready, 1)
            act.activation(xn[:, 1, :], xs[:, 1, :], ACT.Copy, scale=stat[:, 0, 2, 1:2]).then_inc(xn1_ready, 1)
            split_hi(1)
            for b in range(2 * T):
                t, k = b % T, 4 * (b // T)
                v = slice(P * t, P * t + P)
                act.wait_ge(hf_ready, b + 1)
                act.activation(hT_hi[:, k:k + 4, v], h_f[:, k:k + 4, v], ACT.Copy).then_inc(hThi_ready, 1)

            def attention_exp(u):
                t, pair = divmod(u, HEADS // 2)
                act.wait_ge(rowmax_ready, u + 1)
                for h in range(2):
                    i = HEADS * t + 2 * pair + h
                    row = pr[:, u % 2, h, 0:P * (t + 1)]
                    act.activation(row, row, ACT.Exp, bias=nmax[:, i:i + 1], scale=SCALE,
                                   accum_out=rsum[:, i:i + 1]).then_inc(exp_ready, 1)

            def attention_pT(u):
                n = 2 * (u // (HEADS // 2) + 1)
                act.wait_ge(p_turned, u + 1)
                act.activation(pT[:, u % 2, 0:n, :], ps[:, 6, 0:n * P].rearrange("p (a b) -> p a b", b=P), ACT.Copy)\
                    .then_inc(pT_ready, 1)

            def branch_turned_hi(i, t):
                act.wait_ge(branch_turned, i + 1)
                act.activation(bT_hi[:, :, P * t:P * t + P], ps[:, 5, :].rearrange("p (a b) -> p a b", b=P), ACT.Copy)\
                    .then_inc(bThi_ready, 1)

            for n in range(N_MIX):
                if n == H_QUP:
                    act.wait_ge(half_used, H_QUP)
                    act.activation(z_sb[:, :, TAPS - 1:], joined(ps[:, 2:4, :]).rearrange("p (a b) -> p a b", b=SEQ),
                                   ACT.Copy).then_inc(cc_ready, 1)
                if 0 <= n - H_ATT - 2 < UNITS:
                    attention_pT(n - H_ATT - 2)
                if n + AHEAD < N_MIX:
                    split_hi(n + AHEAD)
                else:
                    split_hi(n + AHEAD, 0, True)
                if n == H_CQ + 1:
                    act.wait_ge(ang_ready, 1)
                    act.activation(rot[:], ang[:, 0:2, :, :], ACT.Sin).then_inc(rot_ready, 1)
                if n == H_CKV:
                    act.wait_ge(half_used, H_CKV)
                    for t in range(T):
                        squares(1, t, ps[:, t, 0:QR], xn[:, t, 0:QR])
                if n == H_CB:
                    act.wait_ge(half_used, H_CB)
                    for t in range(T):
                        squares(2, t, ps[:, 2 + t, 0:KVR], xn[:, t, QR:QR + KVR])
                if n == H_CC:
                    act.wait_ge(half_used, H_CC)
                    act.activation(cb_sb[:].rearrange("p a b -> p (a b)"), joined(ps[:, 6:8, :]), ACT.Copy)\
                        .then_inc(cb_ready, 1)
                    act.wait_ge(cTf_ready, 1)
                    act.activation(cT_hi[:], cT_f[:], ACT.Copy).then_inc(cThi_ready, 1)
                if n == H_KVUP:
                    act.wait_ge(half_used, H_KVUP)
                    for t in range(T):
                        act.activation(q9[:, t, 0:HEADS, :].rearrange("p h d -> p (h d)"),
                                       joined(ps[:, 2 * t:2 * t + 2, :])[:, 0:HEADS * QK],
                                       ACT.Copy).then_inc(q_ready, 1)
                if n == H_CH:
                    act.wait_ge(half_used, H_CH)
                    for t in range(T):
                        kv = joined(ps[:, 4 + 2 * t:6 + 2 * t, :]).rearrange("p (h d) -> p h d", d=NOPE + VH)
                        act.activation(kk[:, t, :, 0:NOPE], kv[:, :, 0:NOPE], ACT.Copy).then_inc(kv_ready, 1)
                        act.activation(v_sb[:, t, :, :], kv[:, :, NOPE:], ACT.Copy).then_inc(kv_ready, 1)
                if n in (H_SGV, H_SGV + 1):
                    t = n - H_SGV
                    act.wait_ge(qk_turned, t + 1)
                    act.activation(qT[:, :, P * t:P * t + P],
                                   joined(ps[0:QK, 4:6, :]).rearrange("p (a b) -> p a b", b=P), ACT.Copy)\
                        .then_inc(qT_ready, 1)
                if n == H_SGU:
                    act.wait_ge(half_used, H_SGU)
                    for t in range(T):
                        act.activation(gv[:, t, :], ps[:, 2 + t, :], ACT.Gelu_apprx_tanh).then_inc(gv_ready, 1)
                    act.wait_ge(gv_ready, T)
                    for t in range(T):
                        squares(3, t, gv[:, t, :], merged[:, t, 0:SG])
                    act.wait_ge(bTf_ready, 1)
                    act.activation(bT_hi[:], bT_f[:], ACT.Copy).then_inc(bThi_ready, 1)
                if 0 <= n - H_ATT - 1 < UNITS:
                    attention_exp(n - H_ATT - 1)
                if n == H_GATE:
                    act.wait_ge(half_used, H_GATE)
                    for t in range(T):
                        act.activation(gu_s[:, t, :], ps[:, t, :], ACT.Gelu_apprx_tanh).then_inc(gu_ready, 1)
                for b in (1, 2):
                    for t in range(T):
                        if n == H_GATE + 6 * b + t:
                            branch_turned_hi(T * (b - 1) + t, t)
                for c in range(6):
                    if n == H_GATE + 3 * c + 2:
                        act.wait_ge(half_used, H_GATE + 3 * c + 2)
                        act.wait_ge(gvn_ready if not c else merged_ready, T * max(c, 1))
                        if not c:
                            act.wait_ge(mixed_done, T)
                        for t in range(T):
                            act.activation(gv[:, t, :], ps[:, 2 + t, :], ACT.Tanh, scale=0.5).then_inc(gate_ready, 1)
                if n in (H_WO - 1, H_WO + 1):
                    for b in ((0, 1) if n < H_WO else (2, 3)):
                        t, k = b % 2, 4 * (b // 2)
                        act.wait_ge(m_turned, b + 1)
                        act.activation(hT_hi[:, k:k + 4, P * t:P * t + P],
                                       ps[:, 4 + b, :].rearrange("p (a b) -> p a b", b=P), ACT.Copy, scale=0.5)\
                            .then_inc(mhi_ready, 1)

            def x1_hi(c, t):
                v = slice(BANK * c, BANK * c + BANK)
                act.wait_ge(xf1_ready if t else xf0_ready, c + 1)
                act.activation(x_hi[:, t, v], xf[:, t, v], ACT.Copy).then_inc(xhi_ready, 1)

            for t in range(T):
                x1_hi(0, t)
            for t in range(T):
                act.wait_ge(x1_ready, T + t + 1)
                squares(4, t, xs[:, t, :], sq[:, t, :])
            for t in range(T):
                x1_hi(1, t)
            split_hi(N_MIX + AHEAD, 0, True)
            act.wait_ge(gmax_ready, 1)
            act.activation(gt[:, 1, :, :], gt[:, 0, :, :], ACT.Exp).then_inc(gexp_ready, 1)
            act.wait_ge(d_ready, 1)
            act.activation(sc[:, 8, :, :], sc[:, 7, :, :], ACT.Exp).then_inc(eexp_ready, 1)
            act.activation(stat[:, 4, 3, :], stat[:, 4, 2, :], ACT.Silu)

            def gathered_hi(g, h):
                act.wait_ge(tokens_gathered, 2 * g + h + 1)
                act.activation(xg_hi[:, 4 * h:4 * h + 4, :], ps[:, h, :].rearrange("p (a b) -> p a b", b=P), ACT.Copy)\
                    .then_inc(xghi_ready, 1)

            def turned_hi(e, g):
                act.wait_ge(hid_turned, EPG * g + e + 1)
                act.activation(hidT_hi[:, e % 2, :, :], ps[:, e % 2, 0:DE].rearrange("p (a b) -> p a b", b=P),
                               ACT.Copy).then_inc(hidThi_ready, 1)

            def gate(e, g):
                act.wait_ge(half_used, PER_GROUP * g + N_MIX + order.index(("up1", e)) + 1)
                if e == 0:
                    act.wait_ge(rootg_ready, g + 1)
                act.activation(silu[:, e % 2, :], ps[:, e % 2, 0:DE], ACT.Silu,
                               scale=root_g[:]).then_inc(silu_ready, 1)

            def group(g, more, opening=False, again=False):
                if again:
                    for j in range(AHEAD_E):
                        split_hi(N_MIX + j, g)
                for j, (what, e) in enumerate(order):
                    if what == "up0" and e == 1:
                        gate(0, g)
                    if what == "up1" and e:
                        turned_hi(e - 1, g)
                    if what == "down" and e < EPG - 1:
                        gate(e + 1, g)
                    if what == "down" and e == EPG - 2 and not more:
                        turned_hi(e + 1, g)
                    if what == "down" and e == EPG - 1 and more:
                        turned_hi(e, g)
                        gathered_hi(g + 1, 0)
                    if more or j + AHEAD_E < PER_GROUP:
                        split_hi(N_MIX + j + AHEAD_E, g, opening)
                    if opening and j == 1:
                        act.wait_ge(selT_done, 1)
                        act.activation(selT[:].rearrange("p a b -> p (a b)"),
                                       joined(ps[:, 2:5, :])[:, 0:(NG + 1) * SEQ], ACT.Copy).then_inc(selT_ready, 1)
                if more:
                    gathered_hi(g + 1, 1)
                act.wait_ge(scattered, g + 1)
                for c in range(2):
                    if c == 0:
                        act.wait_ge(sum_done, g + 1)
                    else:
                        act.wait_ge(half_used, PER_GROUP * g + N_MIX + PER_GROUP)
                    act.activation(y_hi[:, BANK * c:BANK * c + BANK], ps[:, 2 + c, :], ACT.Copy).then_inc(yhi_ready, 1)

            gathered_hi(0, 0)
            act.wait_ge(comb_split, 1)
            act.activation(cw_parts[:, :, 0, :], cw[:], ACT.Copy).then_inc(comb_hi, 1)
            gathered_hi(0, 1)
            group(0, True, opening=True)
            with act.Fori(1, NG - 1) as g:
                group(g, True)
            group(NG - 1, False)
            act.wait_ge(ctl_ready, 1)
            over = act.value_load(ctl[0:1, 0:1], min_val=0, max_val=1)
            with act.If(over > 0):
                gathered_hi(NG, 0)
                gathered_hi(NG, 1)
                group(NG, False, again=True)
            for c in range(2):
                for t in range(T):
                    v = slice(BANK * c, BANK * c + BANK)
                    act.wait_ge(x2_ready, T * c + t + 1)
                    act.activation(sq[:, t, v], x2[:, t, v], ACT.Square, accum_out=ssq_half[:, c, t:t + 1])\
                        .then_inc(ssq_ready, 1)
            act.wait_ge(r5_ready, 1)
            act.wait_ge(x2g_ready, 1)
            act.activation(xs[:, 1, :], x2g[:, 1, :], ACT.Copy, scale=stat[:, 5, 2, 1:2]).then_inc(y1_ready, 1)

        @block.vector
        def _(dve):
            counts = {}

            def then(ins, signal=dve_chain):
                counts[id(signal)] = counts.get(id(signal), 0) + 1
                ins.then_inc(signal, 1)
                dve.wait_ge(signal, counts[id(signal)])

            def split_lo(n, g=None):
                shift = 0 if g is None else PER_GROUP * g
                dve.wait_ge(hi_ready, shift + n + 1)
                if n < N_MIX:
                    dst, src, hi = half_view(w_lo, SPLIT, n), half_view(raw, RAW, n), half_view(w_hi, SPLIT, n)
                else:
                    (hi, dst), src = expert_split(n - N_MIX), expert_raw(n - N_MIX)
                dve.tensor_tensor(dst, src, hi, ALU.subtract).then_inc(lo_ready, 1)

            def mean_square(norm, width):
                dve.wait_ge(ssq_ready, T * (norm + 1))
                dve.tensor_scalar(stat[:, norm, 1, :], stat[:, norm, 0, :], 1.0 / width, EPS, ALU.mult, ALU.add)\
                   .then_inc(ms_ready, 1)

            def refine(norm, signal=dve_chain):
                ms, r, a = (stat[:, norm, i, :] for i in (1, 2, 3))
                dve.wait_ge(root_ready, norm + 1)
                dve.wait_ge(ms_ready, norm + 1)
                then(dve.tensor_tensor(a, r, r, ALU.mult))
                then(dve.scalar_tensor_tensor(a, a, -0.5, ms, ALU.mult, ALU.mult))
                then(dve.scalar_tensor_tensor(r, a, 1.5, r, ALU.add, ALU.mult), signal)
                return r

            mean_square(0, D)
            r = refine(0, r0_ready)
            dve.tensor_scalar(xn[:, 0, :], xs[:, 0, :], r[:, 0:1], None, ALU.mult).then_inc(xn0_ready, 1)
            split_lo(0)
            dve.wait_ge(mix_gain_in, 16)
            for k in (0, 4):
                for t in range(T):
                    b = T * (k // 4) + t
                    dve.wait_ge(h_turned, b + 1)
                    dve.tensor_tensor(h_f[:, k:k + 4, P * t:P * t + P],
                                      ps[:, 4 + b, :].rearrange("p (a b) -> p a b", b=P),
                                      g_mix[:, k:k + 4].unsqueeze(2).to_broadcast([P, 4, P]), ALU.mult)\
                       .then_inc(hf_ready, 1)
                for t in range(T):
                    b = T * (k // 4) + t
                    v = slice(P * t, P * t + P)
                    dve.wait_ge(hThi_ready, b + 1)
                    dve.tensor_tensor(hT_lo[:, k:k + 4, v], h_f[:, k:k + 4, v], hT_hi[:, k:k + 4, v], ALU.subtract)\
                       .then_inc(hTlo_ready, 1)
            split_lo(1)

            dve.wait_ge(pos_in, 16 * T)
            then(dve.tensor_copy(pos_f[:], pos_i[:]))
            dve.wait_ge(inv_ready, 1)
            a0, a1, turns, far = (ang[:, i, :, :] for i in range(4))
            for t in range(T):
                last = dve.tensor_scalar(ang[:, 0, t, :], inv_f[:], pos_f[:, t:t + 1], None, ALU.mult)
            then(last)
            then(dve.tensor_scalar(turns, a0, 1.0 / (2 * np.pi), MAGIC, ALU.mult, ALU.add))
            then(dve.tensor_scalar(turns, turns, -MAGIC, None, ALU.add))
            for part in two_pi_parts():
                then(dve.scalar_tensor_tensor(a0, turns, -part, a0, ALU.mult, ALU.add))
            then(dve.tensor_scalar(a1, a0, np.pi / 2, None, ALU.add))
            then(dve.tensor_scalar(far, a1, np.pi, 2 * np.pi, ALU.is_gt, ALU.mult))
            then(dve.tensor_tensor(a1, a1, far, ALU.subtract))
            limit = float(np.nextafter(np.float32(np.pi), np.float32(0)))
            dve.tensor_scalar(ang[:, 0:2, :, :], ang[:, 0:2, :, :], limit, -limit, ALU.min, ALU.max)\
               .then_inc(ang_ready, 1)

            def attention_scores(u):
                t, pair = divmod(u, HEADS // 2)
                keys = P * (t + 1)
                i = HEADS * t + 2 * pair
                dve.wait_ge(scored, u + 1)
                then(dve.tensor_tensor(pr[:, u % 2, :, 0:keys],
                                       ps[:, 4, 0:2 * keys].rearrange("p (h k) -> p h k", k=keys),
                                       causal[:, SEQ - keys:].unsqueeze(1).to_broadcast([P, 2, keys]), ALU.add))
                then(dve.tensor_reduce(rmax[:, i:i + 2], pr[:, u % 2, :, 0:keys], AX_X, ALU.max))
                dve.tensor_scalar(nmax[:, i:i + 2], rmax[:, i:i + 2], -SCALE, None, ALU.mult)\
                   .then_inc(rowmax_ready, 1)

            def attention_out(t):
                v = slice(HEADS * t, HEADS * t + HEADS)
                dve.wait_ge(exp_ready, HEADS * (t + 1))
                then(dve.reciprocal(rinv[:, v], rsum[:, v]))
                dve.wait_ge(pv_done, UNITS // T * (t + 1))
                dve.tensor_tensor(o_sb[:, t, :].rearrange("p (h d) -> p h d", d=VH),
                                  ps[:, 7, :].rearrange("p (h d) -> p h d", d=VH),
                                  rinv[:, v].unsqueeze(2).to_broadcast([P, HEADS, VH]), ALU.mult)\
                   .then_inc(o_ready, 1)

            def branch_turned_lo(i, t):
                v = slice(P * t, P * t + P)
                dve.wait_ge(bThi_ready, 1 + i + 1)
                dve.tensor_tensor(bT_lo[:, :, v], ps[:, 5, :].rearrange("p (a b) -> p a b", b=P), bT_hi[:, :, v],
                                  ALU.subtract).then_inc(bTlo_ready, 1)

            def merge(c):
                b, cols = c // 2, slice(BANK * (c % 2), BANK * (c % 2) + BANK)
                dve.wait_ge(half_used, H_GATE + 3 * c + 3)
                dve.wait_ge(gate_ready, T * (c + 1))
                if b:
                    for t in range(T):
                        last = dve.scalar_tensor_tensor(gv[:, t, :], gv[:, t, :], 1.0, ps[:, t, :], ALU.add, ALU.mult)
                    then(last)
                for t in range(T):
                    if b:
                        ins = dve.tensor_tensor(merged[:, t, cols], merged[:, t, cols], gv[:, t, :], ALU.add)
                    else:
                        ins = dve.scalar_tensor_tensor(merged[:, t, cols], gv[:, t, :], 1.0, ps[:, t, :],
                                                       ALU.add, ALU.mult)
                    ins.then_inc(merged_ready, 1)

            def residual(c):
                dve.wait_ge(half_used, H_WO + 3 + c)
                v = slice(BANK * c, BANK * c + BANK)
                for t in range(T):
                    dve.tensor_tensor(xs[:, t, v], xs[:, t, v], ps[:, 2 - 2 * c + t, :], ALU.add)\
                       .then_inc(x1_ready, 1)

            def x1_turned(c):
                for t in range(T):
                    b = T * c + t
                    dve.wait_ge(x_turned, b + 1)
                    dve.tensor_copy(x1T[:, 4 * c:4 * c + 4, P * t:P * t + P],
                                    ps[:, 4 + b, :].rearrange("p (a b) -> p a b", b=P)).then_inc(x1T_ready, 1)

            for n in range(N_MIX):
                if n == N_MIX - 1:
                    residual(0)
                if n == H_CKV:
                    mean_square(1, QR)
                if n == H_CB:
                    mean_square(2, KVR)
                if n == H_SGV:
                    dve.wait_ge(qk_turned, 1)
                    dve.tensor_copy(kT[:, :, 0:P], joined(ps[0:QK, 6:8, :]).rearrange("p (a b) -> p a b", b=P))\
                       .then_inc(kT_ready, 1)
                if n == H_CC:
                    dve.wait_ge(small_turned, 1)
                    dve.tensor_copy(taps[:], ps[:, 4, 0:ROWS]).then_inc(taps_ready, 1)
                    dve.tensor_copy(wsT[:], ps[:, 5, :].rearrange("p (a b) -> p a b", b=P)).then_inc(wsT_ready, 1)
                if n == H_WO:
                    merge(5)
                if 0 <= n - H_ATT - 1 < UNITS:
                    attention_scores(n - H_ATT - 1)
                if n + AHEAD < N_MIX:
                    split_lo(n + AHEAD)
                else:
                    split_lo(n + AHEAD, 0)
                if n == H_CKV:
                    r = refine(1)
                    for t in range(T):
                        dve.tensor_scalar(cn[:, t, 0:QR], ps[:, t, 0:QR], r[:, t:t + 1], None, ALU.mult)\
                           .then_inc(cn_ready, 1)
                if n == H_CB:
                    r = refine(2)
                    for t in range(T):
                        dve.tensor_copy(q9[:, t, HEADS, NOPE:], ps[:, 2 + t, KVR:KVR + ROPE])
                        dve.tensor_scalar(cn[:, t, QR:], ps[:, 2 + t, 0:KVR], r[:, t:t + 1], None, ALU.mult)\
                           .then_inc(cn_ready, 1)
                if n == H_CC:
                    dve.wait_ge(small_in, 16 * SMALL)
                    dve.wait_ge(c_turned, 1)
                    for k0, k1, src in ((0, 4, joined(ps[:, 0:2, :])), (4, KC, ps[:, 4, 0:SEQ])):
                        ins = dve.tensor_tensor(cT_f[:, k0:k1, :], src.rearrange("p (a b) -> p a b", b=SEQ),
                                                g_c[:, k0:k1].unsqueeze(2).to_broadcast([P, k1 - k0, SEQ]), ALU.mult)
                    ins.then_inc(cTf_ready, 1)
                if n == H_CC + 1:
                    dve.wait_ge(cThi_ready, 1)
                    dve.tensor_tensor(cT_lo[:], cT_f[:], cT_hi[:], ALU.subtract).then_inc(cTlo_ready, 1)
                if n == H_CH:
                    dve.wait_ge(q_ready, T)
                    dve.wait_ge(rot_ready, 1)
                    one, two = q9[:, :, :, NOPE:NOPE + R2], q9[:, :, :, NOPE + R2:]
                    sin, cos = (rot[:, i, :, :].unsqueeze(2).to_broadcast([P, T, HEADS + 1, R2]) for i in range(2))
                    dve.tensor_tensor(rt[:, 0, :, :, :], one, cos, ALU.mult)
                    dve.tensor_tensor(rt[:, 1, :, :, :], two, sin, ALU.mult)
                    dve.tensor_tensor(rt[:, 2, :, :, :], two, cos, ALU.mult)
                    then(dve.tensor_tensor(rt[:, 3, :, :, :], one, sin, ALU.mult))
                    dve.tensor_tensor(one, rt[:, 0, :, :, :], rt[:, 1, :, :, :], ALU.subtract)
                    then(dve.tensor_tensor(two, rt[:, 2, :, :, :], rt[:, 3, :, :, :], ALU.add))
                    for t in range(T):
                        dve.tensor_copy(kk[:, t, :, NOPE:], q9[:, t, HEADS:, NOPE:].to_broadcast([P, HEADS, ROPE]))\
                           .then_inc(rope_ready, 1)
                if n == H_SGV:
                    dve.wait_ge(half_used, H_SGV)
                    dve.wait_ge(cc_ready, 1)
                    dve.wait_ge(zpad_ready, 1)
                    z = z_sb[:, :, TAPS - 1:]
                    then(dve.tensor_tensor(z, joined(ps[:, 0:2, :]).rearrange("p (a b) -> p a b", b=SEQ), z, ALU.mult),
                         z_ready)
                if n == H_SGV + 1:
                    dve.wait_ge(qk_turned, 2)
                    dve.tensor_copy(kT[:, :, P:], joined(ps[0:QK, 6:8, :]).rearrange("p (a b) -> p a b", b=P))\
                       .then_inc(kT_ready, 1)
                    dve.wait_ge(cb_ready, 1)
                    for j in range(TAPS):
                        for b in range(4):
                            w, zj = taps[:, 4 * j + b:4 * j + b + 1], z_sb[:, b, j:j + SEQ]
                            if j == 0:
                                last = dve.tensor_scalar(bT_f[:, b, :], zj, w, None, ALU.mult)
                            else:
                                last = dve.scalar_tensor_tensor(bT_f[:, b, :], zj, w, bT_f[:, b, :], ALU.mult, ALU.add)
                        then(last)
                    dve.tensor_tensor(bT_f[:], bT_f[:], cb_sb[:], ALU.mult).then_inc(bTf_ready, 1)
                if n == H_SGU:
                    dve.wait_ge(bThi_ready, 1)
                    dve.tensor_tensor(bT_lo[:], bT_f[:], bT_hi[:], ALU.subtract).then_inc(bTlo_ready, 1)
                    mean_square(3, SG)
                if n == H_SGU + 1:
                    r = refine(3)
                    for t in range(T):
                        dve.scalar_tensor_tensor(gv[:, t, :], gv[:, t, :], r[:, t:t + 1], g_sg[:], ALU.mult, ALU.mult)\
                           .then_inc(gvn_ready, 1)
                for t in range(T):
                    if n == H_GATE + 1 + t:
                        dve.wait_ge(mixed_done, t + 1)
                        dve.wait_ge(gu_ready, T)
                        for g in range(SGG):
                            v = slice(P * g, P * g + P)
                            last = dve.scalar_tensor_tensor(gu_s[:, t, v], ps[:, 5, v],
                                                            taps[:, 4 * TAPS + g:4 * TAPS + g + 1],
                                                            gu_s[:, t, v], ALU.add, ALU.mult)
                        last.then_inc(sgy_ready, 1)
                for t in range(T):
                    if n == H_ATT + UNITS // T * (t + 1) + 2:
                        attention_out(t)
                for b in (1, 2):
                    for t in range(T):
                        if n == H_GATE + 6 * b + t:
                            branch_turned_lo(T * (b - 1) + t, t)
                for c in range(5):
                    if n == H_GATE + 3 * c + 3:
                        merge(c)
                if n in (H_WO - 1, H_WO + 1):
                    for b in ((0, 1) if n < H_WO else (2, 3)):
                        t, k = b % 2, 4 * (b // 2)
                        v = slice(P * t, P * t + P)
                        dve.wait_ge(mhi_ready, b + 1)
                        dve.scalar_tensor_tensor(hT_lo[:, k:k + 4, v],
                                                 ps[:, 4 + b, :].rearrange("p (a b) -> p a b", b=P), 0.5,
                                                 hT_hi[:, k:k + 4, v], ALU.mult, ALU.subtract)\
                           .then_inc(mlo_ready, 1)

            def x1_lo(t):
                dve.wait_ge(xhi_ready, t + 1)
                dve.tensor_tensor(x_lo[:, t, 0:BANK], xf[:, t, 0:BANK], x_hi[:, t, 0:BANK], ALU.subtract)\
                   .then_inc(xlo0_ready, 1)

            def x1_gains(c):
                v = slice(BANK * c, BANK * c + BANK)
                dve.wait_ge(x1_ready, T * c + 1)
                dve.tensor_tensor(xf[:, 0, v], xs[:, 0, v], g_row[:, v], ALU.mult).then_inc(xf0_ready, 1)

            x1_turned(0)
            x1_gains(0)
            residual(1)
            x1_gains(1)
            x1_turned(1)
            mean_square(4, D)
            for t in range(T):
                x1_lo(t)
            r = refine(4)

            def gathered_lo(g, h):
                dve.wait_ge(xghi_ready, 2 * g + h + 1)
                v = slice(4 * h, 4 * h + 4)
                dve.tensor_tensor(xg_lo[:, v, :], ps[:, h, :].rearrange("p (a b) -> p a b", b=P), xg_hi[:, v, :],
                                  ALU.subtract).then_inc(xglo_ready, 1)

            def over(ap, n):
                return ap.to_broadcast([P, T, n])

            def one_hot(out, values, best, index, n, tmp, low):
                if best is not scal[4]:
                    then(dve.tensor_reduce(best, values, AX_X, ALU.max))
                then(dve.tensor_tensor(tmp, values, over(best, n), ALU.is_equal))
                then(dve.scalar_tensor_tensor(tmp, tmp, -BIG, index[:].unsqueeze(1).to_broadcast([P, T, n]),
                                              ALU.mult, ALU.add))
                then(dve.tensor_reduce(low, tmp, AX_X, ALU.min))
                return dve.tensor_tensor(out, tmp, over(low, n), ALU.is_equal)

            scal = [sc[:, i, :, :] for i in range(14)]
            dve.wait_ge(logits_done, 1)
            for t in range(T):
                last = dve.scalar_tensor_tensor(lg[:, t, :], ps[:, 2 + t, 0:NR], r[:, t:t + 1], b_rt[:],
                                                ALU.mult, ALU.add)
            then(last)
            dve.wait_ge(index_ready, 1)
            then(one_hot(goh[:], lg[:, :, 0:NG], scal[0], idx_g, NG, gt[:, 2, :, :], scal[1]), goh_ready)
            unchosen, place = gt[:, 3, :, :], gt[:, 4, :, :]
            dve.tensor_scalar(unchosen, goh[:], NOWHERE, -NOWHERE, ALU.mult, ALU.add)
            dve.tensor_tensor(gt[:, 0, :, :], lg[:, :, 0:NG], over(scal[0], NG), ALU.subtract).then_inc(gmax_ready, 1)
            then(dve.tensor_tensor(eg[:], lg[:, :, NG:].rearrange("p t (g e) -> p t g e", e=EPG),
                                   goh[:].unsqueeze(3).to_broadcast([P, T, NG, EPG]), ALU.mult))
            dve.wait_ge(ranked, 1)
            then(dve.tensor_tensor(place, ps[:, 2, 0:T * NG].rearrange("p (t g) -> p t g", g=NG), unchosen, ALU.add))
            for g in range(NG):
                for t in range(T):
                    dve.tensor_scalar(sel[:, t, P * g:P * g + P], slot_f[:], place[:, t, g:g + 1], None, ALU.is_equal)\
                       .then_inc(sel_ready, 1)
            chosen = et[:, 0, :, :]
            dve.tensor_reduce(chosen, eg[:].rearrange("p t g e -> p t e g"), AX_X, ALU.add)
            then(dve.tensor_reduce(scal[6], place, AX_X, ALU.max))
            then(dve.tensor_scalar(scal[12], scal[6], -float(P), None, ALU.add))
            for t in range(T):
                dve.tensor_scalar(sel[:, t, P * NG:], slot_f[:], scal[12][:, t, :], None, ALU.is_equal)\
                   .then_inc(sel_ready, 1)
            first, rest, second = et[:, 2, :, :], et[:, 3, :, :], et[:, 4, :, :]
            then(one_hot(first, chosen, scal[2], idx_e, EPG, et[:, 1, :, :], scal[3]))
            then(dve.scalar_tensor_tensor(rest, first, LOWEST, chosen, ALU.mult, ALU.add))
            then(dve.tensor_reduce(scal[4], rest, AX_X, ALU.max))
            dve.tensor_tensor(scal[7], scal[4], scal[2], ALU.subtract).then_inc(d_ready, 1)
            then(one_hot(second, rest, scal[4], idx_e, EPG, et[:, 1, :, :], scal[5]))
            gathered_lo(0, 0)
            root_r = r.unsqueeze(2)
            dve.wait_ge(gexp_ready, 1)
            then(dve.tensor_reduce(scal[9], gt[:, 1, :, :], AX_X, ALU.add))
            dve.wait_ge(eexp_ready, 1)
            then(dve.scalar_tensor_tensor(scal[10], scal[8], 1.0, scal[9], ALU.add, ALU.mult))
            then(dve.reciprocal(scal[11], scal[10]))
            then(dve.tensor_tensor(scal[11], scal[11], root_r, ALU.mult))
            then(dve.tensor_tensor(scal[13], scal[11], scal[8], ALU.mult))
            dve.tensor_tensor(et[:, 5, :, :], first, over(scal[11], EPG), ALU.mult)
            dve.tensor_copy(cw[:, :, EPG:], root_r)
            then(dve.tensor_tensor(et[:, 6, :, :], second, over(scal[13], EPG), ALU.mult))
            then(dve.tensor_tensor(cw[:, :, 0:EPG], et[:, 5, :, :], et[:, 6, :, :], ALU.add), comb_split)
            dve.wait_ge(comb_hi, 1)
            dve.tensor_tensor(cw_parts[:, :, 1, :], cw[:], cw_parts[:, :, 0, :], ALU.subtract).then_inc(comb_lo, 1)
            dve.wait_ge(counted, 1)
            then(dve.tensor_scalar(cnt[:, 0, :], ps[:, 3, 0:NG], float(P), None, ALU.is_gt))
            then(dve.scalar_tensor_tensor(cnt[:, 1, :], idx_g[:], -BIG, cnt[:, 0, :], ALU.add, ALU.mult))
            dve.tensor_reduce(ctl_f[:, 0:1], cnt[:, 0, :], AX_X, ALU.add)
            then(dve.tensor_reduce(ctl_f[:, 1:2], cnt[:, 1, :], AX_X, ALU.add))
            dve.tensor_copy(ctl[:], ctl_f[:, 0:2]).then_inc(ctl_ready, 1)

            def turned_lo(e, g):
                dve.wait_ge(hidThi_ready, EPG * g + e + 1)
                dve.tensor_tensor(hidT_lo[:, e % 2, :, :], ps[:, e % 2, 0:DE].rearrange("p (a b) -> p a b", b=P),
                                  hidT_hi[:, e % 2, :, :], ALU.subtract).then_inc(hidTlo_ready, 1)

            def hidden(e, g):
                dve.wait_ge(silu_ready, EPG * g + e + 1)
                dve.scalar_tensor_tensor(hid[:, e % 2, :], silu[:, e % 2, :],
                                         comb[:, bass.ds(g, 1), e:e + 1].rearrange("p a b -> p (a b)"),
                                         ps[:, e % 2, DE:2 * DE], ALU.mult, ALU.mult).then_inc(hid_ready, 1)

            def group(g, more, opening=False, again=False):
                if again:
                    for j in range(AHEAD_E):
                        split_lo(N_MIX + j, g)
                for j, (what, e) in enumerate(order):
                    if opening and j == 1:
                        dve.wait_ge(comb_done, 1)
                        dve.tensor_reduce(comb[:],
                                          ps[:, 1, 0:COMB_COLS].rearrange("p (g i e) -> p g e i", i=2, e=EPG + 1),
                                          AX_X, ALU.add).then_inc(comb_ready, 1)
                        dve.wait_ge(comb_ready, 1)
                    if j == 1:
                        dve.tensor_copy(root_g[:], comb[:, bass.ds(g, 1), EPG:].rearrange("p a b -> p (a b)"))\
                           .then_inc(rootg_ready, 1)
                    if what == "up0" and e == 1:
                        hidden(0, g)
                    if what == "up1" and e:
                        turned_lo(e - 1, g)
                    if what == "down" and e < EPG - 1:
                        hidden(e + 1, g)
                    if what == "down" and e == EPG - 2:
                        turned_lo(e + 1, g)
                    if what == "down" and e == EPG - 1 and more:
                        gathered_lo(g + 1, 0)
                    if more or j + AHEAD_E < PER_GROUP:
                        split_lo(N_MIX + j + AHEAD_E, g)
                if more:
                    gathered_lo(g + 1, 1)
                for c in range(2):
                    v = slice(BANK * c, BANK * c + BANK)
                    dve.wait_ge(yhi_ready, 2 * g + c + 1)
                    dve.tensor_tensor(y_lo[:, v], ps[:, 2 + c, :], y_hi[:, v], ALU.subtract).then_inc(ylo_ready, 1)

            gathered_lo(0, 1)
            split_lo(N_MIX + AHEAD, 0)
            group(0, True, opening=True)
            with dve.Fori(1, NG - 1) as g:
                group(g, True)
            group(NG - 1, False)
            dve.wait_ge(ctl_ready, 1)
            more_tokens = dve.value_load(ctl[0:1, 0:1], min_val=0, max_val=1)
            with dve.If(more_tokens > 0):
                for h in range(2):
                    gathered_lo(NG, h)
                group(NG, False, again=True)
            dve.wait_ge(final_gain_in, 16)
            for c in range(2):
                v = slice(BANK * c, BANK * c + BANK)
                dve.wait_ge(output_done, c + 1)
                for t in range(T):
                    dve.tensor_tensor(x2[:, t, v], xs[:, t, v], ps[:, 4 + 2 * t + c, :], ALU.add).then_inc(x2_ready, 1)
            dve.wait_ge(x2_ready, 2 * T)
            then(dve.tensor_tensor(x2g[:, 0, :], x2[:, 0, :], g_row[:], ALU.mult))
            dve.wait_ge(ssq_ready, T * 5 + 2 * T)
            then(dve.tensor_tensor(stat[:, 5, 0, :], ssq_half[:, 0, :], ssq_half[:, 1, :], ALU.add))
            mean_square(5, D)
            r = refine(5, r5_ready)
            dve.tensor_scalar(xs[:, 0, :], x2g[:, 0, :], r[:, 0:1], None, ALU.mult).then_inc(y0_ready, 1)

        @block.tensor
        def _(pe):
            def three(dst, x_hi, x_lo, hi, lo, first, last, weights_stand=False):
                for i, (x_part, w_part) in enumerate(((x_hi, hi), (x_hi, lo), (x_lo, hi))):
                    a, b = (w_part, x_part) if weights_stand else (x_part, w_part)
                    ins = pe.matmul(dst, a, b, start=first and i == 0, stop=last and i == 2, skip_group_check=True)
                return ins

            def use(n):
                pe.wait_ge(lo_ready, n + 1)
                return half_view(w_hi, SPLIT, n), half_view(w_lo, SPLIT, n)

            def by_token(n, k0, banks, a_hi, a_lo, first, last, part=None):
                hi, lo = use(n)
                _, blocks, cols = halves[n]
                for k in range(*(part or (0, blocks))):
                    for t in range(T):
                        v = slice(P * t, P * t + P)
                        ins = three(ps[:, banks + t, 0:cols], a_hi[:, k0 + k, v], a_lo[:, k0 + k, v],
                                    hi[:, k, :], lo[:, k, :], first and k == 0, last and k == blocks - 1)
                if k == blocks - 1:
                    ins.then_inc(half_used, 1)

            def by_channel(n, k0, banks, first, last):
                hi, lo = use(n)
                for k in range(4):
                    for j in range(4):
                        ins = three(ps[:, banks + j // 2, SEQ * (j % 2):SEQ * (j % 2) + SEQ],
                                    hT_hi[:, k0 + k, :], hT_lo[:, k0 + k, :], hi[:, k, P * j:P * j + P],
                                    lo[:, k, P * j:P * j + P], first and k == 0 and j % 2 == 0, last and k == 3,
                                    weights_stand=True)
                ins.then_inc(half_used, 1)

            def wide(n, k0, a_k0, banks, first, last):
                hi, lo = use(n)
                _, blocks, cols = halves[n]
                for t in range(T):
                    if t and n == H_QUP:
                        pe.wait_ge(cc_ready, 1)
                    for k in range(blocks):
                        v = slice(P * t, P * t + P)
                        for c in range(0, cols, BANK):
                            w = min(BANK, cols - c)
                            ins = three(ps[:, banks + 2 * t + c // BANK, 0:w], cT_hi[:, a_k0 + k0 + k, v],
                                        cT_lo[:, a_k0 + k0 + k, v], hi[:, k, c:c + w], lo[:, k, c:c + w],
                                        first and k == 0, last and k == blocks - 1)
                ins.then_inc(half_used, 1)
            def place(u):
                t, pair = divmod(u, HEADS // 2)
                return t, 2 * pair, P * (t + 1)

            def attention_s(u):
                t, h0, keys = place(u)
                pe.wait_ge(qT_ready, t + 1)
                pe.wait_ge(kT_ready, T if u == 0 else t + 1)
                if u == 0:
                    pe.wait_ge(qT_ready, T)
                else:
                    pe.wait_ge(rowmax_ready, u)
                for h in range(2):
                    ins = pe.matmul(ps[:, 4, keys * h:keys * h + keys], qT[:, h0 + h, P * t:P * t + P],
                                    kT[:, h0 + h, 0:keys], start=True, stop=True)
                ins.then_inc(scored, 1)

            def attention_t(u):
                t, _, _ = place(u)
                pe.wait_ge(exp_ready, 2 * (u + 1))
                if u:
                    pe.wait_ge(pT_ready, u)
                for h in range(2):
                    for b in range(t + 1):
                        i = h * (t + 1) + b
                        ins = pe.transpose(ps[:, 6, P * i:P * i + P], pr[:, u % 2, h, P * b:P * b + P], ident[:])
                ins.then_inc(p_turned, 1)

            def attention_pv(u):
                t, h0, _ = place(u)
                pe.wait_ge(pT_ready, u + 1)
                if u == UNITS // T:
                    pe.wait_ge(o_ready, 1)
                for h in range(2):
                    for b in range(t + 1):
                        ins = pe.matmul(ps[:, 7, VH * (h0 + h):VH * (h0 + h) + VH], pT[:, u % 2, h * (t + 1) + b, :],
                                        v_sb[:, b, h0 + h, :], start=b == 0, stop=b == t)
                ins.then_inc(pv_done, 1)

            def turn_branch(src, i, t):
                if i:
                    pe.wait_ge(bTlo_ready, 1 + i)
                for b in range(4):
                    ins = pe.transpose(ps[:, 5, P * b:P * b + P], src[:, t, P * b:P * b + P], ident[:])
                ins.then_inc(branch_turned, 1)

            def turn_merged(b):
                t, k0 = b % 2, 4 * (b // 2)
                for k in range(4):
                    ins = pe.transpose(ps[:, 4 + b, P * k:P * k + P], merged[:, t, P * (k0 + k):P * (k0 + k) + P],
                                       ident[:])
                ins.then_inc(m_turned, 1)

            def turn_x1(c):
                for t in range(T):
                    pe.wait_ge(x1_ready, T * c + t + 1)
                    for k in range(4):
                        v = slice(P * (4 * c + k), P * (4 * c + k) + P)
                        ins = pe.transpose(ps[:, 4 + T * c + t, P * k:P * k + P], xs[:, t, v], ident[:])
                    ins.then_inc(x_turned, 1)

            def logits(c):
                for t in range(T):
                    pe.wait_ge(x1T_ready, T * c + t + 1)
                    for k in range(4 * c, 4 * c + 4):
                        ins = pe.matmul(ps[:, 2 + t, 0:NR], x1T[:, k, P * t:P * t + P], w_rt[:, k, :],
                                        start=k == 0, stop=k == KD - 1)
                return ins

            pe.wait_ge(consts_ready, 1)
            for b in range(2 * T):
                t, k0 = b % T, 4 * (b // T)
                if b < T:
                    pe.wait_ge(xn1_ready if t else xn0_ready, 1)
                for k in range(4):
                    ins = pe.transpose(ps[:, 4 + b, P * k:P * k + P], xn[:, t, k0 + k:D:KD], ident[:])
                ins.then_inc(h_turned, 1)

            for n in (H_CQ, H_CQ + 1):
                pe.wait_ge(hTlo_ready, T * (n - H_CQ + 1))
                by_token(n, 4 * (n - H_CQ), 0, hT_hi, hT_lo, n == H_CQ, n != H_CQ)
            for n in (H_CKV, H_CKV + 1):
                by_token(n, 4 * (n - H_CKV), 2, hT_hi, hT_lo, n == H_CKV, n != H_CKV)
            for n in (H_CB, H_CB + 1):
                by_channel(n, 4 * (n - H_CB), 6, n == H_CB, n != H_CB)
            pe.wait_ge(small_in, 16 * SMALL)
            pe.transpose(ps[:, 4, 0:ROWS], cw_raw[:], ident[0:ROWS, 0:ROWS])
            for g in range(SGG):
                ins = pe.transpose(ps[:, 5, P * g:P * g + P], ws_raw[:, g, :], ident[:])
            ins.then_inc(small_turned, 1)
            pe.wait_ge(cn_ready, 2 * T)
            for b in range(KC):
                if b == 4:
                    pe.wait_ge(taps_ready, 1)
                c0, step, end = (b, KQ, QR) if b < KQ else (QR + b - KQ, KKV, QR + KVR)
                for t in range(T):
                    c = SEQ * (b % 2) + P * t
                    ins = pe.transpose(ps[:, (0, 1, 4)[b // 2], c:c + P], cn[:, t, c0:end:step], ident[:])
            ins.then_inc(c_turned, 1)
            for n in (H_CC, H_CC + 1):
                by_channel(n, 4 * (n - H_CC), 2, n == H_CC, n != H_CC)
            pe.wait_ge(cTlo_ready, 1)
            pe.wait_ge(cb_ready, 1)
            wide(H_QUP, 0, 0, 0, True, False)
            wide(H_QUP + 1, 2, 0, 0, False, True)
            pe.wait_ge(wsT_ready, 1)
            wide(H_KVUP, 0, KQ, 4, True, True)
            pe.wait_ge(q_ready, 1)
            for n in (H_CH, H_CH + 1):
                by_channel(n, 4 * (n - H_CH), 0, n == H_CH, n != H_CH)

            def turn_qk(t):
                pe.wait_ge(rope_ready, T)
                if t == 0:
                    pe.wait_ge(kv_ready, 2 * T)
                else:
                    pe.wait_ge(qT_ready, t)
                    pe.wait_ge(kT_ready, t)
                for i, src in enumerate((q9, kk)):
                    for h in range(HEADS):
                        ins = pe.transpose(ps[0:QK, 4 + 2 * i + h // 4, P * (h % 4):P * (h % 4) + P],
                                           src[:, t, h, :], ident[:])
                ins.then_inc(qk_turned, 1)

            turn_qk(0)
            pe.wait_ge(q_ready, T)
            by_token(H_SGV, 0, 2, hT_hi, hT_lo, True, False)
            turn_qk(1)
            by_token(H_SGV + 1, 4, 2, hT_hi, hT_lo, False, True)
            pe.wait_ge(z_ready, 1)

            for n in range(H_SGU, N_MIX):
                if n < H_GATE:
                    by_token(n, 4 * (n - H_SGU), 0, hT_hi, hT_lo, n == H_SGU, n != H_SGU)
                elif n < H_WO:
                    c, j = divmod(n - H_GATE, 3)
                    if j == 0:
                        if c == 0:
                            pe.wait_ge(gv_ready, T)
                        else:
                            pe.wait_ge(gate_ready, T * c)
                    if j < 2:
                        by_token(n, 4 * j, 2, hT_hi, hT_lo, j == 0, j == 1)
                    else:
                        b = c // 2
                        if c == 0:
                            pe.wait_ge(gu_ready, T)
                        else:
                            pe.wait_ge(merged_ready, T * c)
                        pe.wait_ge(bTlo_ready, 1 + T * b)
                        by_token(n, 0, 0, bT_hi, bT_lo, True, True)
                else:
                    j, c = divmod(n - H_WO, 2)
                    if n == H_WO:
                        pe.wait_ge(gate_ready, 6 * T)
                        pe.wait_ge(mlo_ready, 2)
                    if n == H_WO + 1:
                        pe.wait_ge(merged_ready, 6 * T)
                    if n == H_WO + 2:
                        pe.wait_ge(mlo_ready, 4)
                    if n < N_MIX - 1:
                        by_token(n, 4 * j, 2 - 2 * c, hT_hi, hT_lo, j == 0, j == 1)
                    else:
                        by_token(n, 4 * j, 2 - 2 * c, hT_hi, hT_lo, False, True, (0, 2))
                        turn_x1(0)
                        by_token(n, 4 * j, 2 - 2 * c, hT_hi, hT_lo, False, True, (2, 4))
                if 0 <= n - H_ATT < UNITS:
                    attention_s(n - H_ATT)
                if 0 <= n - H_ATT - 1 < UNITS:
                    attention_t(n - H_ATT - 1)
                if 0 <= n - H_ATT - 2 < UNITS:
                    attention_pv(n - H_ATT - 2)
                for t in range(T):
                    if n == H_GATE + t:
                        pe.wait_ge(gvn_ready, t + 1)
                        pe.wait_ge(wsT_masked, 1)
                        if t:
                            pe.wait_ge(sgy_ready, t)
                        for g in range(SGG):
                            v = slice(P * g, P * g + P)
                            ins = pe.matmul(ps[:, 5, v], wsT[:, g, :], gv[:, t, v], start=True, stop=True)
                        ins.then_inc(mixed_done, 1)
                    if n == H_GATE + 5 + t:
                        pe.wait_ge(sgy_ready, T)
                        turn_branch(gu_s, t, t)
                    if n == H_GATE + 11 + t:
                        pe.wait_ge(o_ready, t + 1)
                        turn_branch(o_sb, T + t, t)
                if n == H_WO - 2:
                    pe.wait_ge(merged_ready, 5 * T)
                    turn_merged(0)
                    turn_merged(1)
                if n == H_WO:
                    pe.wait_ge(merged_ready, 6 * T)
                    turn_merged(2)
                    turn_merged(3)

            pe.wait_ge(router_w_ready, 1)
            logits(0)
            turn_x1(1)
            logits(1).then_inc(logits_done, 1)
            pe.wait_ge(x1T_ready, 2 * T)
            pe.wait_ge(ylo_ready, 1)
            pe.wait_ge(selTg_ready, 1)
            for b in range(1, 4):
                pe.matmul(ps[:, 4 + b, :], selT_g[:, 0:P], y_hi[:, 0:BANK], start=True, stop=True)
            pe.wait_ge(goh_ready, 1)
            chosen = goh[:].rearrange("p t g -> p (t g)")
            pe.matmul(ps[:, 2, 0:2 * NG], before[:], chosen, start=True, stop=False, skip_group_check=True)
            pe.matmul(ps[:, 2, NG:2 * NG], ones[:], goh[:, 0, :], start=False, stop=True, skip_group_check=True)\
              .then_inc(ranked, 1)
            for t in range(T):
                ins = pe.matmul(ps[:, 3, 0:NG], ones[:], goh[:, t, :], start=t == 0, stop=t == 1)
            ins.then_inc(counted, 1)

            def gather(g, h):
                for k in range(4):
                    cols = slice(4 * h + k, D, KD)
                    for i in range(2 * T):
                        part, t = (x_hi, x_lo)[i // T], i % T
                        ins = pe.matmul(ps[:, h, P * k:P * k + P], part[:, t, cols],
                                        sel[:, t, bass.ds(g * P, P)], start=i == 0, stop=i == 2 * T - 1)
                ins.then_inc(tokens_gathered, 1)

            pe.wait_ge(xlo0_ready, T)
            pe.wait_ge(xlo1_ready, T)
            pe.wait_ge(sel_ready, T)
            gather(0, 0)
            gather(0, 1)

            def maps():
                pe.wait_ge(sel_ready, T * (NG + 1))
                pe.wait_ge(ctl_ready, 1)
                pe.wait_ge(comb_lo, 1)
                pe.wait_ge(xglo_ready, 2)
                for g in range(NG + 1):
                    c = 2 * (EPG + 1) * g
                    for t in range(T):
                        ins = pe.matmul(ps[:, 1, c:c + 2 * (EPG + 1)], sel[:, t, P * g:P * g + P],
                                        cw_parts[:, t, :, :].rearrange("p i e -> p (i e)"),
                                        start=t == 0, stop=t == T - 1)
                ins.then_inc(comb_done, 1)
                for g in range(NG + 1):
                    for t in range(T):
                        c = SEQ * (g % 2) + P * t
                        ins = pe.matmul(ps[:, 2 + g // 2, c:c + P], sel[:, t, P * g:P * g + P], ident_r[:],
                                        start=True, stop=True)
                ins.then_inc(selT_done, 1)

            def scatter(g, signal=None):
                pe.wait_ge(selTg_ready, g + 1)
                for c in range(2):
                    pe.wait_ge(ylo_ready, 2 * g + c)
                    for t in range(T):
                        for i, part in enumerate((y_hi, y_lo)):
                            ins = pe.matmul(ps[:, 4 + 2 * t + c, :], selT_g[:, P * t:P * t + P],
                                            part[:, BANK * c:BANK * c + BANK], start=False, stop=i == 1,
                                            skip_group_check=True)
                    if signal is not None:
                        ins.then_inc(signal, 1)
                return ins

            def turn_hidden(e, g):
                pe.wait_ge(hid_ready, EPG * g + e + 1)
                for k in range(2):
                    ins = pe.transpose(ps[:, e % 2, P * k:P * k + P], hid[:, e % 2, k:DE:2], ident[:])
                ins.then_inc(hid_turned, 1)

            def expert_half(j, g, more):
                what, e = order[j]
                n = N_MIX + j
                pe.wait_ge(lo_ready, PER_GROUP * g + n + 1)
                cols = BANK if what != "down" else D
                hi, lo = (w.rearrange("p (k n) -> p k n", n=cols) for w in expert_split(j))
                if what != "down":
                    k0 = 4 * int(what[2])
                    if e == 0:
                        pe.wait_ge(xglo_ready, 2 * g + 1 + int(what[2]))
                    for k in range(4):
                        ins = three(ps[:, e % 2, :], xg_hi[:, k0 + k, :], xg_lo[:, k0 + k, :], hi[:, k, :], lo[:, k, :],
                                    k0 + k == 0, k0 + k == KD - 1)
                else:
                    pe.wait_ge(hidTlo_ready, EPG * g + e + 1)
                    for c in range(2):
                        for k in range(2):
                            v = slice(BANK * c, BANK * c + BANK)
                            ins = three(ps[:, 2 + c, :], hidT_hi[:, e % 2, k, :], hidT_lo[:, e % 2, k, :],
                                        hi[:, k, v], lo[:, k, v], e == 0 and k == 0, e == EPG - 1 and k == 1)
                        if e == EPG - 1 and c == 0:
                            ins.then_inc(sum_done, 1)
                        if e == EPG - 2 and c == 0 and not more:
                            turn_hidden(EPG - 1, g)
                ins.then_inc(half_used, 1)

            def group(g, more, opening=False):
                for j, (what, e) in enumerate(order):
                    if opening and j == 1:
                        maps()
                    if opening and j == 2:
                        pe.wait_ge(comb_ready, 1)
                    if opening and j == 3:
                        pe.wait_ge(selT_ready, 1)
                        pe.matmul(ps[:, 4, :], selT_g[:, 0:P], y_hi[:, 0:BANK], start=True, stop=True)\
                          .then_inc(scattered, 1)
                    if what == "up1" and e:
                        turn_hidden(e - 1, g)
                    if what == "down" and e == EPG - 1 and more:
                        turn_hidden(e, g)
                        gather(g + 1, 0)
                    expert_half(j, g, more)
                    if what == "up1" and e == 0 and not opening:
                        scatter(g).then_inc(scattered, 1)
                if more:
                    gather(g + 1, 1)

            group(0, True, opening=True)
            with pe.Fori(1, NG - 1) as g:
                group(g, True)
            group(NG - 1, False)
            pe.wait_ge(ctl_ready, 1)
            over = pe.value_load(ctl[0:1, 0:1], min_val=0, max_val=1)
            with pe.If(over > 0):
                pe.wait_ge(hidTlo_ready, EPG * NG)
                gather(NG, 0)
                gather(NG, 1)
                group(NG, False)
            scatter(over + NG, output_done)


_INS = ["x", "positions", "norm_mix", "w_in", "q_norm", "w_q_up", "kv_norm", "w_kv_up", "sg_norm", "w_s", "b_s",
        "conv_w", "w_a_out", "w_b_out", "w_c_out", "w_o", "norm_ffn", "w_group_router", "b_group_router",
        "w_expert_router", "b_expert_router", "w_gate_up", "w_down", "final_norm"]


def kernel(**inputs):
    import concourse.bacc as bacc
    from concourse.bass_utils import run_bass_kernel_spmd

    nc = bacc.Bacc("TRN2", target_bir_lowering=False, num_devices=1)
    arrays, args = {}, []
    for name in _INS:
        a = np.ascontiguousarray(inputs[name])
        arrays[f"in_{name}"] = a
        args.append(nc.dram_tensor(f"in_{name}", a.shape, mybir.dt.from_np(a.dtype), kind="ExternalInput").ap())
    args.append(nc.dram_tensor("out_0", (1, SEQ, D), F32, kind="ExternalOutput").ap())
    trunk(nc, *args)
    r = run_bass_kernel_spmd(nc, [arrays], core_ids=[0])
    return r.results[0]["out_0"]
```
